# Optimizing a Trainium2 kernel written in Bass

```python
import math
import jax, jax.numpy as jnp
from jax import lax
import numpy as np
import jax
import jax.numpy as jnp

D_MODEL = 1024
BATCH = 1
SEQ = 512
DEPTH = 2

RET_WIDTH = D_MODEL // 2
RET_HEAD_DIM = 64
RET_HEADS = RET_WIDTH // RET_HEAD_DIM
DIFF_WIDTH = D_MODEL - RET_WIDTH
DIFF_HEAD_DIM = 64
DIFF_V_DIM = 2 * DIFF_HEAD_DIM
DIFF_HEADS = DIFF_WIDTH // DIFF_V_DIM
MIX_WIDTH = RET_WIDTH + DIFF_WIDTH
D_IN_PROJ = 4 * RET_WIDTH + 3 * DIFF_WIDTH
D_FF = -(-8 * D_MODEL // (3 * 256)) * 256
CHUNK = 128
Q_BLOCK = 128
EPS = 1e-6


def rms_norm(x, g):
    xf = x.astype(jnp.float32)
    y = xf * lax.rsqrt(jnp.mean(xf * xf, axis=-1, keepdims=True) + EPS)
    return (y * g.astype(jnp.float32)).astype(x.dtype)

def alibi_slopes(n):
    return 2.0 ** (-8.0 * jnp.arange(1, n + 1, dtype=jnp.float32) / n)

def retention_bidir(q, k, v, lg_f, lg_b):
    B, S, H, D = q.shape
    N = S // CHUNK
    qc = q.astype(jnp.float32).reshape(B, N, CHUNK, H, D)
    kc = k.astype(jnp.float32).reshape(B, N, CHUNK, H, D)
    vc = v.astype(jnp.float32).reshape(B, N, CHUNK, H, D)
    pos = jnp.arange(CHUNK, dtype=jnp.float32)
    dist = pos[:, None] - pos[None, :]
    mask_f = jnp.where(dist >= 0, jnp.exp(lg_f[:, None, None] * jnp.maximum(dist, 0.0)), 0.0)
    mask_b = jnp.where(dist < 0, jnp.exp(lg_b[:, None, None] * jnp.maximum(-dist, 0.0)), 0.0)
    dmask = mask_f + mask_b
    scores = jnp.einsum('bnthd,bnshd->bnhts', qc, kc) * dmask[None, None]
    intra = jnp.einsum('bnhts,bnshd->bnthd', scores, vc)

    wk_f = jnp.exp(lg_f[None, :] * (CHUNK - 1 - pos)[:, None])
    wq_f = jnp.exp(lg_f[None, :] * (pos + 1)[:, None])
    kv_f = jnp.einsum('bnshd,bnshe->nbhde', kc * wk_f[None, None, :, :, None], vc)
    dc_f = jnp.exp(lg_f * CHUNK)[None, :, None, None]
    wk_b = jnp.exp(lg_b[None, :] * pos[:, None])
    wq_b = jnp.exp(lg_b[None, :] * (CHUNK - pos)[:, None])
    kv_b = jnp.einsum('bnshd,bnshe->nbhde', kc * wk_b[None, None, :, :, None], vc)
    dc_b = jnp.exp(lg_b * CHUNK)[None, :, None, None]

    zeros = jnp.zeros((B, H, D, D), jnp.float32)

    def fwd_step(R, kv):
        return dc_f * R + kv, R

    def bwd_step(R, kv):
        return dc_b * R + kv, R

    _, R_f = lax.scan(fwd_step, zeros, kv_f)
    _, R_b = lax.scan(bwd_step, zeros, kv_b, reverse=True)
    cross_f = jnp.einsum('bnthd,nbhde->bnthe', qc * wq_f[None, None, :, :, None], R_f)
    cross_b = jnp.einsum('bnthd,nbhde->bnthe', qc * wq_b[None, None, :, :, None], R_b)
    out = (intra + cross_f + cross_b).reshape(B, S, H, D)
    return out.astype(q.dtype)

def diff_attention(q, k, v, lam, slopes):
    B, S, H, _, Dh = q.shape
    NB = S // Q_BLOCK
    q_blocks = q.reshape(B, NB, Q_BLOCK, H, 2, Dh).transpose(1, 0, 2, 3, 4, 5)
    starts = jnp.arange(NB, dtype=jnp.int32) * Q_BLOCK
    kpos = jnp.arange(S, dtype=jnp.int32)
    vf = v.astype(jnp.float32)

    def block(args):
        qb, start = args
        s = jnp.einsum('bqhmd,bkhmd->bhmqk', qb, k).astype(jnp.float32)
        qpos = start + jnp.arange(Q_BLOCK, dtype=jnp.int32)
        dist = jnp.abs(qpos[:, None] - kpos[None, :]).astype(jnp.float32)
        s = s - slopes[None, :, None, None, None] * dist[None, None, None]
        p = jax.nn.softmax(s, axis=-1)
        a = p[:, :, 0] - lam * p[:, :, 1]
        return jnp.einsum('bhqk,bkhe->bqhe', a, vf)

    o = lax.map(block, (q_blocks, starts))
    return o.transpose(1, 0, 2, 3, 4).reshape(B, S, H, DIFF_V_DIM).astype(q.dtype)

def first_inputs(seed: int = 0) -> dict:
    key = jax.random.key(seed)
    ks = jax.random.split(key, 20)
    f32 = jnp.float32
    nrm = lambda k, shape, scale: jax.random.normal(k, shape, f32) * scale
    heads = jnp.arange(RET_HEADS, dtype=f32)
    base = jnp.log(-jnp.log1p(-(2.0 ** (-5.0 - heads))))
    return {
        "x": jax.random.normal(ks[0], (BATCH, SEQ, D_MODEL), f32),
        "attn_norm_g": 1.0 + nrm(ks[1], (DEPTH, D_MODEL), 0.02),
        "w_in": nrm(ks[2], (DEPTH, D_MODEL, D_IN_PROJ), D_MODEL ** -0.5),
        "ret_decay_fwd": base[None, :] + nrm(ks[3], (DEPTH, RET_HEADS), 0.1),
        "ret_decay_bwd": base[None, :] + nrm(ks[4], (DEPTH, RET_HEADS), 0.1),
        "ret_norm_g": 1.0 + nrm(ks[5], (DEPTH, RET_HEAD_DIM), 0.02),
        "dq_norm_g": 1.0 + nrm(ks[6], (DEPTH, DIFF_HEAD_DIM), 0.02),
        "dk_norm_g": 1.0 + nrm(ks[7], (DEPTH, DIFF_HEAD_DIM), 0.02),
        "lambda_q1": nrm(ks[8], (DEPTH, DIFF_HEAD_DIM), 0.1),
        "lambda_k1": nrm(ks[9], (DEPTH, DIFF_HEAD_DIM), 0.1),
        "lambda_q2": nrm(ks[10], (DEPTH, DIFF_HEAD_DIM), 0.1),
        "lambda_k2": nrm(ks[11], (DEPTH, DIFF_HEAD_DIM), 0.1),
        "diff_norm_g": 1.0 + nrm(ks[12], (DEPTH, DIFF_V_DIM), 0.02),
        "w_out": nrm(ks[13], (DEPTH, MIX_WIDTH, D_MODEL), MIX_WIDTH ** -0.5),
        "ffn_norm_g": 1.0 + nrm(ks[14], (DEPTH, D_MODEL), 0.02),
        "w_gate": nrm(ks[15], (DEPTH, D_MODEL, D_FF), D_MODEL ** -0.5),
        "w_up": nrm(ks[16], (DEPTH, D_MODEL, D_FF), D_MODEL ** -0.5),
        "w_down": nrm(ks[17], (DEPTH, D_FF, D_MODEL), D_FF ** -0.5),
    }

def first_block(x, attn_norm_g, w_in, ret_decay_fwd, ret_decay_bwd, ret_norm_g,
              dq_norm_g, dk_norm_g, lambda_q1, lambda_k1, lambda_q2, lambda_k2,
              diff_norm_g, w_out, ffn_norm_g, w_gate, w_up, w_down):
    B, S, _ = x.shape
    slopes = alibi_slopes(DIFF_HEADS)
    split_at = [RET_WIDTH, 2 * RET_WIDTH, 3 * RET_WIDTH, 4 * RET_WIDTH,
                4 * RET_WIDTH + DIFF_WIDTH, 4 * RET_WIDTH + 2 * DIFF_WIDTH]
    for l in range(DEPTH):
        lam_init = 0.8 - 0.6 * math.exp(-0.3 * l)
        h = rms_norm(x, attn_norm_g[l])
        proj = h @ w_in[l]
        rq, rk, rv, rg, dq, dk, dv = jnp.split(proj, split_at, axis=-1)

        shp = (B, S, RET_HEADS, RET_HEAD_DIM)
        lg_f = -jnp.exp(ret_decay_fwd[l].astype(jnp.float32))
        lg_b = -jnp.exp(ret_decay_bwd[l].astype(jnp.float32))
        ret = retention_bidir(rq.reshape(shp), rk.reshape(shp) * RET_HEAD_DIM ** -0.5,
                              rv.reshape(shp), lg_f, lg_b)
        ret = rms_norm(ret, ret_norm_g[l]) * jax.nn.silu(rg.reshape(shp))
        ret = ret.reshape(B, S, RET_WIDTH)

        qk_shp = (B, S, DIFF_HEADS, 2, DIFF_HEAD_DIM)
        dqn = rms_norm(dq.reshape(qk_shp), dq_norm_g[l]) * DIFF_HEAD_DIM ** -0.5
        dkn = rms_norm(dk.reshape(qk_shp), dk_norm_g[l])
        lam = (jnp.exp(jnp.sum(lambda_q1[l].astype(jnp.float32) * lambda_k1[l].astype(jnp.float32)))
               - jnp.exp(jnp.sum(lambda_q2[l].astype(jnp.float32) * lambda_k2[l].astype(jnp.float32)))
               + lam_init)
        da = diff_attention(dqn, dkn, dv.reshape(B, S, DIFF_HEADS, DIFF_V_DIM), lam, slopes)
        da = (rms_norm(da, diff_norm_g[l]) * (1.0 - lam_init)).reshape(B, S, DIFF_WIDTH)

        x = x + jnp.concatenate([ret, da], axis=-1) @ w_out[l]

        h = rms_norm(x, ffn_norm_g[l])
        x = x + (jax.nn.silu(h @ w_gate[l]) * (h @ w_up[l])) @ w_down[l]
    return x


CTX_LEN = 256
GRID_W = 64
N_MIXERS = 3
HEAD_DIM = 64
N_HEADS = D_MODEL // HEAD_DIM
N_KV_HEADS = max(1, N_HEADS // 4)
NA_WIN_H = 8
NA_WIN_W = 16
NA_QCOLS = 16
NA_KCOLS = NA_QCOLS + NA_WIN_W
SWA_RADIUS = 128
ROPE_THETA = 10000.0
D_FF_2 = ((8 * D_MODEL // 3 + 127) // 128) * 128
CONV_W = 3
RMS_EPS = 1e-6
NEG_INF = -1e30
N_LAYERS_NA = (DEPTH + N_MIXERS - 1) // N_MIXERS
N_LAYERS_SWA = (DEPTH + N_MIXERS - 2) // N_MIXERS
N_LAYERS_GA = (DEPTH + N_MIXERS - 3) // N_MIXERS


def rmsnorm(x, g):
    x32 = x.astype(jnp.float32)
    y = x32 * lax.rsqrt(jnp.mean(x32 * x32, axis=-1, keepdims=True) + RMS_EPS)
    return (y * g.astype(jnp.float32)).astype(x.dtype)

def modulate(h, shift, scale):
    return h * (1 + scale) + shift

def axial_rope_tables(seq):
    t = jnp.arange(seq)
    row = (t // GRID_W).astype(jnp.float32)
    col = (t % GRID_W).astype(jnp.float32)
    n_axis = HEAD_DIM // 4
    inv = ROPE_THETA ** (-jnp.arange(n_axis, dtype=jnp.float32) / n_axis)
    ang = jnp.concatenate([row[:, None] * inv, col[:, None] * inv], axis=-1)
    return jnp.cos(ang), jnp.sin(ang)

def apply_rope(x, cos, sin):
    shp = (x.shape[1],) + (1,) * (x.ndim - 3) + (x.shape[-1] // 2,)
    cos = cos.reshape(shp).astype(x.dtype)
    sin = sin.reshape(shp).astype(x.dtype)
    x1, x2 = jnp.split(x, 2, axis=-1)
    return jnp.concatenate([x1 * cos - x2 * sin, x2 * cos + x1 * sin], axis=-1)

def attend(q, k, v, bias=None, mask=None, sink=None):
    s = jnp.einsum('...qngd,...knd->...ngqk', q, k).astype(jnp.float32) * (HEAD_DIM ** -0.5)
    if bias is not None:
        s = s + bias.astype(jnp.float32)
    if mask is not None:
        s = jnp.where(mask, s, NEG_INF)
    if sink is not None:
        sink_col = jnp.broadcast_to(sink.astype(jnp.float32)[:, :, None, None], s.shape[:-1] + (1,))
        s = jnp.concatenate([s, sink_col], axis=-1)
    p = jax.nn.softmax(s, axis=-1)
    if sink is not None:
        p = p[..., :-1]
    return jnp.einsum('...ngqk,...knd->...qngd', p.astype(v.dtype), v)

def attn_inputs(h, w_qkv, g_q, g_k, n_kv, with_q=True):
    bsz, t = h.shape[:2]
    kv_w = n_kv * HEAD_DIM
    if with_q:
        y = h @ w_qkv
        q = rmsnorm(y[..., :D_MODEL].reshape(bsz, t, n_kv, N_HEADS // n_kv, HEAD_DIM), g_q)
        kv = y[..., D_MODEL:]
    else:
        q = None
        kv = h @ w_qkv[:, D_MODEL:]
    k = rmsnorm(kv[..., :kv_w].reshape(bsz, t, n_kv, HEAD_DIM), g_k)
    v = kv[..., kv_w:].reshape(bsz, t, n_kv, HEAD_DIM)
    return q, k, v

def neighbourhood_attention(q, k, v, k_c, v_c, rpb):
    bsz, seq = q.shape[:2]
    n_ctx = k_c.shape[1]
    rows = seq // GRID_W
    kh = min(NA_WIN_H, rows)
    ncb = GRID_W // NA_QCOLS
    qg = q.reshape(bsz, rows, ncb, NA_QCOLS, N_HEADS, 1, HEAD_DIM)
    kg = k.reshape(bsz, rows, GRID_W, N_HEADS, HEAD_DIM)
    vg = v.reshape(bsz, rows, GRID_W, N_HEADS, HEAD_DIM)
    qcol = np.arange(GRID_W).reshape(ncb, NA_QCOLS)
    kcs = np.clip(np.arange(ncb) * NA_QCOLS - NA_WIN_W // 2, 0, GRID_W - NA_KCOLS)
    kcol = kcs[:, None] + np.arange(NA_KCOLS)
    cs = np.clip(qcol - NA_WIN_W // 2, 0, GRID_W - NA_WIN_W)
    col_ok = (kcol[:, None, :] >= cs[..., None]) & (kcol[:, None, :] < cs[..., None] + NA_WIN_W)
    dc_idx = np.clip(kcol[:, None, :] - qcol[..., None], -(NA_WIN_W - 1), NA_WIN_W - 1) + NA_WIN_W - 1
    lat_ok = np.broadcast_to(col_ok[:, :, None, :], (ncb, NA_QCOLS, kh, NA_KCOLS)).reshape(ncb, NA_QCOLS, kh * NA_KCOLS)
    mask = np.concatenate([lat_ok, np.ones((ncb, NA_QCOLS, n_ctx), bool)], axis=-1)[:, None, None]
    k_cb = jnp.broadcast_to(k_c[:, None], (bsz, ncb) + k_c.shape[1:])
    v_cb = jnp.broadcast_to(v_c[:, None], (bsz, ncb) + v_c.shape[1:])
    zero_ctx_bias = jnp.zeros((ncb, N_HEADS, NA_QCOLS, n_ctx), rpb.dtype)

    def row_step(r):
        rs = jnp.clip(r - kh // 2, 0, rows - kh)
        k_r = lax.dynamic_slice_in_dim(kg, rs, kh, axis=1)
        v_r = lax.dynamic_slice_in_dim(vg, rs, kh, axis=1)
        k_b = jnp.moveaxis(k_r[:, :, kcol], 1, 2).reshape(bsz, ncb, kh * NA_KCOLS, N_HEADS, HEAD_DIM)
        v_b = jnp.moveaxis(v_r[:, :, kcol], 1, 2).reshape(bsz, ncb, kh * NA_KCOLS, N_HEADS, HEAD_DIM)
        k_cat = jnp.concatenate([k_b, k_cb], axis=2)
        v_cat = jnp.concatenate([v_b, v_cb], axis=2)
        dr_idx = rs + jnp.arange(kh) - r + NA_WIN_H - 1
        b_lat = rpb[:, dr_idx[:, None, None, None], dc_idx[None]]
        b_lat = jnp.transpose(b_lat, (2, 0, 3, 1, 4)).reshape(ncb, N_HEADS, NA_QCOLS, kh * NA_KCOLS)
        bias = jnp.concatenate([b_lat, zero_ctx_bias], axis=-1)[:, :, None]
        q_r = lax.dynamic_index_in_dim(qg, r, axis=1, keepdims=False)
        return attend(q_r, k_cat, v_cat, bias=bias, mask=mask)

    out = lax.map(row_step, jnp.arange(rows))
    return jnp.moveaxis(out, 0, 1).reshape(bsz, seq, D_MODEL)

def sliding_window_attention(q, k, v, k_c, v_c, sink):
    bsz, seq = q.shape[:2]
    n_ctx = k_c.shape[1]
    nb = seq // Q_BLOCK
    span = Q_BLOCK + 2 * SWA_RADIUS
    pad = ((0, 0), (SWA_RADIUS, SWA_RADIUS), (0, 0), (0, 0))
    k_p = jnp.pad(k, pad)
    v_p = jnp.pad(v, pad)
    qoff = np.arange(Q_BLOCK)
    koff = np.arange(span) - SWA_RADIUS
    band = np.abs(qoff[:, None] - koff[None, :]) <= SWA_RADIUS
    ctx_ok = jnp.ones((Q_BLOCK, n_ctx), bool)

    def block_step(j):
        start = j * Q_BLOCK
        q_j = lax.dynamic_slice_in_dim(q, start, Q_BLOCK, axis=1)
        k_j = lax.dynamic_slice_in_dim(k_p, start, span, axis=1)
        v_j = lax.dynamic_slice_in_dim(v_p, start, span, axis=1)
        kpos = start - SWA_RADIUS + jnp.arange(span)
        valid = band & ((kpos >= 0) & (kpos < seq))[None, :]
        mask = jnp.concatenate([valid, ctx_ok], axis=-1)
        return attend(q_j, jnp.concatenate([k_j, k_c], axis=1), jnp.concatenate([v_j, v_c], axis=1),
                      mask=mask, sink=sink)

    out = lax.map(block_step, jnp.arange(nb))
    return jnp.moveaxis(out, 0, 1).reshape(bsz, seq, D_MODEL)

def blocked_global_attention(q, k, v, k_c, v_c):
    bsz, seq = q.shape[:2]
    nb = seq // Q_BLOCK
    k_all = jnp.concatenate([k, k_c], axis=1)
    v_all = jnp.concatenate([v, v_c], axis=1)

    def block_step(j):
        q_j = lax.dynamic_slice_in_dim(q, j * Q_BLOCK, Q_BLOCK, axis=1)
        return attend(q_j, k_all, v_all)

    out = lax.map(block_step, jnp.arange(nb))
    return jnp.moveaxis(out, 0, 1).reshape(bsz, seq, D_MODEL)

def conv_ffn(h, w_up, conv_w, conv_b, w_down):
    t = h.shape[1]
    u = h @ w_up
    u_p = jnp.pad(u, ((0, 0), (CONV_W // 2, CONV_W // 2), (0, 0)))
    u = sum(u_p[:, tap:tap + t] * conv_w[tap] for tap in range(CONV_W)) + conv_b
    a, g = jnp.split(u, 2, axis=-1)
    return (a * jax.nn.silu(g)) @ w_down

def second_inputs(seed: int = 0) -> dict:
    key = jax.random.key(seed)
    ks = iter(jax.random.split(key, 32))
    d = D_MODEL
    qkv_na = d + 2 * N_HEADS * HEAD_DIM
    qkv_gqa = d + 2 * N_KV_HEADS * HEAD_DIM

    def nrm(shape, scale):
        return scale * jax.random.normal(next(ks), shape, jnp.float32)

    return {
        'x': nrm((BATCH, SEQ, d), 1.0),
        'c': nrm((BATCH, d), 1.0),
        'ctx': nrm((BATCH, CTX_LEN, d), 1.0),
        'c_ctx': nrm((d,), 1.0),
        'w_mod': nrm((DEPTH, d, 6 * d), 0.5 * d ** -0.5),
        'b_mod': nrm((DEPTH, 6 * d), 0.02),
        'g_attn': 1.0 + nrm((DEPTH, d), 0.02),
        'g_ffn': 1.0 + nrm((DEPTH, d), 0.02),
        'na_w_qkv': nrm((N_LAYERS_NA, d, qkv_na), d ** -0.5),
        'na_g_q': 1.0 + nrm((N_LAYERS_NA, HEAD_DIM), 0.02),
        'na_g_k': 1.0 + nrm((N_LAYERS_NA, HEAD_DIM), 0.02),
        'na_rpb': nrm((N_LAYERS_NA, N_HEADS, 2 * NA_WIN_H - 1, 2 * NA_WIN_W - 1), 0.5),
        'na_w_o': nrm((N_LAYERS_NA, d, d), d ** -0.5),
        'swa_w_qkv': nrm((N_LAYERS_SWA, d, qkv_gqa), d ** -0.5),
        'swa_g_q': 1.0 + nrm((N_LAYERS_SWA, HEAD_DIM), 0.02),
        'swa_g_k': 1.0 + nrm((N_LAYERS_SWA, HEAD_DIM), 0.02),
        'swa_sink': nrm((N_LAYERS_SWA, N_HEADS), 0.5),
        'swa_w_o': nrm((N_LAYERS_SWA, d, d), d ** -0.5),
        'ga_w_qkv': nrm((N_LAYERS_GA, d, qkv_gqa), d ** -0.5),
        'ga_g_q': 1.0 + nrm((N_LAYERS_GA, HEAD_DIM), 0.02),
        'ga_g_k': 1.0 + nrm((N_LAYERS_GA, HEAD_DIM), 0.02),
        'ga_w_o': nrm((N_LAYERS_GA, d, d), d ** -0.5),
        'ffn_w_up': nrm((DEPTH, d, 2 * D_FF_2), d ** -0.5),
        'ffn_conv_w': nrm((DEPTH, CONV_W, 2 * D_FF_2), CONV_W ** -0.5),
        'ffn_conv_b': nrm((DEPTH, 2 * D_FF_2), 0.02),
        'ffn_w_down': nrm((DEPTH, D_FF_2, d), D_FF_2 ** -0.5),
    }

def second_block(x, c, ctx, c_ctx, w_mod, b_mod, g_attn, g_ffn,
              na_w_qkv, na_g_q, na_g_k, na_rpb, na_w_o,
              swa_w_qkv, swa_g_q, swa_g_k, swa_sink, swa_w_o,
              ga_w_qkv, ga_g_q, ga_g_k, ga_w_o,
              ffn_w_up, ffn_conv_w, ffn_conv_b, ffn_w_down):
    bsz, seq = x.shape[:2]
    n_ctx = ctx.shape[1]
    cos, sin = axial_rope_tables(seq)
    silu_c = jax.nn.silu(c)
    silu_cc = jax.nn.silu(c_ctx)
    for i in range(DEPTH):
        last = i == DEPTH - 1
        kind, j = i % N_MIXERS, i // N_MIXERS
        mod = silu_c @ w_mod[i] + b_mod[i]
        mod_c = silu_cc @ w_mod[i] + b_mod[i]
        sh1, sc1, gt1, sh2, sc2, gt2 = jnp.split(mod[:, None, :], 6, axis=-1)
        sh1c, sc1c, gt1c, sh2c, sc2c, gt2c = jnp.split(mod_c, 6, axis=-1)

        h = modulate(rmsnorm(x, g_attn[i]), sh1, sc1)
        hc = modulate(rmsnorm(ctx, g_attn[i]), sh1c, sc1c)
        if kind == 0:
            w_in, w_out, gq, gk, n_kv, sink = na_w_qkv[j], na_w_o[j], na_g_q[j], na_g_k[j], N_HEADS, None
        elif kind == 1:
            w_in, w_out, gq, gk, n_kv = swa_w_qkv[j], swa_w_o[j], swa_g_q[j], swa_g_k[j], N_KV_HEADS
            sink = swa_sink[j].reshape(n_kv, N_HEADS // n_kv)
        else:
            w_in, w_out, gq, gk, n_kv, sink = ga_w_qkv[j], ga_w_o[j], ga_g_q[j], ga_g_k[j], N_KV_HEADS, None
        q, k, v = attn_inputs(h, w_in, gq, gk, n_kv)
        q_c, k_c, v_c = attn_inputs(hc, w_in, gq, gk, n_kv, with_q=not last)
        if kind == 0:
            o = neighbourhood_attention(q, k, v, k_c, v_c, na_rpb[j])
        else:
            q = apply_rope(q, cos, sin)
            k = apply_rope(k, cos, sin)
            if kind == 1:
                o = sliding_window_attention(q, k, v, k_c, v_c, sink)
            else:
                o = blocked_global_attention(q, k, v, k_c, v_c)
        x = x + gt1 * (o @ w_out)
        if not last:
            o_c = attend(q_c, k_c, v_c, sink=sink).reshape(bsz, n_ctx, D_MODEL)
            ctx = ctx + gt1c * (o_c @ w_out)

        h = modulate(rmsnorm(x, g_ffn[i]), sh2, sc2)
        x = x + gt2 * conv_ffn(h, ffn_w_up[i], ffn_conv_w[i], ffn_conv_b[i], ffn_w_down[i])
        if not last:
            hc = modulate(rmsnorm(ctx, g_ffn[i]), sh2c, sc2c)
            ctx = ctx + gt2c * conv_ffn(hc, ffn_w_up[i], ffn_conv_w[i], ffn_conv_b[i], ffn_w_down[i])
    return x


def setup_inputs(seed=0):
    out = dict(first_inputs(seed))
    for name, value in second_inputs(seed + 1).items():
        if name != "x":
            out[name + "_2"] = value
    return out


def reference(
    x, attn_norm_g, w_in, ret_decay_fwd, ret_decay_bwd, ret_norm_g, dq_norm_g, dk_norm_g,
    lambda_q1, lambda_k1, lambda_q2, lambda_k2, diff_norm_g, w_out, ffn_norm_g, w_gate, w_up,
    w_down, c_2, ctx_2, c_ctx_2, w_mod_2, b_mod_2, g_attn_2, g_ffn_2, na_w_qkv_2, na_g_q_2,
    na_g_k_2, na_rpb_2, na_w_o_2, swa_w_qkv_2, swa_g_q_2, swa_g_k_2, swa_sink_2, swa_w_o_2,
    ga_w_qkv_2, ga_g_q_2, ga_g_k_2, ga_w_o_2, ffn_w_up_2, ffn_conv_w_2, ffn_conv_b_2,
    ffn_w_down_2,
):
    x = first_block(
        x, attn_norm_g, w_in, ret_decay_fwd, ret_decay_bwd, ret_norm_g, dq_norm_g, dk_norm_g,
        lambda_q1, lambda_k1, lambda_q2, lambda_k2, diff_norm_g, w_out, ffn_norm_g, w_gate,
        w_up, w_down,
    )
    return second_block(
        x, c_2, ctx_2, c_ctx_2, w_mod_2, b_mod_2, g_attn_2, g_ffn_2, na_w_qkv_2, na_g_q_2,
        na_g_k_2, na_rpb_2, na_w_o_2, swa_w_qkv_2, swa_g_q_2, swa_g_k_2, swa_sink_2, swa_w_o_2,
        ga_w_qkv_2, ga_g_q_2, ga_g_k_2, ga_w_o_2, ffn_w_up_2, ffn_conv_w_2, ffn_conv_b_2,
        ffn_w_down_2,
    )


_drawn_inputs = setup_inputs


def setup_inputs(seed=0):
    import zlib

    import numpy as np

    out = dict(_drawn_inputs(seed))
    spreads = {}
    factors = {'ret_norm_g': 4.442,
     'dq_norm_g': 4.166,
     'dk_norm_g': 4.032,
     'lambda_q1': 2.861,
     'diff_norm_g': 3.921,
     'ffn_norm_g': 2.939,
     'ctx_2': 3.268,
     'b_mod_2': 3.475,
     'g_attn_2': 8.0,
     'g_ffn_2': 8.0,
     'na_g_q_2': 8.0,
     'na_g_k_2': 8.0,
     'na_rpb_2': 8.0,
     'swa_g_q_2': 8.0,
     'swa_g_k_2': 21.518,
     'swa_sink_2': 8.0,
     'ffn_conv_b_2': 8.0}
    for name, (base, spread) in spreads.items():
        noise = np.random.default_rng([zlib.crc32(name.encode()), seed]).standard_normal(out[name].shape)
        drawn = base * np.exp(spread * noise) if base else spread * noise
        out[name] = jnp.asarray(drawn.astype(out[name].dtype))
    for name, factor in factors.items():
        out[name] = (out[name] * factor).astype(out[name].dtype)
    return out
```

```python
from contextlib import ExitStack

import concourse.bass as bass
from concourse import mybir
import numpy as np

P = 128
D = 1024
KT = D // P
S = 512
C = 256
T2 = S + C
DEPTH = 2
HD = 64
D_FF = 2816
FT = D_FF // P
FH = FT // 2
GRID = 64
ROWS = S // GRID
EPS = 1e-6
NEG = -1e30
UNIT = FH * P
STRIP = S + S - P
CTX_AT = S + 2
ACTW = CTX_AT + C

ALU = mybir.AluOpType
ACT = mybir.ActivationFunctionType
F32 = mybir.dt.float32
F32R = mybir.dt.float32r
AX_X = mybir.AxisListType.X

SMALL = {}


def _small(name, width):
    SMALL[name] = (sum(w for _, w in SMALL.values()), width)


for _name, _width in (
    ("g_attn", DEPTH * KT), ("g_ffn", DEPTH * KT), ("g_ret", DEPTH), ("g_diff", DEPTH),
    ("g_dqk", DEPTH * 8), ("g_na", 16), ("g_swa", 10), ("decay", DEPTH * 16), ("slope", 4),
    ("sink", 16), ("conv", DEPTH * 2 * FT * 4), ("g2_attn", DEPTH * KT * 2), ("g2_ffn", DEPTH * KT * 2),
    ("b_mod", DEPTH * 48 * 2),
):
    _small(_name, _width)
NSMALL = sum(w for _, w in SMALL.values())

IDENT, MEAN64, MEAN128, MEAN1024, ROT = range(5)

MOD_UNITS = 2 * DEPTH * 48

BEGUN = 1

KEY_COL = [0, 8, 24, 32]
MASK_KIND = [0, 1, 1, 2]


def schedule():
    phases, count = [], {"unit": 0, "norm": 0, "part": 0, "hn": 0, "fin": 0, "glu": 0, "conv": 0, "na": 0}

    def add(kind, **kw):
        kw.update(kind=kind, **{k + "0": v for k, v in count.items()})
        phases.append(kw)

    def norm(block, layer, which, T):
        add("norm", block=block, layer=layer, which=which, T=T)
        count["norm"] += 1
        count["part"] += KT * len(segments(T))

    def proj(weight, first, units, T, tile0, func="copy"):
        add("proj", weight=weight, first=first, units=units, T=T, tile0=tile0, func=func, K=KT)
        count["unit"] += units

    def normed(weight, first, units, T, tile0, gains):
        add("normed", weight=weight, first=first, units=units, T=T, tile0=tile0, gains=gains, K=KT)
        count["unit"] += units
        count["hn"] += units

    def resid(weight, first, T, gate, K):
        add("resid", weight=weight, first=first, units=KT, T=T, gate=gate, K=K)
        count["unit"] += KT

    def hidden(kind, weight, first, T, layer, half):
        add(kind, weight=weight, first=first, units=2 * FH, T=T, layer=layer, half=half, K=KT)
        count["unit"] += 2 * FH
        count[kind] += FH

    for l in range(DEPTH):
        norm(1, l, "attn", S)
        normed("w_in", 28 * l, 8, S, 0, ("g_dqk", 8 * l))
        proj("w_in", 28 * l + 8, 16, S, 8)
        proj("w_in", 28 * l + 24, 4, S, 24, "silu")
        add("retention", layer=l)
        add("diff", layer=l)
        add("fin1", layer=l)
        count["fin"] += 8
        resid("w_out", 8 * l, S, None, KT)
        norm(1, l, "ffn", S)
        for half in range(2):
            hidden("glu", "w_gu", 44 * l + 22 * half, S, l, half)
            resid("w_down", 16 * l + 8 * half, S, None, FH)
    norm(2, 0, "attn", T2)
    normed("na_qkv", 0, 16, T2, 0, ("g_na", 0))
    proj("na_qkv", 16, 8, T2, 16)
    add("na")
    add("fin2", T=T2)
    count["fin"] += 8
    resid("na_o", 0, T2, (0, 2), KT)
    norm(2, 0, "ffn", T2)
    for half in range(2):
        hidden("conv", "w_up2", 22 * half, T2, 0, half)
        resid("w_down2", 8 * half, T2, (0, 5), FH)
    norm(2, 1, "attn", T2)
    normed("swa_qkv", 0, 8, S, 0, ("g_swa", 0))
    normed("swa_qkv", 8, 2, T2, 8, ("g_swa", 8))
    proj("swa_qkv", 10, 2, T2, 10)
    add("swa")
    add("fin2", T=S)
    count["fin"] += 8
    resid("swa_o", 0, S, (1, 2), KT)
    norm(2, 1, "ffn", S)
    for half in range(2):
        hidden("conv", "w_up2", 44 + 22 * half, S, 1, half)
        resid("w_down2", 16 + 8 * half, S, (1, 5), FH)
    add("end")
    return phases


def ahead(phases):
    out, moved = [], None
    for n, ph in enumerate(phases):
        if ph["kind"] in ("retention", "na", "swa"):
            moved = next(p for p in phases[n:] if "weight" in p)
            out.append(dict(moved, pairs=(0, 1)))
        out.append(dict(ph, pairs=(1, ph["units"] // 2)) if ph is moved else ph)
    return out


def segments(T, at=S):
    segs = [(0, 0, S, 0)]
    if T == T2:
        segs.append((S, at, C, 1))
    return segs


def _f_y(n):
    return 2 * (n + 1) if n < 4 else 8 + (n - 3)


def build(nc, d, out):
    phases = schedule()
    total_units = phases[-1]["unit0"]

    with ExitStack() as stack:
        def sem(name):
            return stack.enter_context(nc.semaphore(name))

        top = [nc.sbuf_base]
        names = [0]

        def at(offset, shape, dt=F32, name="t"):
            names[0] += 1
            return nc.alloc_sbuf_tensor_at(f"{name}{names[0]}", shape, dt, offset=offset)

        def nbytes(shape):
            n = 4
            for s in shape[1:]:
                n *= s
            return (n + 31) // 32 * 32

        def sb(name, shape, dt=F32):
            t = at(top[0], shape, dt, name)
            top[0] += nbytes(shape)
            return t

        class Area:

            def __init__(self, offset, size):
                self.offset, self.end = offset, offset + size

            def __call__(self, name, shape, dt=F32):
                t = at(self.offset, shape, dt, name)
                self.offset += nbytes(shape)
                assert self.offset <= self.end, (name, self.offset - self.end)
                return t

        top[0] = (top[0] + 31) // 32 * 32
        base = top[0]
        xT = sb("xT", [P, KT, T2])
        h_at = top[0]
        h_hi = sb("h_hi", [P, KT, T2], F32R)
        h_lo = sb("h_lo", [P, KT, T2], F32R)
        h_size = top[0] - h_at
        w_raw = [sb(f"w_raw{i}", [P, UNIT]) for i in range(2)]
        w_hi = [sb(f"w_hi{i}", [P, UNIT], F32R) for i in range(2)]
        w_lo = [sb(f"w_lo{i}", [P, UNIT], F32R) for i in range(2)]
        small = sb("small", [P, NSMALL])
        mats = sb("mats", [P, 5, P])
        mod = sb("mod", [P, DEPTH, 6, KT, 2])
        gs = sb("gs", [P, DEPTH, 2, KT, 2])
        mod_sum = sb("mod_sum", [P, 2])
        zero1 = sb("zero1", [P, 1])
        eps1 = sb("eps1", [P, 1])
        lgam = sb("lgam", [P, DEPTH * 16])
        lam = sb("lam", [P, 16])
        stats = sb("stats", [P, 24])
        pace = sb("pace", [P, 4])
        wide_at = top[0]
        wide_size = nbytes([P, 24, T2])
        top[0] += wide_size
        temp_at = top[0]
        temp_size = 4 * nbytes([P, 4 + ACTW])
        top[0] += temp_size
        assert top[0] <= nc.sbuf_usable_end, (top[0], nc.sbuf_usable_end)

        wide = Area(wide_at, wide_size)
        proj = wide("proj", [P, 24, T2])
        proj1 = at(wide_at, [P, 28, S], F32, "proj1")
        wide = Area(wide_at, wide_size)
        a_hi = wide("a_hi", [P, FH, ACTW], F32R)
        a_lo = wide("a_lo", [P, FH, ACTW], F32R)
        wide = Area(wide_at, wide_size)
        b_hi = wide("b_hi", [P, FH, S], F32R)
        b_lo = wide("b_lo", [P, FH, S], F32R)
        wide = Area(wide_at, wide_size)
        n_sq = [wide(f"n_sq{i}", [P, T2]) for i in range(2)]
        n_rstd = wide("n_rstd", [P, T2])
        n_xn = [wide(f"n_xn{i}", [P, T2]) for i in range(2)]
        wide = Area(wide_at, wide_size)
        lam_vec = wide("lam_vec", [P, DEPTH * 4, HD])
        lam_prod = wide("lam_prod", [P, HD])

        wide = Area(wide_at + nbytes([P, 28, S]), wide_size - nbytes([P, 28, S]))
        mod_w = wide("mod_w", [P, D])
        mod_junk = wide("mod_junk", [P, D])
        silu_c = wide("silu_c", [P, 2, D])

        temp = Area(temp_at, temp_size)
        u_pad = [temp(f"u_pad{i}", [P, 4 + ACTW]) for i in range(2)]
        conv_y = [temp(f"conv_y{i}", [P, ACTW]) for i in range(2)]
        temp = Area(temp_at, temp_size)
        hn_sq = [temp(f"hn_sq{i}", [P, T2]) for i in range(2)]
        hn_r = [temp(f"hn_r{i}", [P, T2]) for i in range(2)]
        temp = Area(temp_at, temp_size)
        f_sq = [temp(f"f_sq{i}", [P, S]) for i in range(2)]
        f_r = [temp(f"f_r{i}", [P, S]) for i in range(2)]
        temp = Area(temp_at, temp_size)
        glu_g = temp("glu_g", [P, S])
        glu_a = temp("glu_a", [P, S])

        area = Area(h_at, h_size)
        r_q, r_k, r_v = (area(f"r_{n}", [P, S]) for n in "qkv")
        r_vs = area("r_vs", [P, 4, P])
        r_dpos, r_dneg, r_tmp = (area(f"r_d{n}", [P, STRIP]) for n in "pnt")
        r_mask = [area(f"r_mask{i}", [P, STRIP]) for i in range(2)]
        r_sc = [area(f"r_sc{i}", [P, S]) for i in range(3)]
        d_dist = area("d_dist", [P, STRIP])
        d_dist_at = area.offset - nbytes([P, STRIP])
        area = Area(h_at, d_dist_at - h_at)
        d_q, d_k, d_v = (area(f"d_{n}", [P, S]) for n in "qkv")
        d_vs = area("d_vs", [P, 4, P])
        d_bias = area("d_bias", [P, STRIP])
        d_s = [area(f"d_s{i}", [P, S]) for i in range(4)]
        d_aT = area("d_aT", [P, 4, S])
        area = Area(h_at, h_size)
        n_q, n_k, n_v = (area(f"n_{n}", [P, T2]) for n in "qkv")
        n_vs = area("n_vs", [P, 9, P])
        n_s = [area(f"n_s{i}", [P, S]) for i in range(3)]
        n_pT = [area(f"n_pT{i}", [P, S]) for i in range(2)]
        n_bias = area("n_bias", [P, 2, 3, S])
        n_rpb = area("n_rpb", [P, 2, ROWS * 48])
        n_mask = area("n_mask", [P, 3, 2 * P])
        area = Area(h_at, h_size)
        s_q = area("s_q", [P, S])
        s_k, s_v = (area(f"s_{n}", [P, T2]) for n in "kv")
        s_vs = area("s_vs", [P, 6, P])
        s_s = [area(f"s_s{i}", [P, 5 * P + 8]) for i in range(3)]
        s_pT = [area(f"s_pT{i}", [P, 5 * P]) for i in range(2)]
        s_band = area("s_band", [P, 9 * P])
        s_cos, s_sin, s_t1, s_t2 = (area(f"s_{n}", [P, S]) for n in ("cos", "sin", "t1", "t2"))

        ps = stack.enter_context(nc.psum_tensor("ps", [P, 8 * 512], F32))
        acc = [ps[:, 1024 * i:1024 * i + 1024] for i in range(2)]
        sums = [ps[:, 2048 + 1024 * i:3072 + 1024 * i] for i in range(2)]

        def bank(i, n=512):
            return ps[:, 512 * i:512 * i + n]

        loaded = sem("loaded")
        ready = sem("ready")
        w_loaded = [sem(f"w_loaded{i}") for i in range(2)]
        w_hi_ready = sem("w_hi_ready")
        w_lo_ready = sem("w_lo_ready")
        mm_done = sem("mm_done")
        acc_free = sem("acc_free")
        mod_loaded, mod_step, mod_kept = sem("mod_loaded"), sem("mod_step"), sem("mod_kept")
        silu_c_ready, mod_ready = sem("silu_c_ready"), sem("mod_ready")
        lam_step, lam_exp = sem("lam_step"), sem("lam_exp")
        n_sq_ready, n_sum, n_std = sem("n_sq_ready"), sem("n_sum"), sem("n_std")
        n_recip, n_xn_ready, n_hi, n_lo = sem("n_recip"), sem("n_xn_ready"), sem("n_hi"), sem("n_lo")
        hn_sq_ready, hn_sum, hn_std = sem("hn_sq_ready"), sem("hn_sum"), sem("hn_std")
        hn_recip, hn_out = sem("hn_recip"), sem("hn_out")
        glu_g_ready, a_lo_ready = sem("glu_g_ready"), sem("a_lo_ready")
        conv_step, conv_gate, conv_hi = sem("conv_step"), sem("conv_gate"), sem("conv_hi")
        conv_zero, glu_hi = sem("conv_zero"), sem("glu_hi")
        f_sq_ready, f_sum, f_std, f_recip = sem("f_sq_ready"), sem("f_sum"), sem("f_std"), sem("f_recip")
        f_y_ready, f_hi, f_lo = sem("f_y_ready"), sem("f_hi"), sem("f_lo")
        tab = {k: sem("tab_" + k) for k in ("retention", "na", "swa")}
        sems = {}
        for k, stage in (("r", "retention"), ("d", "diff"), ("n", "neighbour"), ("s", "sliding")):
            sems[k] = {n: sem(f"{stage}_{n}") for n in (
                "staged_act", "staged_dve", "v_turned", "v_kept", "scored", "biased", "negmax",
                "exped", "recip", "probs", "turned", "kept", "summed", "evacuated", "bias", "mask_arg")}
        rope_mm, rope_a, rope_b, rope_out = sem("rope_mm"), sem("rope_a"), sem("rope_b"), sem("rope_out")
        rpb_loaded = sem("rpb_loaded")
        stored = sem("stored")

        block = stack.enter_context(nc.Block())

        def begin(eng, names, others=()):
            for k in sems:
                for n in names:
                    eng.sem_inc(sems[k][n], BEGUN)
            for s_ in others:
                eng.sem_inc(s_, BEGUN)

        def col(name, i=0, n=1):
            return small[:, SMALL[name][0] + i:SMALL[name][0] + i + n]

        def dcol(name, i):
            return small[:, bass.ds(SMALL[name][0] + i, 1)]

        def pairs(eng, ph, body):
            begin_, end = ph.get("pairs", (0, ph["units"] // 2))
            if ph["unit0"] == 0:
                body(0, True)
                begin_ = 1
            if end - begin_ == 1:
                body(begin_, False)
            elif end > begin_:
                with eng.Fori(begin_, end) as i:
                    body(i, False)

        def dyn(i):
            return bass.ds(i, 1)

        def mat(i):
            return mats[:, i, :]

        N_INPUTS = 16 * 6

        @block.sync
        def _(sp):
            def weights(ph):
                u0 = ph["unit0"]

                def body(i, first):
                    for par in range(2):
                        if not first:
                            sp.wait_ge(w_lo_ready, i * 2 + (u0 + par - 1))
                        sp.dma_start(w_raw[par][:, 0:ph["K"] * P].rearrange("p (a n) -> p a n", a=1),
                                     d[ph["weight"]][bass.ds(i * 2 + (ph["first"] + par), 1)].rearrange(
                                         "a p n -> p a n")).then_inc(w_loaded[par], 16)
                    if u0 < MOD_UNITS:
                        if not first:
                            sp.wait_ge(mod_step, i * 2 + u0)
                        sp.dma_start(mod_w[:].rearrange("p (a n) -> p a n", a=1),
                                     d["w_mod"][bass.ds(i + u0 // 2, 1)].rearrange("a p n -> p a n")
                                     ).then_inc(mod_loaded, 16)
                pairs(sp, ph, body)

            for ph in ahead(phases):
                if "weight" in ph:
                    weights(ph)
                elif ph["kind"] == "retention":
                    sp.wait_ge(mm_done, ph["unit0"])
                    sp.dma_start(r_dpos[:], d["dist"][0]).then_inc(tab["retention"], 16)
                    sp.dma_start(r_dneg[:], d["dist"][1]).then_inc(tab["retention"], 16)
                    sp.dma_start(d_dist[:], d["dist"][2]).then_inc(tab["retention"], 16)
                elif ph["kind"] == "na":
                    sp.wait_ge(mm_done, ph["unit0"])
                    sp.dma_start(n_mask[:], d["na_mask"]).then_inc(tab["na"], 16)
                    sp.dma_start(n_rpb[:], d["rpb"][0]).then_inc(rpb_loaded, 16)
                    with sp.Fori(1, 8) as j:
                        sp.wait_ge(sems["n"]["bias"], j * 6)
                        sp.dma_start(n_rpb[:].rearrange("p (a h) n -> p a h n", a=1),
                                     d["rpb"][bass.ds(j, 1)].rearrange("a p h n -> p a h n")
                                     ).then_inc(rpb_loaded, 16)
                elif ph["kind"] == "swa":
                    sp.wait_ge(mm_done, ph["unit0"])
                    sp.dma_start(s_band[:], d["band"]).then_inc(tab["swa"], 16)
                    sp.dma_start(s_cos[:], d["rope"][0]).then_inc(tab["swa"], 16)
                    sp.dma_start(s_sin[:], d["rope"][1]).then_inc(tab["swa"], 16)
            sp.wait_ge(acc_free, total_units)
            sp.dma_start(out, xT[:, :, 0:S]).then_inc(stored, 16)
            sp.wait_ge(stored, 16)

        @block.gpsimd
        def _(pool):
            def split(ph):
                u0, cols = ph["unit0"], ph["K"] * P

                def body(i, first):
                    for par in range(2):
                        pool.wait_ge(w_hi_ready, i * 2 + (u0 + par + 1))
                        pool.tensor_tensor(w_lo[par][:, 0:cols], w_raw[par][:, 0:cols],
                                           w_hi[par][:, 0:cols].bitcast(F32), ALU.subtract).then_inc(w_lo_ready, 1)
                pairs(pool, ph, body)

            def na_bias(ph):
                q = sems["n"]
                pool.wait_ge(tab["na"], 16)
                with pool.Fori(0, 8) as j:
                    pool.wait_ge(rpb_loaded, j * 16 + 16)
                    pool.wait_ge(q["biased"], BEGUN + j * 12)
                    for hd in range(2):
                        for kind, off in enumerate((16, 8, 0)):
                            strip = n_rpb[:, hd, :].rearrange("p (r u) -> p r u", u=48)
                            pool.tensor_tensor(
                                n_bias[:, hd, kind, 0:2 * P].rearrange("p (i r c) -> p i r c", i=4, c=8),
                                strip[:, :, off:off + 32].rearrange("p r (i c) -> p i r c", c=8),
                                n_mask[:, kind, :].rearrange("p (i r c) -> p i r c", i=4, c=8),
                                ALU.add).then_inc(q["bias"], 1)

            def rope(ph):
                pool.wait_ge(tab["swa"], 48)
                pool.wait_ge(hn_out, ph["hn0"])
                pool.wait_ge(mm_done, ph["unit0"])
                for kv in range(2):
                    n = 5 * kv
                    pool.wait_ge(acc_free, ph["unit0"])
                    if kv:
                        pool.wait_ge(sems["s"]["scored"], BEGUN + 32)
                    pool.tensor_tensor(s_t2[:], proj[:, 8 + kv, 0:S], s_cos[:], ALU.mult).then_inc(rope_b, 1)
                    pool.wait_ge(rope_a, n + 1)
                    pool.wait_ge(rope_b, n + 1)
                    pool.tensor_tensor(s_k[:, 0:S], s_t1[:], s_t2[:], ALU.add).then_inc(rope_out, 1)
                    with pool.Fori(0, 4) as g:
                        pool.wait_ge(rope_out, g * 1 + (n + 1))
                        pool.tensor_tensor(s_t2[:].rearrange("p (a n) -> p a n", a=1),
                                           proj[:, bass.ds(g + 4 * kv, 1), 0:S],
                                           s_cos[:].rearrange("p (a n) -> p a n", a=1), ALU.mult).then_inc(rope_b, 1)
                        pool.wait_ge(rope_a, g + (n + 2))
                        pool.wait_ge(rope_b, g + (n + 2))
                        pool.wait_ge(sems["s"]["scored"], BEGUN + g * 8 + 32 * kv)
                        pool.tensor_tensor(s_q[:], s_t1[:], s_t2[:], ALU.add).then_inc(rope_out, 1)

            for ph in ahead(phases):
                if "weight" in ph:
                    split(ph)
                elif ph["kind"] == "na":
                    na_bias(ph)
                elif ph["kind"] == "swa":
                    rope(ph)

        @block.tensor
        def _(pe):
            def unit(ph, i, par, first):
                u0, K = ph["unit0"], ph["K"]
                hidden = ph["K"] == FH
                hi, lo = (h_hi, h_lo) if not hidden else (b_hi, b_lo) if u0 < MOD_UNITS else (a_hi, a_lo)
                segs = segments(ph["T"], CTX_AT if hidden else S)
                pe.wait_ge(w_lo_ready, i * 2 + (u0 + par + 1))
                if not first:
                    pe.wait_ge(acc_free, i * 2 + (u0 + par - 1))
                for k in range(K):
                    for w, r, begin, end in ((w_hi, hi, k == 0, False), (w_hi, lo, False, False),
                                             (w_lo, hi, False, k == K - 1)):
                        for to, frm, n, _ in segs:
                            last = pe.matmul(acc[par][:, to:to + n], w[par][:, k * P:k * P + P],
                                             r[:, k, frm:frm + n], start=begin, stop=end)
                last.then_inc(mm_done, 1)

            def plain_units(ph):
                def body(i, first):
                    for par in range(2):
                        unit(ph, i, par, first)
                pairs(pe, ph, body)

            def head_sum(ph, n, par):
                pe.wait_ge(hn_sq_ready, n + (ph["hn0"] + 1))
                for to, _, w, _ in segments(ph["T"]):
                    last = pe.matmul(sums[par][:, to:to + w], mat(MEAN64), hn_sq[par][:, to:to + w],
                                     start=True, stop=True)
                last.then_inc(hn_sum, 1)

            def normed_units(ph):
                first = ph["unit0"] == 0
                unit(ph, 0, 0, first)
                unit(ph, 0, 1, first)
                head_sum(ph, 0, 0)
                if ph["units"] > 2:
                    with pe.Fori(1, ph["units"] // 2) as i:
                        unit(ph, i, 0, False)
                        head_sum(ph, i * 2 - 1, 1)
                        unit(ph, i, 1, False)
                        head_sum(ph, i * 2, 0)
                head_sum(ph, ph["units"] - 1, 1)

            def norm(ph):
                n0 = 8 * ph["norm0"]
                for k in range(KT):
                    pe.wait_ge(n_sq_ready, n0 + k + 1)
                    for to, _, w, _ in segments(ph["T"]):
                        last = pe.matmul(sums[0][:, to:to + w], mat(MEAN1024), n_sq[k % 2][:, to:to + w],
                                         start=(k == 0), stop=(k == KT - 1))
                    last.then_inc(n_sum, 1)

            def retention(ph):
                q = sems["r"]
                l = ph["layer"]
                with pe.Fori(0, 4) as j:
                    pe.wait_ge(q["staged_act"], j * 1 + (4 * l + 1))
                    pe.wait_ge(q["staged_dve"], j * 2 + (8 * l + 2))
                    pe.wait_ge(q["evacuated"], BEGUN + j * 2 + 8 * l)
                    pe.wait_ge(acc_free, ph["unit0"])
                    for t in range(4):
                        last = pe.transpose(bank(0)[:, t * P:t * P + P], r_v[:, t * P:t * P + P], mat(IDENT))
                    last.then_inc(q["v_turned"], 1)

                    def score(t):
                        hd, s = divmod(t, 4)
                        half = slice(HD * hd, HD * hd + HD)
                        if t >= 2:
                            pe.wait_ge(q["biased"], BEGUN + j * 8 + (32 * l + t - 1))
                        pe.matmul(bank(4 + t % 2), r_k[half, s * P:s * P + P], r_q[half, :],
                                  start=True, stop=True).then_inc(q["scored"], 1)

                    def values(t):
                        hd, s = divmod(t, 4)
                        pe.wait_ge(q["v_kept"], j * 1 + (4 * l + 1))
                        pe.wait_ge(q["biased"], BEGUN + j * 8 + (32 * l + t + 1))
                        pe.matmul(bank(2 + hd), r_vs[:, s, :], r_sc[t % 3][:],
                                  start=(s == 0), stop=(s == 3)).then_inc(q["summed"], 1)

                    for t in range(8 + 1):
                        if t < 8:
                            score(t)
                        if t >= 1:
                            values(t - 1)

            def diff(ph):
                q = sems["d"]
                l = ph["layer"]
                pe.wait_ge(sems["r"]["evacuated"], BEGUN + 8 * (l + 1))
                with pe.Fori(0, 4) as j:
                    pe.wait_ge(q["staged_act"], j * 1 + (4 * l + 1))
                    pe.wait_ge(q["staged_dve"], j * 2 + (8 * l + 2))
                    pe.wait_ge(q["kept"], BEGUN + j * 4 + 16 * l)
                    for t in range(4):
                        last = pe.transpose(bank(0)[:, t * P:t * P + P], d_v[:, t * P:t * P + P], mat(IDENT))
                    last.then_inc(q["v_turned"], 1)

                    def score(t):
                        b, m = divmod(t, 2)
                        half = slice(HD * m, HD * m + HD)
                        if t >= 4:
                            pe.wait_ge(q["biased"], BEGUN + j * 8 + (32 * l + t - 3))
                        pe.matmul(bank(4 + t % 4), d_q[half, b * P:b * P + P], d_k[half, :],
                                  start=True, stop=True).then_inc(q["scored"], 1)

                    def turn(b):
                        pe.wait_ge(q["probs"], BEGUN + j * 8 + (32 * l + 2 * b + 2))
                        pe.wait_ge(q["v_kept"], j * 1 + (4 * l + 1))
                        if b >= 2:
                            pe.wait_ge(q["kept"], BEGUN + j * 4 + (16 * l + b - 1))
                        for t in range(4):
                            last = pe.transpose(bank(b % 2)[:, t * P:t * P + P],
                                                d_s[2 * b % 4][:, t * P:t * P + P], mat(IDENT))
                        last.then_inc(q["turned"], 1)

                    for b in range(4 + 1):
                        if b < 4:
                            score(2 * b)
                            score(2 * b + 1)
                        if b >= 1:
                            turn(b - 1)
                    pe.wait_ge(q["kept"], BEGUN + j * 4 + (16 * l + 4))
                    pe.wait_ge(q["evacuated"], BEGUN + j * 1 + 4 * l)
                    for t in range(4):
                        last = pe.matmul(bank(2), d_vs[:, t, :], d_aT[:, t, :], start=(t == 0), stop=(t == 3))
                    last.then_inc(q["summed"], 1)

            def fin1(ph):
                for n in range(8):
                    pe.wait_ge(f_sq_ready, 8 * ph["layer"] + n + 1)
                    if n == 0:
                        pe.wait_ge(sems["d"]["biased"], BEGUN + 32 * (ph["layer"] + 1))
                    if n >= 2:
                        pe.wait_ge(f_std, 8 * ph["layer"] + n - 1)
                    pe.matmul(bank(4 + n % 2), mat(MEAN64 if n < 4 else MEAN128), f_sq[n % 2][:],
                              start=True, stop=True).then_inc(f_sum, 1)

            def na(ph):
                q = sems["n"]

                with pe.Fori(0, 8) as j:
                    pe.wait_ge(q["staged_act"], j * 2 + 2)
                    pe.wait_ge(q["staged_dve"], j * 4 + 4)
                    pe.wait_ge(q["kept"], BEGUN + j * 12)
                    pe.wait_ge(q["evacuated"], BEGUN + j * 4)
                    pe.wait_ge(acc_free, ph["unit0"])
                    for t in range(9):
                        frm = 8 * ROWS * t if t < 7 else S + (t - 7) * P
                        src = n_v[:, frm:frm + P]
                        last = pe.transpose(bank(t // 4)[:, t % 4 * P:t % 4 * P + P], src, mat(IDENT))
                    last.then_inc(q["v_turned"], 1)

                    def score(t):
                        hd, b = divmod(t, 6)
                        half = slice(HD * hd, HD * hd + HD)
                        if t >= 2:
                            pe.wait_ge(q["biased"], BEGUN + j * 12 + (t - 1))
                        S_ = bank(4 + t % 2)
                        if b < 4:
                            queries = n_q[half, b * P:b * P + P]
                            frm = KEY_COL[b] * ROWS
                            pe.matmul(S_[:, 0:2 * P], queries, n_k[half, frm:frm + 2 * P], start=True, stop=True)
                            pe.matmul(S_[:, 2 * P:4 * P], queries, n_k[half, S:T2],
                                      start=True, stop=True).then_inc(q["scored"], 1)
                        else:
                            pe.matmul(S_[:, 0:C], n_q[half, S + (b - 4) * P:S + (b - 3) * P],
                                      n_k[half, S:T2], start=True, stop=True).then_inc(q["scored"], 1)

                    def turn(t):
                        b = t % 6
                        pe.wait_ge(q["probs"], BEGUN + j * 12 + (t + 1))
                        if t >= 2:
                            pe.wait_ge(q["kept"], BEGUN + j * 12 + (t - 1))
                        else:
                            pe.wait_ge(q["v_kept"], j * 1 + 1)
                        for c in range(4 if b < 4 else 2):
                            last = pe.transpose(bank(t % 2)[:, c * P:c * P + P],
                                                n_s[t % 3][:, c * P:c * P + P], mat(IDENT))
                        last.then_inc(q["turned"], 1)

                    def values(t):
                        hd, b = divmod(t, 6)
                        pe.wait_ge(q["kept"], BEGUN + j * 12 + (t + 1))
                        if hd and b == 0:
                            pe.wait_ge(q["evacuated"], BEGUN + j * 4 + 2)
                        if b < 4:
                            o = bank(2)[:, b * P:b * P + P]
                            tiles = [KEY_COL[b] // 8, KEY_COL[b] // 8 + 2, 7, 8]
                        else:
                            o = bank(3)[:, (b - 4) * P:(b - 3) * P]
                            tiles = [7, 8]
                        for c, v in enumerate(tiles):
                            last = pe.matmul(o, n_vs[:, v, :], n_pT[t % 2][:, c * P:c * P + P],
                                             start=(c == 0), stop=(c == len(tiles) - 1))
                        last.then_inc(q["summed"], 1)

                    for t in range(12 + 2):
                        if t < 12:
                            score(t)
                        if 1 <= t <= 12:
                            turn(t - 1)
                        if t >= 2:
                            values(t - 2)

            def swa(ph):
                q = sems["s"]
                pe.wait_ge(acc_free, ph["unit0"])
                pe.wait_ge(hn_out, ph["hn0"])
                for kv in range(2):
                    if kv:
                        pe.wait_ge(q["biased"], BEGUN + 32)
                    pe.matmul(bank(6), mat(ROT), proj[:, 8 + kv, 0:S], start=True, stop=True).then_inc(rope_mm, 1)
                    pe.wait_ge(q["staged_dve"], kv + 1)
                    if kv:
                        pe.wait_ge(q["kept"], BEGUN + 32)
                    for t in range(6):
                        last = pe.transpose(bank(t // 4)[:, t % 4 * P:t % 4 * P + P],
                                            s_v[:, t * P:t * P + P], mat(IDENT))
                    last.then_inc(q["v_turned"], 1)
                    with pe.Fori(0, 4) as g:
                        n = g * 8 + 32 * kv
                        pe.wait_ge(rope_a, g + (5 * kv + 1))
                        pe.wait_ge(q["biased"], BEGUN + n)
                        pe.matmul(bank(6).rearrange("p (a n) -> p a n", a=1), mat(ROT),
                                  proj[:, bass.ds(g + 4 * kv, 1), 0:S], start=True, stop=True).then_inc(rope_mm, 1)
                        pe.wait_ge(rope_out, g + (5 * kv + 2))
                        pe.wait_ge(q["staged_act"], kv + 1)

                        def score(t):
                            hd, b = divmod(t, 4)
                            half = slice(HD * hd, HD * hd + HD)
                            if t >= 2:
                                pe.wait_ge(q["biased"], BEGUN + n + (t - 1))
                            S_ = sums[t % 2]
                            lo, hi = max(b - 1, 0) * P, min(b + 2, 4) * P
                            queries = s_q[half, b * P:b * P + P]
                            pe.matmul(S_[:, 0:hi - lo], queries, s_k[half, lo:hi], start=True, stop=True)
                            for c in range(2):
                                at_ = hi - lo + c * P
                                last = pe.matmul(S_[:, at_:at_ + P], queries,
                                                 s_k[half, S + c * P:S + c * P + P], start=True, stop=True)
                            last.then_inc(q["scored"], 1)

                        def turn(t):
                            b = t % 4
                            pe.wait_ge(q["probs"], BEGUN + n + (t + 1))
                            if t >= 1:
                                pe.wait_ge(q["kept"], BEGUN + n + t)
                            else:
                                pe.wait_ge(q["kept"], BEGUN + n)
                                pe.wait_ge(q["v_kept"], kv + 1)
                            for c in range(5 if 0 < b < 3 else 4):
                                last = pe.transpose(ps[:, c * P:c * P + P],
                                                    s_s[t % 3][:, c * P:c * P + P], mat(IDENT))
                            last.then_inc(q["turned"], 1)

                        def values(t):
                            hd, b = divmod(t, 4)
                            pe.wait_ge(q["kept"], BEGUN + n + (t + 1))
                            if b == 0:
                                pe.wait_ge(q["evacuated"], BEGUN + g * 2 + (8 * kv + hd - 1 + (hd == 0)))
                            lo, hi = max(b - 1, 0), min(b + 2, 4)
                            tiles = list(range(lo, hi)) + [4, 5]
                            for c, v in enumerate(tiles):
                                last = pe.matmul(bank(2 + hd)[:, b * P:b * P + P], s_vs[:, v, :],
                                                 s_pT[t % 2][:, c * P:c * P + P],
                                                 start=(c == 0), stop=(c == len(tiles) - 1))
                            last.then_inc(q["summed"], 1)

                        for t in range(8 + 2):
                            if t < 8:
                                score(t)
                            if 1 <= t <= 8:
                                turn(t - 1)
                            if t >= 2:
                                values(t - 2)

            begin(pe, ("v_turned", "scored", "turned", "summed"))
            pe.wait_ge(loaded, N_INPUTS)
            for ph in phases:
                kind = ph["kind"]
                if kind == "norm":
                    norm(ph)
                    pe.wait_ge(n_lo, ph["part0"] + KT * len(segments(ph["T"])))
                elif kind == "normed":
                    normed_units(ph)
                elif kind in ("proj", "glu", "conv"):
                    plain_units(ph)
                elif kind == "resid":
                    if ph["K"] == FH:
                        pe.wait_ge(a_lo_ready, BEGUN + ph["glu0"] + ph["conv0"])
                    else:
                        pe.wait_ge(f_lo, ph["fin0"])
                    plain_units(ph)
                elif kind == "retention":
                    pe.wait_ge(hn_out, ph["hn0"])
                    retention(ph)
                elif kind == "diff":
                    diff(ph)
                elif kind == "fin1":
                    fin1(ph)
                elif kind == "na":
                    pe.wait_ge(hn_out, ph["hn0"])
                    na(ph)
                elif kind == "swa":
                    swa(ph)

        @block.scalar
        def _(act):
            begin(act, ("kept",))
            act.dma_start(xT[:, :, 0:S], d["x"]).then_inc(loaded, 16)
            act.dma_start(xT[:, :, S:T2], d["ctx"]).then_inc(loaded, 16)
            act.dma_start(small[:], d["small"]).then_inc(loaded, 16)
            act.dma_start(mats[:], d["mats"]).then_inc(loaded, 16)
            act.dma_start(lam_vec[:], d["lam"]).then_inc(loaded, 16)
            act.dma_start(silu_c[:], d["c"]).then_inc(loaded, 16)
            def row(ap):
                return ap.rearrange("p (a n) -> p a n", a=1)

            def hi_part(par, loads, K):
                act.wait_ge(w_loaded[par], loads)
                act.activation(w_hi[par][:, 0:K * P], w_raw[par][:, 0:K * P], ACT.Copy).then_inc(w_hi_ready, 1)

            act.wait_ge(loaded, N_INPUTS)
            for par in range(2):
                hi_part(par, 16, KT)
            act.activation(silu_c[:], silu_c[:], ACT.Silu).then_inc(silu_c_ready, 1)
            act.activation(lgam[:], col("decay", 0, DEPTH * 16), ACT.Exp).then_inc(lam_exp, 1)
            act.wait_ge(lam_step, 4)
            act.activation(lam[:, 4:8], lam[:, 0:4], ACT.Exp).then_inc(lam_exp, 1)
            act.wait_ge(ready, 2)

            def units_of(ph, body, peel=0):
                n, u0 = ph["units"] // 2, ph["unit0"]
                k_next = next((p["K"] for p in phases if p.get("weight") and p["unit0"] == u0 + 2 * n), None)
                same = n if k_next == ph["K"] else n - 1

                def pair(i, K):
                    def split(par):
                        if K is not None:
                            hi_part(par, i * 16 + (8 * u0 + 32), K)
                    body(i, split)

                peel = max(peel, same if same == 1 else 0)
                for i in range(min(peel, n)):
                    pair(i, ph["K"] if i < same else k_next)
                if same > peel:
                    with act.Fori(peel, same) as i:
                        pair(i, ph["K"])
                if same < n and n > peel:
                    pair(n - 1, k_next)

            def resid(ph):
                def body(i, split):
                    for par in range(2):
                        act.wait_ge(mm_done, i * 2 + (ph["unit0"] + par + 1))
                        split(par)
                units_of(ph, body)

            def norm(ph):
                n0, T = ph["norm0"], ph["T"]
                for k in range(KT):
                    if n0:
                        act.wait_ge(acc_free, ph["unit0"] - KT + k + 1)
                    if k == 0 and n0:
                        act.wait_ge(mm_done, ph["unit0"])
                    elif k == 0:
                        act.wait_ge(lam_step, 4)
                    if k >= 2:
                        act.wait_ge(n_sum, 8 * n0 + k - 1)
                    act.activation(n_sq[k % 2][:, 0:T], xT[:, k, 0:T], ACT.Square).then_inc(n_sq_ready, 1)
                act.wait_ge(n_sum, 8 * n0 + 8)
                act.activation(n_rstd[:, 0:T], sums[0][:, 0:T], ACT.Sqrt, bias=eps1[:]).then_inc(n_std, 1)
                parts = ph["part0"]
                for k in range(KT):
                    for to, _, w, c in segments(T):
                        parts += 1
                        act.wait_ge(n_xn_ready, parts)
                        shift = zero1[:] if ph["block"] == 1 else \
                            mod[:, ph["layer"], 0 if ph["which"] == "attn" else 3, k, c:c + 1]
                        act.activation(h_hi[:, k, to:to + w], n_xn[k % 2][:, to:to + w], ACT.Identity,
                                       bias=shift).then_inc(n_hi, 1)

            def take_out(ph):
                def body(i, split):
                    for par in range(2):
                        act.wait_ge(mm_done, i * 2 + (ph["unit0"] + par + 1))
                        dst = proj1 if ph["T"] == S and ph["weight"] == "w_in" else proj
                        act.activation(dst[:, bass.ds(i * 2 + (ph["tile0"] + par), 1), 0:ph["T"]],
                                       row(acc[par][:, 0:ph["T"]]),
                                       ACT.Silu if ph["func"] == "silu" else ACT.Copy).then_inc(acc_free, 1)
                        split(par)
                units_of(ph, body)

            def head_norm(ph):
                T, h0 = ph["T"], ph["hn0"]
                dst = proj1 if ph["weight"] == "w_in" else proj

                def square(i, par):
                    act.wait_ge(acc_free, i * 2 + (ph["unit0"] + par + 1))
                    act.activation(row(hn_sq[par][:, 0:T]), dst[:, bass.ds(i * 2 + (ph["tile0"] + par), 1), 0:T],
                                   ACT.Square).then_inc(hn_sq_ready, 1)

                def root(i, par):
                    act.wait_ge(hn_sum, i * 2 + (h0 + par + 1))
                    if isinstance(i, int):
                        act.wait_ge(hn_out, max(2 * i + h0 + par - 1, h0))
                    else:
                        act.wait_ge(hn_out, i * 2 + (h0 + par - 1))
                    act.activation(hn_r[par][:, 0:T], sums[par][:, 0:T], ACT.Sqrt, bias=eps1[:]).then_inc(hn_std, 1)

                def body(i, split):
                    for par in range(2):
                        act.wait_ge(mm_done, i * 2 + (ph["unit0"] + par + 1))
                        split(par)
                        square(i, par)
                        if par:
                            root(i, 0)
                        elif not (isinstance(i, int) and i == 0):
                            root(i - 1, 1)
                units_of(ph, body, peel=1 if h0 else 2)
                root(ph["units"] // 2 - 1, 1)

            def glu(ph):
                def body(f, split):
                    act.wait_ge(mm_done, f * 2 + (ph["unit0"] + 1))
                    split(0)
                    act.activation(glu_g[:], acc[0][:, 0:S], ACT.Silu).then_inc(glu_g_ready, 1)
                    act.wait_ge(mm_done, f * 2 + (ph["unit0"] + 2))
                    split(1)
                    act.wait_ge(acc_free, f * 2 + (ph["unit0"] + 2))
                    act.activation(b_hi[:, dyn(f), :], row(glu_a[:]), ACT.Copy).then_inc(glu_hi, 1)
                units_of(ph, body)

            def conv(ph):
                n0, T = ph["conv0"], ph["T"]
                W = ACTW if T == T2 else S
                act.wait_ge(acc_free, ph["unit0"])

                def body(f, split):
                    for par in range(2):
                        act.wait_ge(mm_done, f * 2 + (ph["unit0"] + par + 1))
                        split(par)
                        act.wait_ge(conv_step, BEGUN + f * 7 + 7 * n0)
                        for to, frm, n, _ in segments(T, CTX_AT):
                            last = act.activation(u_pad[par][:, 2 + frm:2 + frm + n], acc[par][:, to:to + n], ACT.Copy)
                        last.then_inc(acc_free, 1)
                    act.wait_ge(conv_step, BEGUN + f * 7 + (7 * n0 + 6))
                    act.activation(conv_y[1][:, 0:W], conv_y[1][:, 0:W], ACT.Silu).then_inc(conv_gate, 1)
                    act.wait_ge(conv_step, BEGUN + f * 7 + (7 * n0 + 7))
                    act.activation(a_hi[:, dyn(f), 0:W], row(conv_y[0][:, 0:W]), ACT.Copy).then_inc(conv_hi, 1)
                units_of(ph, body)

            def retention(ph):
                q, l = sems["r"], ph["layer"]
                with act.Fori(0, 4) as j:
                    act.wait_ge(q["scored"], BEGUN + j * 8 + 32 * l)
                    act.activation(row(r_q[:]), proj1[:, bass.ds(j + 8, 1), :], ACT.Copy).then_inc(q["staged_act"], 1)
                    act.wait_ge(q["v_turned"], BEGUN + j + (4 * l + 1))
                    act.wait_ge(q["summed"], BEGUN + j * 8 + 32 * l)
                    act.activation(r_vs[:].rearrange("p t n -> p (t n)"), bank(0), ACT.Copy).then_inc(q["v_kept"], 1)
                    for hd in range(2):
                        act.wait_ge(q["mask_arg"], BEGUN + j * 4 + (16 * l + 2 * hd + 2))
                        act.activation(r_mask[hd][:], r_mask[hd][:], ACT.Exp).then_inc(q["bias"], 1)

            def diff(ph):
                q, l = sems["d"], ph["layer"]
                act.wait_ge(sems["r"]["summed"], BEGUN + 32 * (l + 1))
                with act.Fori(0, 4) as j:
                    act.wait_ge(q["scored"], BEGUN + j * 8 + 32 * l)
                    act.activation(row(d_q[:]), proj1[:, bass.ds(j, 1), :], ACT.Copy).then_inc(q["staged_act"], 1)
                    act.wait_ge(q["biased"], BEGUN + j * 8 + 32 * l)
                    act.activation(d_bias[:], d_dist[:], ACT.Copy, scale=dcol("slope", j)).then_inc(q["bias"], 1)
                    act.wait_ge(q["v_turned"], BEGUN + j + (4 * l + 1))
                    act.wait_ge(q["summed"], BEGUN + j + 4 * l)
                    act.activation(d_vs[:].rearrange("p t n -> p (t n)"), bank(0), ACT.Copy).then_inc(q["v_kept"], 1)

                    def exp(t):
                        act.wait_ge(q["negmax"], j * 8 + (32 * l + t + 1))
                        act.activation(d_s[t % 4][:], d_s[t % 4][:], ACT.Exp, bias=stats[:, 8 + t % 4:9 + t % 4],
                                       accum_out=stats[:, 12 + t % 4:13 + t % 4]).then_inc(q["exped"], 1)

                    def keep(b):
                        act.wait_ge(q["turned"], BEGUN + j * 4 + (16 * l + b + 1))
                        act.activation(d_aT[:, :, b * P:b * P + P], bank(b % 2).rearrange("p (t n) -> p t n", n=P),
                                       ACT.Copy).then_inc(q["kept"], 1)

                    for b in range(5):
                        if b < 4:
                            exp(2 * b)
                            exp(2 * b + 1)
                        if b >= 1:
                            keep(b - 1)

            def fin1(ph):
                l = ph["layer"]
                for n in range(8 + 1):
                    if n < 8:
                        tile = 8 + n if n < 4 else n - 4
                        if n == 0:
                            act.wait_ge(sems["r"]["evacuated"], BEGUN + 8 * (l + 1))
                            act.wait_ge(sems["d"]["evacuated"], BEGUN + 4 * (l + 1))
                        if n >= 2:
                            act.wait_ge(f_sum, 8 * l + n - 1)
                        act.activation(f_sq[n % 2][:], proj1[:, tile, :], ACT.Square).then_inc(f_sq_ready, 1)
                    if n >= 1:
                        act.wait_ge(f_sum, 8 * l + n)
                        if n >= 3:
                            act.wait_ge(f_y_ready, 12 * l + _f_y(n - 3))
                        act.activation(f_r[(n - 1) % 2][:], bank(4 + (n - 1) % 2), ACT.Sqrt,
                                       bias=eps1[:]).then_inc(f_std, 1)
                for n in range(8):
                    act.wait_ge(f_y_ready, 12 * l + _f_y(n))
                    act.activation(h_hi[:, n, 0:S], proj1[:, 8 + n if n < 4 else n - 4, :], ACT.Copy).then_inc(f_hi, 1)

            def na(ph):
                q = sems["n"]
                with act.Fori(0, 8) as j:
                    act.wait_ge(q["scored"], BEGUN + j * 12)
                    act.activation(n_q[:, 0:S].rearrange("p (b r c) -> p b r c", b=4, c=16),
                                   proj[:, bass.ds(j, 1), 0:S].rearrange("p a (r b c) -> p (a b) r c", b=4, c=16),
                                   ACT.Copy).then_inc(q["staged_act"], 1)
                    act.activation(row(n_q[:, S:T2]), proj[:, bass.ds(j, 1), S:T2], ACT.Copy
                                   ).then_inc(q["staged_act"], 1)
                    act.wait_ge(q["v_turned"], BEGUN + j + 1)
                    act.wait_ge(q["summed"], BEGUN + j * 12)
                    for b in range(3):
                        n = (P if b == 2 else S)
                        last = act.activation(n_vs[:].rearrange("p t n -> p (t n)")[:, b * S:b * S + n],
                                              bank(b, n), ACT.Copy)
                    last.then_inc(q["v_kept"], 1)

                    def exp(t):
                        w = S if t % 6 < 4 else C
                        act.wait_ge(q["negmax"], j * 12 + (t + 1))
                        act.activation(n_s[t % 3][:, 0:w], n_s[t % 3][:, 0:w], ACT.Exp,
                                       bias=stats[:, 3 + t % 3:4 + t % 3],
                                       accum_out=stats[:, 6 + t % 3:7 + t % 3]).then_inc(q["exped"], 1)

                    def keep(t):
                        w = S if t % 6 < 4 else C
                        act.wait_ge(q["turned"], BEGUN + j * 12 + (t + 1))
                        if t >= 2:
                            act.wait_ge(q["summed"], BEGUN + j * 12 + (t - 1))
                        act.activation(n_pT[t % 2][:, 0:w], bank(t % 2, w), ACT.Copy).then_inc(q["kept"], 1)

                    for t in range(13):
                        if t < 12:
                            exp(t)
                        if t >= 1:
                            keep(t - 1)

            def swa(ph):
                q = sems["s"]
                act.wait_ge(hn_out, ph["hn0"])
                for kv in range(2):
                    if kv:
                        act.wait_ge(q["scored"], BEGUN + 32)
                    act.activation(s_k[:, S:T2], proj[:, 8 + kv, S:T2], ACT.Copy).then_inc(q["staged_act"], 1)
                    act.wait_ge(q["v_turned"], BEGUN + kv + 1)
                    if kv:
                        act.wait_ge(q["summed"], BEGUN + 32)
                    act.activation(s_vs[:].rearrange("p t n -> p (t n)"), ps[:, 0:6 * P], ACT.Copy).then_inc(q["v_kept"], 1)
                    with act.Fori(0, 4) as g:
                        n = g * 8 + 32 * kv

                        def width(t):
                            return (5 if 0 < t % 4 < 3 else 4) * P

                        def exp(t):
                            act.wait_ge(q["negmax"], n + (t + 1))
                            act.activation(s_s[t % 3][:, 0:width(t) + 1], s_s[t % 3][:, 0:width(t) + 1], ACT.Exp,
                                           bias=stats[:, 3 + t % 3:4 + t % 3],
                                           accum_out=stats[:, 6 + t % 3:7 + t % 3]).then_inc(q["exped"], 1)

                        def keep(t):
                            act.wait_ge(q["turned"], BEGUN + n + (t + 1))
                            act.wait_ge(q["summed"], BEGUN + n + max(t - 1, 0))
                            act.activation(s_pT[t % 2][:, 0:width(t)], ps[:, 0:width(t)], ACT.Copy).then_inc(q["kept"], 1)

                        for t in range(9):
                            if t < 8:
                                exp(t)
                            if t >= 1:
                                keep(t - 1)

            def fin2(ph):
                s_done = sems["n"]["evacuated"] if ph["T"] == T2 else sems["s"]["evacuated"]
                act.wait_ge(s_done, BEGUN + (32 if ph["T"] == T2 else 16))
                for n in range(8):
                    act.activation(h_hi[:, n, 0:ph["T"]], proj[:, n, 0:ph["T"]], ACT.Copy).then_inc(f_hi, 1)

            for ph in phases:
                kind = ph["kind"]
                if kind == "norm":
                    norm(ph)
                elif kind == "normed":
                    head_norm(ph)
                elif kind == "proj":
                    take_out(ph)
                elif kind == "resid":
                    resid(ph)
                elif kind == "glu":
                    glu(ph)
                elif kind == "conv":
                    conv(ph)
                elif kind == "retention":
                    act.wait_ge(hn_out, ph["hn0"])
                    act.wait_ge(mm_done, ph["unit0"])
                    retention(ph)
                elif kind == "diff":
                    diff(ph)
                elif kind == "fin1":
                    fin1(ph)
                elif kind == "na":
                    act.wait_ge(hn_out, ph["hn0"])
                    act.wait_ge(mm_done, ph["unit0"])
                    na(ph)
                elif kind == "swa":
                    act.wait_ge(mm_done, ph["unit0"])
                    swa(ph)
                elif kind == "fin2":
                    fin2(ph)

        @block.vector
        def _(dve):
            def row(ap):
                return ap.rearrange("p (a n) -> p a n", a=1)

            begin(dve, ("biased", "evacuated", "mask_arg", "probs"), (conv_step, a_lo_ready))
            dve.memset(zero1[:], 0.0).then_inc(ready, 1)
            dve.memset(eps1[:], EPS).then_inc(ready, 1)
            dve.wait_ge(loaded, N_INPUTS)
            for l in range(DEPTH):
                for m in range(2):
                    n = 2 * l + m
                    if n:
                        dve.wait_ge(lam_step, n)
                    dve.tensor_tensor_reduce(lam_prod[:], lam_vec[:, 4 * l + 2 * m, :], lam_vec[:, 4 * l + 2 * m + 1, :],
                                             1.0, 0.0, ALU.mult, ALU.add, lam[:, n:n + 1]).then_inc(lam_step, 1)
            dve.wait_ge(lam_exp, 2)
            for l in range(DEPTH):
                init = 0.8 - 0.6 * float(np.exp(-0.3 * l))
                dve.scalar_tensor_tensor(out=lam[:, 8 + l:9 + l], in0=lam[:, 4 + 2 * l:5 + 2 * l], scalar=init,
                                         in1=lam[:, 5 + 2 * l:6 + 2 * l], op0=ALU.add, op1=ALU.subtract
                                         ).then_inc(lam_step, 1)
                dve.tensor_scalar(lam[:, 10 + l:11 + l], col("g_diff", l), 1.0 - init, None, ALU.mult
                                  ).then_inc(lam_step, 1)
                dve.tensor_scalar(col("g_dqk", 8 * l, 4), col("g_dqk", 8 * l, 4), HD ** -0.5, None, ALU.mult
                                  ).then_inc(lam_step, 1)
            dve.tensor_scalar(col("g_na", 0, 8), col("g_na", 0, 8), HD ** -0.5, None, ALU.mult).then_inc(lam_step, 1)
            dve.tensor_scalar(col("g_swa", 0, 8), col("g_swa", 0, 8), HD ** -0.5, None, ALU.mult).then_inc(lam_step, 1)
            dve.tensor_scalar(lgam[:], lgam[:], -1.0, None, ALU.mult).then_inc(lam_step, 1)
            dve.wait_ge(lam_step, 13)

            def modulation(i, u0):
                first = isinstance(i, int) and i == 0 and u0 == 0
                dve.wait_ge(silu_c_ready, 1)
                dve.wait_ge(mod_loaded, i * 16 + (8 * u0 + 16))
                if not first:
                    dve.wait_ge(mod_kept, i + u0 // 2)
                    dve.wait_ge(mod_step, i * 2 + u0)
                dve.tensor_tensor_reduce(mod_junk[:], mod_w[:], silu_c[:, 0, :], 1.0, 0.0, ALU.mult, ALU.add,
                                         mod_sum[:, 0:1]).then_inc(mod_step, 1)
                dve.wait_ge(mod_step, i * 2 + (u0 + 1))
                dve.tensor_tensor_reduce(mod_junk[:], mod_w[:], silu_c[:, 1, :], 1.0, 0.0, ALU.mult, ALU.add,
                                         mod_sum[:, 1:2]).then_inc(mod_step, 1)
                dve.wait_ge(mod_step, i * 2 + (u0 + 2))
                dve.tensor_copy(mod[:].rearrange("p l s k c -> p (l s k c)")[:, bass.ds(i * 2 + u0, 2)],
                                mod_sum[:]).then_inc(mod_kept, 1)

            def modulation_pairs(ph):
                if ph["unit0"] < MOD_UNITS:
                    with dve.Fori(0, ph["units"] // 2) as i:
                        modulation(i, ph["unit0"])

            def modulation_end():
                dve.wait_ge(mod_kept, DEPTH * 48)
                dve.tensor_tensor(mod[:].rearrange("p l s k c -> p (l s k c)"),
                                  mod[:].rearrange("p l s k c -> p (l s k c)"),
                                  col("b_mod", 0, DEPTH * 96), ALU.add).then_inc(mod_ready, 1)
                dve.wait_ge(mod_ready, 1)
                for l in range(DEPTH):
                    for w, name in enumerate(("g2_attn", "g2_ffn")):
                        dve.scalar_tensor_tensor(
                            out=gs[:, l, w].rearrange("p k c -> p (k c)"),
                            in0=mod[:, l, 1 + 3 * w].rearrange("p k c -> p (k c)"), scalar=1.0,
                            in1=col(name, 16 * l, 16), op0=ALU.add, op1=ALU.mult).then_inc(mod_ready, 1)
                dve.wait_ge(mod_ready, 5)

            def norm(ph):
                n0, T = ph["norm0"], ph["T"]
                dve.wait_ge(n_std, n0 + 1)
                dve.reciprocal(n_rstd[:, 0:T], n_rstd[:, 0:T]).then_inc(n_recip, 1)
                dve.wait_ge(n_recip, n0 + 1)
                w_i = 0 if ph["which"] == "attn" else 1
                parts = ph["part0"]
                for k in range(KT + 1):
                    if k < KT:
                        if k >= 2:
                            dve.wait_ge(n_lo, ph["part0"] + (k - 1) * len(segments(T)))
                        for to, _, w, c in segments(T):
                            gain = col("g_" + ph["which"], KT * ph["layer"] + k) if ph["block"] == 1 else \
                                gs[:, ph["layer"], w_i, k, c:c + 1]
                            last = dve.scalar_tensor_tensor(
                                out=n_xn[k % 2][:, to:to + w], in0=xT[:, k, to:to + w], scalar=gain,
                                in1=n_rstd[:, to:to + w], op0=ALU.mult, op1=ALU.mult)
                            last.then_inc(n_xn_ready, 1)
                    if k >= 1:
                        kk = k - 1
                        for to, _, w, c in segments(T):
                            shift = zero1[:] if ph["block"] == 1 else \
                                mod[:, ph["layer"], 3 * w_i, kk, c:c + 1]
                            parts += 1
                            dve.wait_ge(n_hi, parts)
                            dve.scalar_tensor_tensor(
                                out=h_lo[:, kk, to:to + w], in0=n_xn[kk % 2][:, to:to + w], scalar=shift,
                                in1=h_hi[:, kk, to:to + w].bitcast(F32), op0=ALU.add, op1=ALU.subtract
                            ).then_inc(n_lo, 1)

            def head_norm(ph):
                T, h0 = ph["T"], ph["hn0"]
                dst = proj1 if ph["weight"] == "w_in" else proj

                def tile(i, par):
                    return dst[:, bass.ds(i * 2 + (ph["tile0"] + par), 1), 0:T]

                def take(i, par):
                    dve.wait_ge(mm_done, i * 2 + (ph["unit0"] + par + 1))
                    dve.tensor_copy(tile(i, par), row(acc[par][:, 0:T])).then_inc(acc_free, 1)

                def scale(i, par):
                    dve.wait_ge(hn_std, i * 2 + (h0 + par + 1))
                    dve.reciprocal(hn_r[par][:, 0:T], hn_r[par][:, 0:T]).then_inc(hn_recip, 1)
                    dve.wait_ge(hn_recip, i * 2 + (h0 + par + 1))
                    dve.scalar_tensor_tensor(out=tile(i, par), in0=tile(i, par),
                                             scalar=dcol(ph["gains"][0], i * 2 + (ph["gains"][1] + par)),
                                             in1=row(hn_r[par][:, 0:T]), op0=ALU.mult, op1=ALU.mult
                                             ).then_inc(hn_out, 1)

                beside = ph["unit0"] < MOD_UNITS
                if beside:
                    modulation(0, ph["unit0"])
                take(0, 0)
                take(0, 1)
                scale(0, 0)
                if ph["units"] > 2:
                    with dve.Fori(1, ph["units"] // 2) as i:
                        if beside:
                            modulation(i, ph["unit0"])
                        take(i, 0)
                        scale(i - 1, 1)
                        take(i, 1)
                        scale(i, 0)
                scale(ph["units"] // 2 - 1, 1)

            def resid(ph):
                def body(i, first):
                    if ph["unit0"] < MOD_UNITS:
                        modulation(i, ph["unit0"])
                    for par in range(2):
                        dve.wait_ge(mm_done, i * 2 + (ph["unit0"] + par + 1))
                        for to, _, n, c in segments(ph["T"]):
                            x_ = xT[:, bass.ds(i * 2 + par, 1), to:to + n]
                            if ph["gate"] is None:
                                gate = 1.0
                            else:
                                l, part = ph["gate"]
                                gate = mod[:].rearrange("p l s k c -> p (l s k c)")[
                                    :, bass.ds(i * 4 + (2 * KT * (6 * l + part) + 2 * par + c), 1)]
                            last = dve.scalar_tensor_tensor(out=x_, in0=row(acc[par][:, to:to + n]), scalar=gate,
                                                            in1=x_, op0=ALU.mult, op1=ALU.add)
                        last.then_inc(acc_free, 1)
                pairs(dve, ph, body)

            def glu(ph):
                n0 = ph["glu0"]
                with dve.Fori(0, FH) as f:
                    modulation(f, ph["unit0"])
                    dve.wait_ge(glu_g_ready, f + (n0 + 1))
                    dve.wait_ge(mm_done, f * 2 + (ph["unit0"] + 2))
                    dve.wait_ge(a_lo_ready, BEGUN + f + n0)
                    dve.tensor_tensor(glu_a[:], acc[1][:, 0:S], glu_g[:], ALU.mult).then_inc(acc_free, 2)
                    dve.wait_ge(glu_hi, f + (n0 + 1))
                    dve.tensor_tensor(b_lo[:, bass.ds(f, 1), :], row(glu_a[:]),
                                      b_hi[:, bass.ds(f, 1), :].bitcast(F32), ALU.subtract).then_inc(a_lo_ready, 1)

            def conv(ph):
                n0, T, l = ph["conv0"], ph["T"], ph["layer"]
                W = ACTW if T == T2 else S
                for par in range(2):
                    for c in (0, 2 + S, 2 + ACTW):
                        dve.memset(u_pad[par][:, c:c + 2], 0.0).then_inc(conv_zero, 1)
                with dve.Fori(0, FH) as f:
                    m = 7 * n0

                    def tap(par, j):
                        return dcol("conv", f * 8 + (((l * FT + ph["half"] * FH) * 2 + par) * 4 + j))
                    for j in range(3):
                        for par in range(2):
                            y, u = conv_y[par][:, 0:W], u_pad[par][:, 1 + j:1 + j + W]
                            if j == 0:
                                dve.wait_ge(a_lo_ready, BEGUN + f + (ph["glu0"] + n0))
                                dve.wait_ge(acc_free, f * 2 + (ph["unit0"] + par + 1))
                                dve.wait_ge(conv_zero, 6 * (n0 // FH + 1))
                                dve.tensor_scalar(y, u, tap(par, 0), tap(par, 3), ALU.mult, ALU.add
                                                  ).then_inc(conv_step, 1)
                            else:
                                dve.wait_ge(conv_step, BEGUN + f * 7 + (m + 2 * j + par - 1))
                                dve.scalar_tensor_tensor(out=y, in0=u, scalar=tap(par, j), in1=y,
                                                         op0=ALU.mult, op1=ALU.add).then_inc(conv_step, 1)
                    dve.wait_ge(conv_gate, f + (n0 + 1))
                    dve.wait_ge(conv_step, BEGUN + f * 7 + (m + 6))
                    dve.tensor_tensor(conv_y[0][:, 0:W], conv_y[0][:, 0:W], conv_y[1][:, 0:W], ALU.mult
                                      ).then_inc(conv_step, 1)
                    dve.wait_ge(conv_hi, f + (n0 + 1))
                    dve.tensor_tensor(a_lo[:, bass.ds(f, 1), 0:W], row(conv_y[0][:, 0:W]),
                                      a_hi[:, bass.ds(f, 1), 0:W].bitcast(F32), ALU.subtract).then_inc(a_lo_ready, 1)

            def retention(ph):
                q, l = sems["r"], ph["layer"]
                dve.wait_ge(tab["retention"], 48 * (l + 1))
                with dve.Fori(0, 4) as j:
                    dve.wait_ge(q["scored"], BEGUN + j * 8 + 32 * l)
                    dve.wait_ge(q["v_turned"], BEGUN + j + 4 * l)
                    dve.tensor_scalar(row(r_k[:]), proj1[:, bass.ds(j + 12, 1), :], HD ** -0.5, None, ALU.mult
                                      ).then_inc(q["staged_dve"], 1)
                    dve.tensor_copy(row(r_v[:]), proj1[:, bass.ds(j + 16, 1), :]).then_inc(q["staged_dve"], 1)
                    for hd in range(2):
                        lg = [lgam[:, bass.ds(j * 2 + (16 * l + 8 * b + hd), 1)] for b in range(2)]
                        m = 16 * l + 2 * hd
                        dve.wait_ge(q["mask_arg"], BEGUN + j * 4 + m)
                        dve.tensor_scalar(r_tmp[:], r_dpos[:], lg[0], None, ALU.mult).then_inc(q["mask_arg"], 1)
                        dve.wait_ge(q["mask_arg"], BEGUN + j * 4 + (m + 1))
                        dve.wait_ge(q["biased"], BEGUN + j * 8 + 32 * l)
                        dve.scalar_tensor_tensor(out=r_mask[hd][:], in0=r_dneg[:], scalar=lg[1], in1=r_tmp[:],
                                                 op0=ALU.mult, op1=ALU.add).then_inc(q["mask_arg"], 1)
                    for t in range(8 + 1):
                        if t < 8:
                            hd, s = divmod(t, 4)
                            dve.wait_ge(q["bias"], j * 2 + (8 * l + hd + 1))
                            dve.wait_ge(q["scored"], BEGUN + j * 8 + (32 * l + t + 1))
                            if t >= 3:
                                dve.wait_ge(q["summed"], BEGUN + j * 8 + (32 * l + t - 2))
                            else:
                                dve.wait_ge(q["summed"], BEGUN + j * 8 + 32 * l)
                            dve.tensor_tensor(r_sc[t % 3][:], bank(4 + t % 2),
                                              r_mask[hd][:, (3 - s) * P:(3 - s) * P + S], ALU.mult
                                              ).then_inc(q["biased"], 1)
                        if t in (5, 8):
                            hd = 0 if t == 5 else 1
                            half = slice(HD * hd, HD * hd + HD)
                            dve.wait_ge(q["summed"], BEGUN + j * 8 + (32 * l + 4 * hd + 4))
                            dve.tensor_copy(proj1[half, bass.ds(j + 8, 1), :], row(bank(2 + hd)[half, :])
                                            ).then_inc(q["evacuated"], 1)

            def diff(ph):
                q, l = sems["d"], ph["layer"]
                dve.wait_ge(sems["r"]["evacuated"], BEGUN + 8 * (l + 1))
                with dve.Fori(0, 4) as j:
                    dve.wait_ge(q["turned"], BEGUN + j * 4 + 16 * l)
                    dve.wait_ge(q["scored"], BEGUN + j * 8 + 32 * l)
                    dve.tensor_copy(row(d_k[:]), proj1[:, bass.ds(j + 4, 1), :]).then_inc(q["staged_dve"], 1)
                    dve.wait_ge(q["v_turned"], BEGUN + j + 4 * l)
                    dve.tensor_copy(row(d_v[:]), proj1[:, bass.ds(j + 20, 1), :]).then_inc(q["staged_dve"], 1)
                    for b in range(5):
                        if b < 4:
                            for t in (2 * b, 2 * b + 1):
                                s = d_s[t % 4]
                                dve.wait_ge(q["bias"], j + (4 * l + 1))
                                dve.wait_ge(q["scored"], BEGUN + j * 8 + (32 * l + t + 1))
                                if b >= 2:
                                    dve.wait_ge(q["turned"], BEGUN + j * 4 + (16 * l + b - 1))
                                dve.memset(pace[:, 2:3], 0.0)
                                dve.tensor_tensor_reduce(s[:], bank(4 + t % 4), d_bias[:, (3 - b) * P:(3 - b) * P + S],
                                                         1.0, NEG, ALU.add, ALU.max,
                                                         stats[:, 4 + t % 4:5 + t % 4]).then_inc(q["biased"], 1)
                                dve.wait_ge(q["biased"], BEGUN + j * 8 + (32 * l + t + 1))
                                dve.tensor_scalar(stats[:, 8 + t % 4:9 + t % 4], stats[:, 4 + t % 4:5 + t % 4],
                                                  -1.0, None, ALU.mult).then_inc(q["negmax"], 1)
                        if b >= 1:
                            t0, t1 = 2 * b - 2, 2 * b - 1
                            n = 16 * 2 * l + 2 * (b - 1)
                            dve.wait_ge(q["exped"], j * 8 + (32 * l + t1 + 1))
                            sm = stats[:, 12 + t0 % 4:14 + t0 % 4]
                            dve.wait_ge(q["probs"], BEGUN + j * 8 + n)
                            dve.reciprocal(stats[:, 16:18], sm).then_inc(q["recip"], 1)
                            dve.wait_ge(q["recip"], j * 8 + (n + 1))
                            dve.tensor_scalar(stats[:, 18:19], stats[:, 17:18], lam[:, 8 + l:9 + l], None, ALU.mult
                                              ).then_inc(q["recip"], 1)
                            dve.wait_ge(q["recip"], j * 8 + (n + 2))
                            dve.tensor_scalar(d_s[t1 % 4][:], d_s[t1 % 4][:], stats[:, 18:19], None, ALU.mult
                                              ).then_inc(q["probs"], 1)
                            dve.wait_ge(q["probs"], BEGUN + j * 8 + (n + 1))
                            dve.scalar_tensor_tensor(out=d_s[t0 % 4][:], in0=d_s[t0 % 4][:], scalar=stats[:, 16:17],
                                                     in1=d_s[t1 % 4][:], op0=ALU.mult, op1=ALU.subtract
                                                     ).then_inc(q["probs"], 1)
                    dve.wait_ge(q["summed"], BEGUN + j + (4 * l + 1))
                    dve.tensor_copy(proj1[:, bass.ds(j, 1), :], row(bank(2))).then_inc(q["evacuated"], 1)

            def fin1(ph):
                l = ph["layer"]
                for n in range(8):
                    tile = proj1[:, 8 + n if n < 4 else n - 4, :]
                    gain = col("g_ret", l) if n < 4 else lam[:, 10 + l:11 + l]
                    dve.wait_ge(f_std, 8 * l + n + 1)
                    dve.reciprocal(f_r[n % 2][:], f_r[n % 2][:]).then_inc(f_recip, 1)
                    dve.wait_ge(f_recip, 8 * l + n + 1)
                    dve.scalar_tensor_tensor(out=tile, in0=tile, scalar=gain, in1=f_r[n % 2][:],
                                             op0=ALU.mult, op1=ALU.mult).then_inc(f_y_ready, 1)
                    if n < 4:
                        dve.wait_ge(f_y_ready, 12 * l + _f_y(n) - 1)
                        dve.tensor_tensor(tile, tile, proj1[:, 24 + n, :], ALU.mult).then_inc(f_y_ready, 1)
                for n in range(8):
                    dve.wait_ge(f_hi, 8 * l + n + 1)
                    dve.tensor_tensor(h_lo[:, n, 0:S], proj1[:, 8 + n if n < 4 else n - 4, :],
                                      h_hi[:, n, 0:S].bitcast(F32), ALU.subtract).then_inc(f_lo, 1)

            def fin2(ph):
                for n in range(8):
                    dve.wait_ge(f_hi, ph["fin0"] + n + 1)
                    dve.tensor_tensor(h_lo[:, n, 0:ph["T"]], proj[:, n, 0:ph["T"]],
                                      h_hi[:, n, 0:ph["T"]].bitcast(F32), ALU.subtract).then_inc(f_lo, 1)

            def na(ph):
                q = sems["n"]
                for hd in range(2):
                    for kind in range(3):
                        last = dve.memset(n_bias[:, hd, kind, 2 * P:4 * P], 0.0)
                        last.then_inc(q["mask_arg"], 1)
                dve.wait_ge(q["mask_arg"], BEGUN + 6)
                with dve.Fori(0, 8) as j:
                    dve.wait_ge(q["scored"], BEGUN + j * 12)
                    dve.wait_ge(q["v_turned"], BEGUN + j * 1)
                    for to, tile in ((n_v, 16), (n_k, 8)):
                        dve.tensor_copy(to[:, 0:S].rearrange("p (b r c) -> p b r c", b=8, c=8),
                                        proj[:, bass.ds(j + tile, 1), 0:S].rearrange(
                                            "p a (r b c) -> p (a b) r c", b=8, c=8)).then_inc(q["staged_dve"], 1)
                        dve.tensor_copy(row(to[:, S:T2]), proj[:, bass.ds(j + tile, 1), S:T2]
                                        ).then_inc(q["staged_dve"], 1)

                    def bias(t):
                        hd, b = divmod(t, 6)
                        w = S if b < 4 else C
                        table = n_bias[:, hd, MASK_KIND[b], :] if b < 4 else n_bias[:, 0, 0, 2 * P:4 * P]
                        dve.wait_ge(q["bias"], j * 6 + 6)
                        dve.wait_ge(q["scored"], BEGUN + j * 12 + (t + 1))
                        if t >= 3:
                            dve.wait_ge(q["turned"], BEGUN + j * 12 + (t - 2))
                        else:
                            dve.wait_ge(q["turned"], BEGUN + j * 12)
                        dve.memset(pace[:, 2:3], 0.0)
                        dve.tensor_tensor_reduce(n_s[t % 3][:, 0:w], bank(4 + t % 2, w), table, 1.0, NEG,
                                                 ALU.add, ALU.max, stats[:, t % 3:t % 3 + 1]).then_inc(q["biased"], 1)
                        dve.wait_ge(q["biased"], BEGUN + j * 12 + (t + 1))
                        dve.tensor_scalar(stats[:, 3 + t % 3:4 + t % 3], stats[:, t % 3:t % 3 + 1], -1.0, None,
                                          ALU.mult).then_inc(q["negmax"], 1)

                    def probs(t):
                        w = S if t % 6 < 4 else C
                        dve.wait_ge(q["exped"], j * 12 + (t + 1))
                        dve.reciprocal(stats[:, 9 + t % 3:10 + t % 3], stats[:, 6 + t % 3:7 + t % 3]
                                       ).then_inc(q["recip"], 1)
                        dve.wait_ge(q["recip"], j * 12 + (t + 1))
                        dve.tensor_scalar(n_s[t % 3][:, 0:w], n_s[t % 3][:, 0:w], stats[:, 9 + t % 3:10 + t % 3],
                                          None, ALU.mult).then_inc(q["probs"], 1)

                    def evacuate(hd):
                        half = slice(HD * hd, HD * hd + HD)
                        dve.wait_ge(q["summed"], BEGUN + j * 12 + (6 * hd + 6))
                        dve.tensor_copy(
                            proj[half, bass.ds(j, 1), 0:S].rearrange("p a (r b c) -> p (a b) r c", b=4, c=16),
                            bank(2)[half, :].rearrange("p (b r c) -> p b r c", b=4, c=16)).then_inc(q["evacuated"], 1)
                        dve.tensor_copy(proj[half, bass.ds(j, 1), S:T2], row(bank(3)[half, 0:C])
                                        ).then_inc(q["evacuated"], 1)

                    for t in range(13):
                        if t < 12:
                            bias(t)
                        if t >= 1:
                            probs(t - 1)
                        if t == 7:
                            evacuate(0)
                    evacuate(1)

            def swa(ph):
                q = sems["s"]
                dve.wait_ge(tab["swa"], 48)
                for kv in range(2):
                    dve.wait_ge(rope_mm, 5 * kv + 1)
                    if kv:
                        dve.wait_ge(rope_out, 5)
                    dve.tensor_tensor(s_t1[:], bank(6), s_sin[:], ALU.mult).then_inc(rope_a, 1)
                    if kv:
                        dve.wait_ge(q["v_turned"], BEGUN + 1)
                    dve.tensor_copy(s_v[:], proj[:, 10 + kv, :]).then_inc(q["staged_dve"], 1)
                    with dve.Fori(0, 4) as g:
                        n = g * 8 + 32 * kv
                        dve.wait_ge(rope_mm, g + (5 * kv + 2))
                        dve.wait_ge(rope_out, g + (5 * kv + 1))
                        dve.tensor_tensor(s_t1[:], bank(6), s_sin[:], ALU.mult).then_inc(rope_a, 1)

                        def width(t):
                            return (5 if 0 < t % 4 < 3 else 4) * P

                        def bias(t):
                            hd, b = divmod(t, 4)
                            w, s = width(t), s_s[t % 3]
                            frm = (P, 0, 0, 5 * P)[b]
                            sink = dcol("sink", g * 2 + (8 * kv + hd))
                            dve.wait_ge(q["scored"], BEGUN + n + (t + 1))
                            dve.wait_ge(q["turned"], BEGUN + n + max(t - 2, 0))
                            dve.memset(pace[:, 2:3], 0.0)
                            dve.tensor_tensor_reduce(s[:, 0:w], sums[t % 2][:, 0:w], s_band[:, frm:frm + w], 1.0, NEG,
                                                     ALU.add, ALU.max, stats[:, t % 3:t % 3 + 1]
                                                     ).then_inc(q["biased"], 1)
                            dve.tensor_copy(s[:, w:w + 1], sink).then_inc(q["mask_arg"], 1)
                            dve.wait_ge(q["biased"], BEGUN + n + (t + 1))
                            dve.wait_ge(q["mask_arg"], BEGUN + n + (t + 1))
                            dve.tensor_scalar(stats[:, 3 + t % 3:4 + t % 3], stats[:, t % 3:t % 3 + 1], sink, -1.0,
                                              ALU.max, ALU.mult).then_inc(q["negmax"], 1)

                        def probs(t):
                            w = width(t)
                            dve.wait_ge(q["exped"], n + (t + 1))
                            dve.reciprocal(stats[:, 9 + t % 3:10 + t % 3], stats[:, 6 + t % 3:7 + t % 3]
                                           ).then_inc(q["recip"], 1)
                            dve.wait_ge(q["recip"], n + (t + 1))
                            dve.tensor_scalar(s_s[t % 3][:, 0:w], s_s[t % 3][:, 0:w], stats[:, 9 + t % 3:10 + t % 3],
                                              None, ALU.mult).then_inc(q["probs"], 1)

                        def evacuate(hd):
                            half = slice(HD * hd, HD * hd + HD)
                            dve.wait_ge(q["summed"], BEGUN + n + (4 * hd + 4))
                            dve.tensor_copy(proj[half, bass.ds(g + 4 * kv, 1), 0:S], row(bank(2 + hd)[half, :])
                                            ).then_inc(q["evacuated"], 1)

                        for t in range(9):
                            if t < 8:
                                bias(t)
                            if t >= 1:
                                probs(t - 1)
                            if t == 6:
                                evacuate(0)
                        evacuate(1)

            for ph in phases:
                kind = ph["kind"]
                if kind == "norm":
                    if ph["unit0"] == MOD_UNITS:
                        modulation_end()
                    norm(ph)
                elif kind == "normed":
                    head_norm(ph)
                elif kind == "proj":
                    modulation_pairs(ph)
                elif kind == "resid":
                    resid(ph)
                elif kind == "glu":
                    glu(ph)
                elif kind == "conv":
                    conv(ph)
                elif kind == "retention":
                    dve.wait_ge(acc_free, ph["unit0"])
                    dve.wait_ge(mm_done, ph["unit0"])
                    retention(ph)
                elif kind == "diff":
                    diff(ph)
                elif kind == "fin1":
                    fin1(ph)
                elif kind == "na":
                    dve.wait_ge(acc_free, ph["unit0"])
                    dve.wait_ge(mm_done, ph["unit0"])
                    na(ph)
                elif kind == "swa":
                    dve.wait_ge(acc_free, ph["unit0"])
                    dve.wait_ge(mm_done, ph["unit0"])
                    swa(ph)
                elif kind == "fin2":
                    fin2(ph)


def constants():
    p = np.arange(P)[:, None]
    j = np.arange(STRIP)[None, :]
    dist = (j - (S - P) - p).astype(np.float32)
    strips = np.stack([np.maximum(dist, 0), np.maximum(-dist, 0), np.abs(dist)])
    mats = np.zeros((P, 5, P), np.float32)
    mats[:, IDENT] = np.eye(P)
    mats[:, MEAN64] = np.kron(np.eye(2), np.full((HD, HD), 1 / HD))
    mats[:, MEAN128] = 1 / P
    mats[:, MEAN1024] = 1 / D
    rot = np.zeros((P, P), np.float32)
    for h in range(2):
        for i in range(HD // 2):
            rot[h * HD + HD // 2 + i, h * HD + i] = -1.0
            rot[h * HD + i, h * HD + HD // 2 + i] = 1.0
    mats[:, ROT] = rot
    mask = np.zeros((P, 3, 4, ROWS, 8), np.float32)
    qc = np.arange(P) % 16
    for kind, b in enumerate((0, 1, 3)):
        c = 16 * b + qc
        first = np.clip(c - 8, 0, GRID - 16)
        key = KEY_COL[b] + np.arange(32).reshape(4, 8)
        ok = (key[None] >= first[:, None, None]) & (key[None] < first[:, None, None] + 16)
        mask[:, kind] = np.where(ok, 0.0, NEG)[:, :, None, :]
    k = np.arange(P)[None, :]
    before = np.where(k >= p, 0.0, NEG)
    after = np.where(k <= p, 0.0, NEG)
    zero = np.zeros((P, P))
    band = np.concatenate([before, zero, after, zero, zero, before, zero, zero, zero], 1)
    t = np.arange(S)
    inv = (10000.0 ** (-np.arange(HD // 4, dtype=np.float32) / (HD // 4))).astype(np.float32)
    ang = np.concatenate([(t // GRID).astype(np.float32)[:, None] * inv,
                          (t % GRID).astype(np.float32)[:, None] * inv], -1).astype(np.float32)
    rope = np.stack([np.tile(f(ang).T, (4, 1)) for f in (np.cos, np.sin)])
    f32 = lambda a: np.ascontiguousarray(a, dtype=np.float32)
    return dict(dist=f32(strips), mats=f32(mats), na_mask=f32(mask.reshape(P, 3, 2 * P)),
                band=f32(band), rope=f32(rope))


def lay_out(i):
    def units(w):
        L, K, N = w.shape
        return w.reshape(L, K // P, P, N // P, P).transpose(0, 3, 2, 1, 4).reshape(L * N // P, P, K)

    def cols(v):
        return v.reshape(-1, P).T

    def rep(v):
        return np.broadcast_to(v.reshape(1, -1), (P, v.size))

    def head(v):
        return np.concatenate([v, v])[:, None]

    x, ctx = i["x"][0], i["ctx_2"][0]
    o = {}
    o["x"] = x.T.reshape(KT, P, S).transpose(1, 0, 2)
    o["ctx"] = ctx.T.reshape(KT, P, C).transpose(1, 0, 2)
    w = i["w_in"].reshape(DEPTH, D, 7, 512)
    o["w_in"] = units(np.concatenate([w[:, :, n] for n in (4, 5, 0, 1, 2, 6, 3)], 2))
    o["w_out"] = units(i["w_out"])
    gu = np.stack([i["w_gate"].reshape(DEPTH, D, FT, P), i["w_up"].reshape(DEPTH, D, FT, P)], 3)
    o["w_gu"] = units(gu.reshape(DEPTH, D, 2 * D_FF))
    o["w_down"] = units(i["w_down"].reshape(DEPTH * 2, D_FF // 2, D))
    o["w_mod"] = i["w_mod_2"].transpose(0, 2, 1).reshape(-1, P, D)
    o["c"] = rep(np.stack([i["c_2"][0], i["c_ctx_2"]])).reshape(P, 2, D)
    o["na_qkv"] = units(i["na_w_qkv_2"])
    o["na_o"] = units(i["na_w_o_2"])
    def pair_heads(a, axis):
        shape = a.shape
        a = np.moveaxis(a, axis, 0).reshape(2, 2, 4, HD, -1).transpose(0, 2, 1, 3, 4)
        return np.moveaxis(a.reshape((D,) + tuple(np.delete(shape, axis))), 0, axis)
    sw = i["swa_w_qkv_2"]
    o["swa_qkv"] = units(np.concatenate([pair_heads(sw[:, :, :D], 2), sw[:, :, D:]], 2))
    o["swa_o"] = units(pair_heads(i["swa_w_o_2"], 1))
    up = i["ffn_w_up_2"].reshape(DEPTH, D, 2, FT, P).transpose(0, 1, 3, 2, 4)
    o["w_up2"] = units(up.reshape(DEPTH, D, 2 * D_FF))
    o["w_down2"] = units(i["ffn_w_down_2"].reshape(DEPTH * 2, D_FF // 2, D))
    o["lam"] = rep(np.stack([i[n] for n in ("lambda_q1", "lambda_k1", "lambda_q2", "lambda_k2")], 1)
                   ).reshape(P, DEPTH * 4, HD)
    pad = np.pad(i["na_rpb_2"][0], ((0, 0), (0, 0), (16, 16)))
    r, c, kr, u = np.ogrid[0:ROWS, 0:16, 0:ROWS, 0:48]
    e = pad[:, kr - r + ROWS - 1, u - c + 15]
    o["rpb"] = e.reshape(8, 2, P, ROWS * 48).transpose(0, 2, 1, 3)
    conv = np.concatenate([i["ffn_conv_w_2"], i["ffn_conv_b_2"][:, None]], 1)
    conv = conv.reshape(DEPTH, 4, 2, FT, P).transpose(4, 0, 3, 2, 1)
    two = lambda v: np.repeat(cols(v), 2, 1)
    heads = lambda v: v.reshape(2, 2, 4).transpose(0, 2, 1)
    s = {
        "g_attn": cols(i["attn_norm_g"]), "g_ffn": cols(i["ffn_norm_g"]),
        "g_ret": np.concatenate([head(v) for v in i["ret_norm_g"]], 1), "g_diff": i["diff_norm_g"].T,
        "g_dqk": np.concatenate([np.repeat(head(i[n][l]), 4, 1) for l in range(DEPTH)
                                 for n in ("dq_norm_g", "dk_norm_g")], 1),
        "g_na": np.concatenate([np.repeat(head(i[n][0]), 8, 1) for n in ("na_g_q_2", "na_g_k_2")], 1),
        "g_swa": np.concatenate([np.repeat(head(i["swa_g_q_2"][0]), 8, 1),
                                 np.repeat(head(i["swa_g_k_2"][0]), 2, 1)], 1),
        "decay": rep(np.stack([i["ret_decay_fwd"], i["ret_decay_bwd"]], 1)),
        "slope": rep(-(2.0 ** (-8.0 * np.arange(1, 5) / 4)).astype(np.float32)),
        "sink": rep(heads(i["swa_sink_2"][0])), "conv": conv.reshape(P, -1),
        "g2_attn": two(i["g_attn_2"]), "g2_ffn": two(i["g_ffn_2"]), "b_mod": two(i["b_mod_2"]),
    }
    for n, (_, width) in SMALL.items():
        assert s[n].shape == (P, width), (n, s[n].shape, width)
    o["small"] = np.concatenate([s[n] for n in SMALL], 1)
    return o


def kernel(**inputs):
    import concourse.bacc as bacc
    from concourse.bass_utils import run_bass_kernel_spmd

    arrays = lay_out({n: np.asarray(a) for n, a in inputs.items()})
    arrays.update(constants())
    arrays = {n + "_dram": np.ascontiguousarray(a) for n, a in arrays.items()}
    nc = bacc.Bacc("TRN2", target_bir_lowering=False, num_devices=1)
    d = {n[:-5]: nc.dram_tensor(n, a.shape, mybir.dt.from_np(a.dtype), kind="ExternalInput").ap()
         for n, a in arrays.items()}
    out = nc.dram_tensor("out_dram", (P, KT, S), F32, kind="ExternalOutput").ap()
    build(nc, d, out)
    r = run_bass_kernel_spmd(nc, [arrays], core_ids=[0])
    got = r.results[0]["out_dram"]
    return np.ascontiguousarray(got.transpose(2, 1, 0)).reshape(1, S, D)
```

```python
from contextlib import ExitStack

import concourse.bass as bass
from concourse import mybir
import numpy as np

P = 128
D = 1024
KT = D // P
S = 512
C = 256
T2 = S + C
DEPTH = 2
HD = 64
D_FF = 2816
FT = D_FF // P
FH = FT // 2
GRID = 64
ROWS = S // GRID
EPS = 1e-6
NEG = -1e30
UNIT = FH * P
STRIP = S + S - P
CTX_AT = S + 2
ACTW = CTX_AT + C

ALU = mybir.AluOpType
ACT = mybir.ActivationFunctionType
F32 = mybir.dt.float32
F32R = mybir.dt.float32r
AX_X = mybir.AxisListType.X

SMALL = {}


def _small(name, width):
    SMALL[name] = (sum(w for _, w in SMALL.values()), width)


for _name, _width in (
    ("g_attn", DEPTH * KT), ("g_ffn", DEPTH * KT), ("g_ret", DEPTH), ("g_diff", DEPTH),
    ("g_dqk", DEPTH * 8), ("g_na", 16), ("g_swa", 10), ("decay", DEPTH * 16), ("slope", 4),
    ("sink", 16), ("conv", DEPTH * 2 * FT * 4), ("g2_attn", DEPTH * KT * 2), ("g2_ffn", DEPTH * KT * 2),
    ("b_mod", DEPTH * 48 * 2),
):
    _small(_name, _width)
NSMALL = sum(w for _, w in SMALL.values())

IDENT, MEAN64, MEAN128, MEAN1024, ROT = range(5)

MOD_UNITS = 2 * DEPTH * 48

BEGUN = 1

ROPE_TILES = [8, 9] + list(range(8))

KEY_COL = [0, 8, 24, 32]
MASK_KIND = [0, 1, 1, 2]


def schedule():
    phases, count = [], {"unit": 0, "norm": 0, "hn": 0, "glu": 0, "conv": 0, "h": 0}

    def add(kind, **kw):
        kw.update(kind=kind, **{k + "0": v for k, v in count.items()})
        phases.append(kw)

    def norm(block, layer, which, T):
        add("norm", block=block, layer=layer, which=which, T=T)
        count["norm"] += 1
        count["h"] += 1

    def proj(weight, first, units, T, tile0, func="copy"):
        add("proj", weight=weight, first=first, units=units, T=T, tile0=tile0, func=func, K=KT)
        count["unit"] += units

    def normed(weight, first, units, T, tile0, gains):
        add("normed", weight=weight, first=first, units=units, T=T, tile0=tile0, gains=gains, K=KT)
        count["unit"] += units
        count["hn"] += units

    def resid(weight, first, T, gate, K):
        add("resid", weight=weight, first=first, units=KT, T=T, gate=gate, K=K)
        count["unit"] += KT

    def hidden(kind, weight, first, T, layer, half):
        add(kind, weight=weight, first=first, units=2 * FH, T=T, layer=layer, half=half, K=KT)
        count["unit"] += 2 * FH
        count[kind] += FH

    for l in range(DEPTH):
        norm(1, l, "attn", S)
        normed("w_in", 28 * l, 8, S, 0, ("g_dqk", 8 * l))
        proj("w_in", 28 * l + 8, 16, S, 8)
        proj("w_in", 28 * l + 24, 4, S, 24, "silu")
        add("retention", layer=l)
        add("diff", layer=l)
        add("fin1", layer=l)
        count["h"] += 1
        resid("w_out", 8 * l, S, None, KT)
        norm(1, l, "ffn", S)
        for half in range(2):
            hidden("glu", "w_gu", 44 * l + 22 * half, S, l, half)
            resid("w_down", 16 * l + 8 * half, S, None, FH)
    norm(2, 0, "attn", T2)
    normed("na_qkv", 0, 16, T2, 0, ("g_na", 0))
    proj("na_qkv", 16, 8, T2, 16)
    add("na")
    add("fin2", T=T2)
    count["h"] += 1
    resid("na_o", 0, T2, (0, 2), KT)
    norm(2, 0, "ffn", T2)
    for half in range(2):
        hidden("conv", "w_up2", 22 * half, T2, 0, half)
        resid("w_down2", 8 * half, T2, (0, 5), FH)
    norm(2, 1, "attn", T2)
    normed("swa_qkv", 0, 8, S, 0, ("g_swa", 0))
    normed("swa_qkv", 8, 2, T2, 8, ("g_swa", 8))
    proj("swa_qkv", 10, 2, T2, 10)
    add("swa")
    add("fin2", T=S)
    count["h"] += 1
    resid("swa_o", 0, S, (1, 2), KT)
    norm(2, 1, "ffn", S)
    for half in range(2):
        hidden("conv", "w_up2", 44 + 22 * half, S, 1, half)
        resid("w_down2", 16 + 8 * half, S, (1, 5), FH)
    add("end")
    for ph, after in zip(phases, phases[1:]):
        after["fresh"] = "weight" in after and ph["kind"] in ("norm", "fin1", "fin2")
        ph["norm_T"] = after["T"] if after["kind"] == "norm" else None
    return phases


def ahead(phases):
    out, moved = [], None
    for n, ph in enumerate(phases):
        if "weight" in ph:
            out.append(dict(ph, pairs=(1, ph["units"] // 2)) if ph is moved else ph)
            moved = None
        else:
            if moved is None and ph["kind"] != "end":
                moved = next(p for p in phases[n:] if "weight" in p)
                out.append(dict(moved, pairs=(0, 1)))
            out.append(ph)
    return out


def segments(T, at=S):
    segs = [(0, 0, S, 0)]
    if T == T2:
        segs.append((S, at, C, 1))
    return segs


def _f_y(n):
    return 2 * (n + 1) if n < 4 else 8 + (n - 3)


def build(nc, d, out):
    phases = schedule()
    total_units = phases[-1]["unit0"]

    with ExitStack() as stack:
        def sem(name):
            return stack.enter_context(nc.semaphore(name))

        top = [nc.sbuf_base]
        names = [0]

        def at(offset, shape, dt=F32, name="t"):
            names[0] += 1
            return nc.alloc_sbuf_tensor_at(f"{name}{names[0]}", shape, dt, offset=offset)

        def nbytes(shape):
            n = 4
            for s in shape[1:]:
                n *= s
            return (n + 31) // 32 * 32

        def sb(name, shape, dt=F32):
            t = at(top[0], shape, dt, name)
            top[0] += nbytes(shape)
            return t

        class Area:

            def __init__(self, offset, size):
                self.offset, self.end = offset, offset + size

            def __call__(self, name, shape, dt=F32):
                t = at(self.offset, shape, dt, name)
                self.offset += nbytes(shape)
                assert self.offset <= self.end, (name, self.offset - self.end)
                return t

        top[0] = (top[0] + 31) // 32 * 32
        base = top[0]
        xT = sb("xT", [P, KT, T2])
        h_at = top[0]
        h_hi = sb("h_hi", [P, KT, T2], F32R)
        h_lo = sb("h_lo", [P, KT, T2], F32R)
        h_size = top[0] - h_at
        w_raw = [sb(f"w_raw{i}", [P, UNIT]) for i in range(2)]
        w_hi = [sb(f"w_hi{i}", [P, UNIT], F32R) for i in range(2)]
        w_lo = [sb(f"w_lo{i}", [P, UNIT], F32R) for i in range(2)]
        small = sb("small", [P, NSMALL])
        mats = sb("mats", [P, 5, P])
        mod = sb("mod", [P, DEPTH, 6, KT, 2])
        gs = sb("gs", [P, DEPTH, 2, KT, 2])
        mod_sum = sb("mod_sum", [P, 2])
        zero1 = sb("zero1", [P, 1])
        eps1 = sb("eps1", [P, 1])
        lgam = sb("lgam", [P, DEPTH * 16])
        lam = sb("lam", [P, 16])
        stats = sb("stats", [P, 24])
        pace = sb("pace", [P, 4])
        wide_at = top[0]
        wide_size = nbytes([P, 24, T2])
        top[0] += wide_size
        temp_at = top[0]
        temp_size = 4 * nbytes([P, 4 + ACTW])
        top[0] += temp_size
        assert top[0] <= nc.sbuf_usable_end, (top[0], nc.sbuf_usable_end)

        wide = Area(wide_at, wide_size)
        proj = wide("proj", [P, 24, T2])
        proj1 = at(wide_at, [P, 28, S], F32, "proj1")
        wide = Area(wide_at, wide_size)
        a_hi = wide("a_hi", [P, FH, ACTW], F32R)
        a_lo = wide("a_lo", [P, FH, ACTW], F32R)
        wide = Area(wide_at, wide_size)
        b_hi = wide("b_hi", [P, FH, S], F32R)
        b_lo = wide("b_lo", [P, FH, S], F32R)
        wide = Area(wide_at, wide_size)
        n_rstd = wide("n_rstd", [P, T2])
        n_xn = [wide(f"n_xn{i}", [P, T2]) for i in range(4)]
        lam_vec = wide("lam_vec", [P, DEPTH * 4, HD])
        lam_prod = wide("lam_prod", [P, HD])

        wide = Area(wide_at + nbytes([P, 28, S]), wide_size - nbytes([P, 28, S]))
        mod_w = wide("mod_w", [P, D])
        mod_junk = wide("mod_junk", [P, D])
        silu_c = wide("silu_c", [P, 2, D])

        temp = Area(temp_at, temp_size)
        u_pad = [temp(f"u_pad{i}", [P, 4 + ACTW]) for i in range(2)]
        conv_y = [temp(f"conv_y{i}", [P, ACTW]) for i in range(2)]
        temp = Area(temp_at, temp_size)
        n_sq = [temp(f"n_sq{i}", [P, T2]) for i in range(2)]
        n_sum_sq = temp("n_sum_sq", [P, T2])
        temp = Area(temp_at, temp_size)
        hn_sq = [temp(f"hn_sq{i}", [P, T2]) for i in range(2)]
        hn_r = [temp(f"hn_r{i}", [P, T2]) for i in range(2)]
        temp = Area(temp_at, temp_size)
        f_sq = [temp(f"f_sq{i}", [P, S]) for i in range(2)]
        f_r = [temp(f"f_r{i}", [P, S]) for i in range(2)]
        temp = Area(temp_at, temp_size)
        d_s_more = [temp(f"d_s{i}", [P, S]) for i in (6, 7)]
        temp = Area(temp_at, temp_size)
        glu_g = temp("glu_g", [P, S])
        glu_a = temp("glu_a", [P, S])

        area = Area(h_at, h_size)
        r_q, r_k, r_v = (area(f"r_{n}", [P, S]) for n in "qkv")
        r_vs = area("r_vs", [P, 4, P])
        r_dpos, r_dneg, r_tmp = (area(f"r_d{n}", [P, STRIP]) for n in "pnt")
        r_mask = [area(f"r_mask{i}", [P, STRIP]) for i in range(2)]
        r_sc = [area(f"r_sc{i}", [P, S]) for i in range(3)]
        d_dist = area("d_dist", [P, STRIP])
        d_dist_at = area.offset - nbytes([P, STRIP])
        area = Area(h_at, d_dist_at - h_at)
        d_q, d_k, d_v = (area(f"d_{n}", [P, S]) for n in "qkv")
        d_vs = area("d_vs", [P, 4, P])
        d_bias = area("d_bias", [P, STRIP])
        d_s = [area(f"d_s{i}", [P, S]) for i in range(6)] + d_s_more
        d_aT = area("d_aT", [P, 4, S])
        area = Area(h_at, h_size)
        n_q, n_k, n_v = (area(f"n_{n}", [P, T2]) for n in "qkv")
        n_vs = area("n_vs", [P, 9, P])
        n_s = [area(f"n_s{i}", [P, S]) for i in range(3)]
        n_pT = [area(f"n_pT{i}", [P, S]) for i in range(2)]
        n_bias = area("n_bias", [P, 2, 3, S])
        n_rpb = area("n_rpb", [P, 2, ROWS * 48])
        n_mask = area("n_mask", [P, 3, 2 * P])
        area = Area(h_at, h_size)
        s_q = area("s_q", [P, S])
        s_vs = area("s_vs", [P, 6, P])
        s_s = [area(f"s_s{i}", [P, 5 * P + 8]) for i in range(3)]
        s_pT = [area(f"s_pT{i}", [P, 5 * P]) for i in range(2)]
        s_band = area("s_band", [P, 9 * P])
        s_cos, s_sin = area("s_cos", [P, S]), area("s_sin", [P, S])
        s_t1, s_t2 = ([area(f"s_t{n}{i}", [P, S]) for i in range(2)] for n in (1, 2))

        ps = stack.enter_context(nc.psum_tensor("ps", [P, 8 * 512], F32))
        acc = [ps[:, 1024 * i:1024 * i + 1024] for i in range(2)]
        sums = [ps[:, 2048 + 1024 * i:3072 + 1024 * i] for i in range(2)]

        def bank(i, n=512):
            return ps[:, 512 * i:512 * i + n]

        loaded = sem("loaded")
        ready = sem("ready")
        w_loaded = [sem(f"w_loaded{i}") for i in range(2)]
        w_hi_ready = sem("w_hi_ready")
        w_lo_ready = sem("w_lo_ready")
        mm_done = sem("mm_done")
        acc_free = sem("acc_free")
        mod_loaded, mod_step, mod_kept = sem("mod_loaded"), sem("mod_step"), sem("mod_kept")
        silu_c_ready, mod_ready = sem("silu_c_ready"), sem("mod_ready")
        lam_step, lam_exp = sem("lam_step"), sem("lam_exp")
        n_sq_ready, n_sum, n_std = sem("n_sq_ready"), sem("n_sum"), sem("n_std")
        n_recip, n_xn_ready, n_scaled, n_added = sem("n_recip"), sem("n_xn_ready"), sem("n_scaled"), sem("n_added")
        h_hi_ready = sem("h_hi_ready")
        h_even, h_odd = sem("h_even"), sem("h_odd")
        x_in = [sem(f"x_in{i}") for i in range(4)]
        constants_in = sem("constants_in")
        hn_sq_ready, hn_sum, hn_std = sem("hn_sq_ready"), sem("hn_sum"), sem("hn_std")
        hn_recip, hn_out = sem("hn_recip"), sem("hn_out")
        a_lo_ready = sem("a_lo_ready")
        conv_step, conv_gate, conv_hi = sem("conv_step"), sem("conv_gate"), sem("conv_hi")
        conv_zero, glu_hi = sem("conv_zero"), sem("glu_hi")
        f_sq_ready, f_sum, f_std, f_recip = sem("f_sq_ready"), sem("f_sum"), sem("f_std"), sem("f_recip")
        f_y_ready = sem("f_y_ready")
        tab = {k: sem("tab_" + k) for k in ("retention", "na", "swa")}
        sems = {}
        for k, stage in (("r", "retention"), ("d", "diff"), ("n", "neighbour"), ("s", "sliding")):
            sems[k] = {n: sem(f"{stage}_{n}") for n in (
                "staged_act", "staged_dve", "v_turned", "v_kept", "scored", "biased", "negmax",
                "exped", "recip", "probs", "turned", "kept", "summed", "evacuated", "bias", "mask_arg")}
        rope_mm, rope_a, rope_b, rope_out = sem("rope_mm"), sem("rope_a"), sem("rope_b"), sem("rope_out")
        rpb_loaded = sem("rpb_loaded")
        stored = sem("stored")

        block = stack.enter_context(nc.Block())

        def begin(eng, names, others=()):
            for k in sems:
                for n in names:
                    eng.sem_inc(sems[k][n], BEGUN)
            for s_ in others:
                eng.sem_inc(s_, BEGUN)

        def col(name, i=0, n=1):
            return small[:, SMALL[name][0] + i:SMALL[name][0] + i + n]

        def dcol(name, i):
            return small[:, bass.ds(SMALL[name][0] + i, 1)]

        def pairs(eng, ph, body, peel=False):
            begin_, end = ph.get("pairs", (0, ph["units"] // 2))
            if begin_ == 0 and (ph["unit0"] == 0 or peel):
                body(0, ph["unit0"] == 0)
                begin_ = 1
            if end - begin_ == 1:
                body(begin_, False)
            elif end > begin_:
                with eng.Fori(begin_, end) as i:
                    body(i, False)

        def dyn(i):
            return bass.ds(i, 1)

        def by_columns(ap):
            return ap.rearrange("p a (b r c) -> p (a b) r c", b=8, c=8)

        def from_rows(ap):
            return ap.rearrange("p (r b c) -> p b r c", b=8, c=8)

        def mat(i):
            return mats[:, i, :]

        N_INPUTS = 16 * 3

        @block.sync
        def _(sp):
            def weights(ph):
                u0 = ph["unit0"]

                def body(i, first):
                    for par in range(2):
                        if not first:
                            sp.wait_ge(w_lo_ready, i * 2 + (u0 + par - 1))
                        sp.dma_start(w_raw[par][:, 0:ph["K"] * P].rearrange("p (a n) -> p a n", a=1),
                                     d[ph["weight"]][bass.ds(i * 2 + (ph["first"] + par), 1)].rearrange(
                                         "a p n -> p a n")).then_inc(w_loaded[par], 16)
                    if u0 < MOD_UNITS:
                        if not first:
                            sp.wait_ge(mod_step, i * 2 + u0)
                        sp.dma_start(mod_w[:].rearrange("p (a n) -> p a n", a=1),
                                     d["w_mod"][bass.ds(i + u0 // 2, 1)].rearrange("a p n -> p a n")
                                     ).then_inc(mod_loaded, 16)
                pairs(sp, ph, body)

            for ph in ahead(phases):
                if "weight" in ph:
                    weights(ph)
                elif ph["kind"] == "retention":
                    sp.wait_ge(mm_done, ph["unit0"])
                    sp.dma_start(r_dpos[:], d["dist"][0]).then_inc(tab["retention"], 16)
                    sp.dma_start(r_dneg[:], d["dist"][1]).then_inc(tab["retention"], 16)
                    sp.dma_start(d_dist[:], d["dist"][2]).then_inc(tab["retention"], 16)
                elif ph["kind"] == "na":
                    sp.wait_ge(mm_done, ph["unit0"])
                    sp.dma_start(n_mask[:], d["na_mask"]).then_inc(tab["na"], 16)
                    sp.dma_start(n_rpb[:], d["rpb"][0]).then_inc(rpb_loaded, 16)
                    with sp.Fori(1, 8) as j:
                        sp.wait_ge(sems["n"]["bias"], j * 6)
                        sp.dma_start(n_rpb[:].rearrange("p (a h) n -> p a h n", a=1),
                                     d["rpb"][bass.ds(j, 1)].rearrange("a p h n -> p a h n")
                                     ).then_inc(rpb_loaded, 16)
                elif ph["kind"] == "swa":
                    sp.wait_ge(mm_done, ph["unit0"])
                    sp.dma_start(s_band[:], d["band"]).then_inc(tab["swa"], 16)
                    sp.dma_start(s_cos[:], d["rope"][0]).then_inc(tab["swa"], 16)
                    sp.dma_start(s_sin[:], d["rope"][1]).then_inc(tab["swa"], 16)
            sp.wait_ge(acc_free, total_units)
            sp.dma_start(out, xT[:, :, 0:S]).then_inc(stored, 16)
            sp.wait_ge(stored, 16)

        @block.gpsimd
        def _(pool):
            def split(ph):
                u0, cols = ph["unit0"], ph["K"] * P

                def body(i, first):
                    for par in range(2):
                        pool.wait_ge(w_hi_ready, i * 2 + (u0 + par + 1))
                        pool.tensor_tensor(w_lo[par][:, 0:cols], w_raw[par][:, 0:cols],
                                           w_hi[par][:, 0:cols].bitcast(F32), ALU.subtract).then_inc(w_lo_ready, 1)
                pairs(pool, ph, body)

            def na_bias(ph):
                q = sems["n"]
                pool.wait_ge(tab["na"], 16)

                def tables(j, first):
                    pool.wait_ge(rpb_loaded, j * 16 + 16)
                    for hd in range(2):
                        if not first:
                            pool.wait_ge(q["biased"], BEGUN + j * 12 + (6 * hd + 4 - 12))
                        for kind, off in enumerate((16, 8, 0)):
                            strip = n_rpb[:, hd, :].rearrange("p (r u) -> p r u", u=48)
                            pool.tensor_tensor(
                                n_bias[:, hd, kind, 0:2 * P].rearrange("p (i r c) -> p i r c", i=4, c=8),
                                strip[:, :, off:off + 32].rearrange("p r (i c) -> p i r c", c=8),
                                n_mask[:, kind, :].rearrange("p (i r c) -> p i r c", i=4, c=8),
                                ALU.add).then_inc(q["bias"], 1)

                tables(0, True)
                with pool.Fori(1, 8) as j:
                    tables(j, False)

            def rope(ph):
                pool.wait_ge(tab["swa"], 48)
                pool.wait_ge(hn_out, ph["hn0"])
                pool.wait_ge(mm_done, ph["unit0"])
                for n, tile in enumerate(ROPE_TILES):
                    if n >= 2:
                        pool.wait_ge(rope_out, n - 1)
                    pool.tensor_tensor(s_t2[n % 2][:], proj[:, tile, 0:S], s_cos[:], ALU.mult).then_inc(rope_b, 1)

            def even_tiles(ph, source, T):
                for k in range(0, KT, 2):
                    pool.wait_ge(h_hi_ready, 8 * ph["h0"] + k + 1)
                    pool.tensor_tensor(h_lo[:, k, 0:T], source(k), h_hi[:, k, 0:T].bitcast(F32), ALU.subtract
                                       ).then_inc(h_even, 1)

            for ph in ahead(phases):
                if "weight" in ph:
                    split(ph)
                elif ph["kind"] == "norm":
                    even_tiles(ph, lambda k: n_xn[k % 4][:, 0:ph["T"]], ph["T"])
                elif ph["kind"] == "fin1":
                    even_tiles(ph, lambda k: proj1[:, 8 + k if k < 4 else k - 4, :], S)
                elif ph["kind"] == "fin2":
                    even_tiles(ph, lambda k: proj[:, k, 0:ph["T"]], ph["T"])
                elif ph["kind"] == "na":
                    na_bias(ph)
                elif ph["kind"] == "swa":
                    rope(ph)

        @block.tensor
        def _(pe):
            def tile_ready(ph, k):
                if ph["K"] == FH:
                    pe.wait_ge(a_lo_ready, BEGUN + ph["glu0"] + ph["conv0"] - FH + k + 1)
                elif ph["fresh"]:
                    pe.wait_ge((h_even, h_odd)[k % 2], 4 * (ph["h0"] - 1) + k // 2 + 1)

            def unit(ph, i, par, first):
                u0, K = ph["unit0"], ph["K"]
                hidden = ph["K"] == FH
                hi, lo = (h_hi, h_lo) if not hidden else (b_hi, b_lo) if u0 < MOD_UNITS else (a_hi, a_lo)
                segs = segments(ph["T"], CTX_AT if hidden else S)
                pe.wait_ge(w_lo_ready, i * 2 + (u0 + par + 1))
                if not first:
                    pe.wait_ge(acc_free, i * 2 + (u0 + par - 1))
                for k in range(K):
                    if isinstance(i, int) and i + par == 0:
                        tile_ready(ph, k)
                    for w, r, begin, end in ((w_hi, hi, k == 0, False), (w_hi, lo, False, False),
                                             (w_lo, hi, False, k == K - 1)):
                        for to, frm, n, _ in segs:
                            last = pe.matmul(acc[par][:, to:to + n], w[par][:, k * P:k * P + P],
                                             r[:, k, frm:frm + n], start=begin, stop=end)
                last.then_inc(mm_done, 1)

            def plain_units(ph):
                def body(i, first):
                    for par in range(2):
                        unit(ph, i, par, first)
                pairs(pe, ph, body, ph["fresh"] or ph["K"] == FH)

            def head_sum(ph, n, par):
                pe.wait_ge(hn_sq_ready, n + (ph["hn0"] + 1))
                for to, _, w, _ in segments(ph["T"]):
                    last = pe.matmul(sums[par][:, to:to + w], mat(MEAN64), hn_sq[par][:, to:to + w],
                                     start=True, stop=True)
                last.then_inc(hn_sum, 1)

            def normed_units(ph):
                first = ph["unit0"] == 0
                unit(ph, 0, 0, first)
                unit(ph, 0, 1, first)
                head_sum(ph, 0, 0)
                if ph["units"] > 2:
                    with pe.Fori(1, ph["units"] // 2) as i:
                        unit(ph, i, 0, False)
                        head_sum(ph, i * 2 - 1, 1)
                        unit(ph, i, 1, False)
                        head_sum(ph, i * 2, 0)
                head_sum(ph, ph["units"] - 1, 1)

            def norm(ph):
                n0, segs = ph["norm0"], segments(ph["T"])

                def add_up(square, begin, end):
                    for to, _, w, _ in segs:
                        last = pe.matmul(sums[0][:, to:to + w], mat(MEAN1024), square[:, to:to + w],
                                         start=begin, stop=end)
                    return last

                if n0 == 0:
                    for k in range(KT):
                        pe.wait_ge(n_sq_ready, k + 1)
                        add_up(n_sq[k % 2], k == 0, k == KT - 1).then_inc(n_sum, 1)
                else:
                    pe.wait_ge(n_added, KT * n0)
                    add_up(n_sum_sq, True, False)
                    pe.wait_ge(n_sq_ready, KT * n0 + KT)
                    add_up(n_sq[1], False, True).then_inc(n_sum, 1)

            def retention(ph):
                q = sems["r"]
                l = ph["layer"]
                with pe.Fori(0, 4) as j:
                    pe.wait_ge(q["staged_act"], j * 1 + (4 * l + 1))
                    pe.wait_ge(q["staged_dve"], j * 2 + (8 * l + 2))
                    pe.wait_ge(q["evacuated"], BEGUN + j * 2 + 8 * l)
                    pe.wait_ge(acc_free, ph["unit0"])
                    for t in range(4):
                        last = pe.transpose(bank(0)[:, t * P:t * P + P], r_v[:, t * P:t * P + P], mat(IDENT))
                    last.then_inc(q["v_turned"], 1)

                    def score(t):
                        hd, s = divmod(t, 4)
                        half = slice(HD * hd, HD * hd + HD)
                        if t >= 2:
                            pe.wait_ge(q["biased"], BEGUN + j * 8 + (32 * l + t - 1))
                        pe.matmul(bank(4 + t % 2), r_k[half, s * P:s * P + P], r_q[half, :],
                                  start=True, stop=True).then_inc(q["scored"], 1)

                    def values(t):
                        hd, s = divmod(t, 4)
                        pe.wait_ge(q["v_kept"], j * 1 + (4 * l + 1))
                        pe.wait_ge(q["biased"], BEGUN + j * 8 + (32 * l + t + 1))
                        pe.matmul(bank(2 + hd), r_vs[:, s, :], r_sc[t % 3][:],
                                  start=(s == 0), stop=(s == 3)).then_inc(q["summed"], 1)

                    for t in range(8 + 1):
                        if t < 8:
                            score(t)
                        if t >= 1:
                            values(t - 1)

            def diff(ph):
                q = sems["d"]
                l = ph["layer"]
                pe.wait_ge(sems["r"]["evacuated"], BEGUN + 8 * (l + 1))

                def score(j, b):
                    for m in range(2):
                        half = slice(HD * m, HD * m + HD)
                        t = 2 * b + m
                        if b >= 2:
                            pe.wait_ge(q["biased"], BEGUN + j * 8 + (32 * l + t - 3))
                        elif m == 0:
                            pe.wait_ge(q["biased"], BEGUN + j * 8 + 32 * l)
                        pe.matmul(bank(4 + t % 4), d_q[half, b * P:b * P + P], d_k[half, :],
                                  start=True, stop=True).then_inc(q["scored"], 1)

                def turn(j, b):
                    pe.wait_ge(q["probs"], BEGUN + j * 8 + (32 * l + 2 * b + 2))
                    if b >= 2:
                        pe.wait_ge(q["kept"], BEGUN + j * 4 + (16 * l + b - 1))
                    else:
                        pe.wait_ge(q["v_kept"], j * 1 + (4 * l + 1))
                    for t in range(4):
                        last = pe.transpose(bank(b % 2)[:, t * P:t * P + P],
                                            d_s[2 * b][:, t * P:t * P + P], mat(IDENT))
                    last.then_inc(q["turned"], 1)

                def values(j):
                    pe.wait_ge(q["kept"], BEGUN + j * 4 + (16 * l + 4))
                    pe.wait_ge(q["evacuated"], BEGUN + j * 1 + 4 * l)
                    for t in range(4):
                        last = pe.matmul(bank(2), d_vs[:, t, :], d_aT[:, t, :], start=(t == 0), stop=(t == 3))
                    last.then_inc(q["summed"], 1)

                def head(j, first):
                    pe.wait_ge(q["staged_act"], j * 1 + (4 * l + 1))
                    pe.wait_ge(q["staged_dve"], j * 2 + (8 * l + 1))
                    score(j, 0)
                    if not first:
                        turn(j - 1, 2)
                    score(j, 1)
                    if not first:
                        turn(j - 1, 3)
                        values(j - 1)
                    pe.wait_ge(q["staged_dve"], j * 2 + (8 * l + 2))
                    pe.wait_ge(q["kept"], BEGUN + j * 4 + 16 * l)
                    for t in range(4):
                        last = pe.transpose(bank(0)[:, t * P:t * P + P], d_v[:, t * P:t * P + P], mat(IDENT))
                    last.then_inc(q["v_turned"], 1)
                    score(j, 2)
                    turn(j, 0)
                    score(j, 3)
                    turn(j, 1)

                head(0, True)
                with pe.Fori(1, 4) as j:
                    head(j, False)
                turn(3, 2)
                turn(3, 3)
                values(3)

            def fin1(ph):
                for n in range(8):
                    pe.wait_ge(f_sq_ready, 8 * ph["layer"] + n + 1)
                    if n == 0:
                        pe.wait_ge(sems["d"]["biased"], BEGUN + 32 * (ph["layer"] + 1))
                    if n >= 2:
                        pe.wait_ge(f_std, 8 * ph["layer"] + n - 1)
                    pe.matmul(bank(4 + n % 2), mat(MEAN64 if n < 4 else MEAN128), f_sq[n % 2][:],
                              start=True, stop=True).then_inc(f_sum, 1)

            def na(ph):
                q = sems["n"]

                with pe.Fori(0, 8) as j:
                    pe.wait_ge(q["staged_act"], j * 1 + 1)
                    pe.wait_ge(q["staged_dve"], j * 2 + 1)

                    def turn_v():
                        pe.wait_ge(q["staged_dve"], j * 2 + 2)
                        pe.wait_ge(q["kept"], BEGUN + j * 12)
                        pe.wait_ge(acc_free, ph["unit0"])
                        for t in range(9):
                            frm = 8 * ROWS * t if t < 7 else S + (t - 7) * P
                            last = pe.transpose(bank(t // 4)[:, t % 4 * P:t % 4 * P + P],
                                                n_v[:, frm:frm + P], mat(IDENT))
                        last.then_inc(q["v_turned"], 1)

                    def score(t):
                        hd, b = divmod(t, 6)
                        half = slice(HD * hd, HD * hd + HD)
                        if t >= 2:
                            pe.wait_ge(q["biased"], BEGUN + j * 12 + (t - 1))
                        S_ = bank(4 + t % 2)
                        if b < 4:
                            queries = n_q[half, b * P:b * P + P]
                            frm = KEY_COL[b] * ROWS
                            pe.matmul(S_[:, 0:2 * P], queries, n_k[half, frm:frm + 2 * P], start=True, stop=True)
                            pe.matmul(S_[:, 2 * P:4 * P], queries, n_k[half, S:T2],
                                      start=True, stop=True).then_inc(q["scored"], 1)
                        else:
                            pe.matmul(S_[:, 0:C], n_q[half, S + (b - 4) * P:S + (b - 3) * P],
                                      n_k[half, S:T2], start=True, stop=True).then_inc(q["scored"], 1)

                    def turn(t):
                        b = t % 6
                        pe.wait_ge(q["probs"], BEGUN + j * 12 + (t + 1))
                        if t >= 2:
                            pe.wait_ge(q["kept"], BEGUN + j * 12 + (t - 1))
                        else:
                            pe.wait_ge(q["v_kept"], j * 1 + 1)
                        for c in range(4 if b < 4 else 2):
                            last = pe.transpose(bank(t % 2)[:, c * P:c * P + P],
                                                n_s[t % 3][:, c * P:c * P + P], mat(IDENT))
                        last.then_inc(q["turned"], 1)

                    def values(t):
                        hd, b = divmod(t, 6)
                        pe.wait_ge(q["kept"], BEGUN + j * 12 + (t + 1))
                        if hd and b == 0:
                            pe.wait_ge(q["evacuated"], BEGUN + j * 4)
                        if b < 4:
                            o = bank(2 + 4 * hd)[:, b * P:b * P + P]
                            tiles = [KEY_COL[b] // 8, KEY_COL[b] // 8 + 2, 7, 8]
                        else:
                            o = bank(3 + 4 * hd)[:, (b - 4) * P:(b - 3) * P]
                            tiles = [7, 8]
                        for c, v in enumerate(tiles):
                            last = pe.matmul(o, n_vs[:, v, :], n_pT[t % 2][:, c * P:c * P + P],
                                             start=(c == 0), stop=(c == len(tiles) - 1))
                        last.then_inc(q["summed"], 1)

                    for t in range(12 + 3):
                        if t < 12:
                            score(t)
                        if t == 1:
                            turn_v()
                        if 2 <= t < 14:
                            turn(t - 2)
                        if t >= 3:
                            values(t - 3)
                    pe.wait_ge(q["evacuated"], BEGUN + j * 4 + 2)

            def swa(ph):
                q = sems["s"]
                pe.wait_ge(acc_free, ph["unit0"])
                pe.wait_ge(hn_out, ph["hn0"])
                for n, tile in enumerate(ROPE_TILES):
                    if n >= 2:
                        pe.wait_ge(rope_a, n - 1)
                    pe.matmul(bank(6 + n % 2), mat(ROT), proj[:, tile, 0:S], start=True, stop=True
                              ).then_inc(rope_mm, 1)
                pe.wait_ge(rope_a, len(ROPE_TILES))
                pe.wait_ge(rope_out, len(ROPE_TILES))
                for kv in range(2):
                    if kv:
                        pe.wait_ge(q["kept"], BEGUN + 32)
                    for t in range(6):
                        last = pe.transpose(bank(t // 4)[:, t % 4 * P:t % 4 * P + P],
                                            proj[:, 10 + kv, t * P:t * P + P], mat(IDENT))
                    last.then_inc(q["v_turned"], 1)
                    with pe.Fori(0, 4) as g:
                        n = g * 8 + 32 * kv
                        pe.wait_ge(q["staged_act"], g * 1 + (4 * kv + 1))

                        def score(t):
                            hd, b = divmod(t, 4)
                            half = slice(HD * hd, HD * hd + HD)
                            if t >= 2:
                                pe.wait_ge(q["biased"], BEGUN + n + (t - 1))
                            else:
                                pe.wait_ge(q["biased"], BEGUN + n)
                            S_ = sums[t % 2]
                            lo, hi = max(b - 1, 0) * P, min(b + 2, 4) * P
                            queries = s_q[half, b * P:b * P + P]
                            pe.matmul(S_[:, 0:hi - lo], queries, proj[half, 8 + kv, lo:hi], start=True, stop=True)
                            for c in range(2):
                                at_ = hi - lo + c * P
                                last = pe.matmul(S_[:, at_:at_ + P], queries,
                                                 proj[half, 8 + kv, S + c * P:S + c * P + P], start=True, stop=True)
                            last.then_inc(q["scored"], 1)

                        def turn(t):
                            b = t % 4
                            pe.wait_ge(q["probs"], BEGUN + n + (t + 1))
                            pe.wait_ge(q["kept"], BEGUN + n + t)
                            if t == 0:
                                pe.wait_ge(q["v_kept"], kv + 1)
                            for c in range(5 if 0 < b < 3 else 4):
                                last = pe.transpose(ps[:, c * P:c * P + P],
                                                    s_s[t % 3][:, c * P:c * P + P], mat(IDENT))
                            last.then_inc(q["turned"], 1)

                        def values(t):
                            hd, b = divmod(t, 4)
                            pe.wait_ge(q["kept"], BEGUN + n + (t + 1))
                            if hd and b == 0:
                                pe.wait_ge(q["evacuated"], BEGUN + g * 2 + 8 * kv)
                            lo, hi = max(b - 1, 0), min(b + 2, 4)
                            tiles = list(range(lo, hi)) + [4, 5]
                            for c, v in enumerate(tiles):
                                last = pe.matmul(bank(2 + hd)[:, b * P:b * P + P], s_vs[:, v, :],
                                                 s_pT[t % 2][:, c * P:c * P + P],
                                                 start=(c == 0), stop=(c == len(tiles) - 1))
                            last.then_inc(q["summed"], 1)

                        for t in range(8 + 3):
                            if t < 8:
                                score(t)
                            if 2 <= t < 10:
                                turn(t - 2)
                            if t >= 3:
                                values(t - 3)
                        pe.wait_ge(q["evacuated"], BEGUN + g * 2 + (8 * kv + 1))

            begin(pe, ("v_turned", "scored", "turned", "summed"))
            pe.wait_ge(constants_in, 32)
            for ph in phases:
                kind = ph["kind"]
                if kind == "norm":
                    norm(ph)
                elif kind == "normed":
                    normed_units(ph)
                elif kind in ("proj", "glu", "conv", "resid"):
                    plain_units(ph)
                elif kind == "retention":
                    pe.wait_ge(hn_out, ph["hn0"])
                    retention(ph)
                elif kind == "diff":
                    diff(ph)
                elif kind == "fin1":
                    fin1(ph)
                elif kind == "na":
                    pe.wait_ge(hn_out, ph["hn0"])
                    na(ph)
                elif kind == "swa":
                    swa(ph)

        @block.scalar
        def _(act):
            begin(act, ("kept",))
            for q in range(4):
                act.dma_start(xT[:, 2 * q:2 * q + 2, 0:S], d["x"][:, 2 * q:2 * q + 2, :]).then_inc(x_in[q], 16)
                if q == 0:
                    act.dma_start(mats[:], d["mats"]).then_inc(constants_in, 16)
            act.dma_start(small[:], d["small"]).then_inc(constants_in, 16)
            act.dma_start(lam_vec[:], d["lam"]).then_inc(loaded, 16)
            act.dma_start(silu_c[:], d["c"]).then_inc(loaded, 16)
            act.dma_start(xT[:, :, S:T2], d["ctx"]).then_inc(loaded, 16)

            def row(ap):
                return ap.rearrange("p (a n) -> p a n", a=1)

            def hi_part(par, loads, K):
                act.wait_ge(w_loaded[par], loads)
                act.activation(w_hi[par][:, 0:K * P], w_raw[par][:, 0:K * P], ACT.Copy).then_inc(w_hi_ready, 1)

            def setup():
                act.wait_ge(loaded, N_INPUTS)
                act.activation(silu_c[:], silu_c[:], ACT.Silu).then_inc(silu_c_ready, 1)
                act.activation(lgam[:], col("decay", 0, DEPTH * 16), ACT.Exp).then_inc(lam_exp, 1)
                act.wait_ge(lam_step, 4)
                act.activation(lam[:, 4:8], lam[:, 0:4], ACT.Exp).then_inc(lam_exp, 1)

            act.wait_ge(ready, 2)

            def units_of(ph, body, peel=0):
                n, u0 = ph["units"] // 2, ph["unit0"]
                k_next = next((p["K"] for p in phases if p.get("weight") and p["unit0"] == u0 + 2 * n), None)
                same = n if k_next == ph["K"] else n - 1

                def pair(i, K):
                    def split(par):
                        if K is not None:
                            hi_part(par, i * 16 + (8 * u0 + 32), K)
                    body(i, split)

                peel = max(peel, same if same == 1 else 0)
                for i in range(min(peel, n)):
                    pair(i, ph["K"] if i < same else k_next)
                if same > peel:
                    with act.Fori(peel, same) as i:
                        pair(i, ph["K"])
                if same < n and n > peel:
                    pair(n - 1, k_next)

            def resid(ph):
                T, n0 = ph["norm_T"], ph["norm0"]

                def body(i, split):
                    for par in range(2):
                        act.wait_ge(mm_done, i * 2 + (ph["unit0"] + par + 1))
                        split(par)
                        if T is not None:
                            act.wait_ge(acc_free, i * 2 + (ph["unit0"] + par + 1))
                            if not (isinstance(i, int) and i == 0):
                                act.wait_ge(n_added, i * 2 + (KT * (n0 - 1) + par))
                            act.activation(row(n_sq[par][:, 0:T]), xT[:, bass.ds(i * 2 + par, 1), 0:T],
                                           ACT.Square).then_inc(n_sq_ready, 1)
                units_of(ph, body, peel=0 if T is None else 1)

            def norm(ph):
                n0, T = ph["norm0"], ph["T"]
                if n0 == 0:
                    for k in range(KT):
                        act.wait_ge(x_in[k // 2], 16)
                        if k >= 2:
                            act.wait_ge(n_sum, k - 1)
                        act.activation(n_sq[k % 2][:, 0:T], xT[:, k, 0:T], ACT.Square).then_inc(n_sq_ready, 1)
                    for par in range(2):
                        hi_part(par, 16, KT)
                else:
                    act.wait_ge(mm_done, ph["unit0"])
                act.wait_ge(n_sum, 8 + n0)
                act.activation(n_rstd[:, 0:T], sums[0][:, 0:T], ACT.Sqrt, bias=eps1[:]).then_inc(n_std, 1)
                for k in range(KT):
                    act.wait_ge(n_xn_ready, KT * n0 + k + 1)
                    if ph["block"] == 1 or k % 2 == 0:
                        act.activation(h_hi[:, k, 0:T], n_xn[k % 4][:, 0:T], ACT.Copy).then_inc(h_hi_ready, 1)
                        continue
                    for to, _, w, c in segments(T):
                        shift = mod[:, ph["layer"], 0 if ph["which"] == "attn" else 3, k, c:c + 1]
                        last = act.activation(h_hi[:, k, to:to + w], n_xn[k % 4][:, to:to + w], ACT.Identity,
                                              bias=shift)
                    last.then_inc(h_hi_ready, 1)

            def take_out(ph):
                def body(i, split):
                    for par in range(2):
                        act.wait_ge(mm_done, i * 2 + (ph["unit0"] + par + 1))
                        dst = proj1 if ph["T"] == S and ph["weight"] == "w_in" else proj
                        if ph["weight"] == "na_qkv":
                            act.activation(by_columns(proj[:, bass.ds(i * 2 + (ph["tile0"] + par), 1), 0:S]),
                                           from_rows(acc[par][:, 0:S]), ACT.Copy)
                            act.activation(proj[:, bass.ds(i * 2 + (ph["tile0"] + par), 1), S:T2],
                                           row(acc[par][:, S:T2]), ACT.Copy).then_inc(acc_free, 1)
                            split(par)
                            continue
                        act.activation(dst[:, bass.ds(i * 2 + (ph["tile0"] + par), 1), 0:ph["T"]],
                                       row(acc[par][:, 0:ph["T"]]),
                                       ACT.Silu if ph["func"] == "silu" else ACT.Copy).then_inc(acc_free, 1)
                        split(par)
                units_of(ph, body)

            def head_norm(ph):
                T, h0 = ph["T"], ph["hn0"]
                dst = proj1 if ph["weight"] == "w_in" else proj

                def square(i, par):
                    act.wait_ge(acc_free, i * 2 + (ph["unit0"] + par + 1))
                    act.activation(row(hn_sq[par][:, 0:T]), dst[:, bass.ds(i * 2 + (ph["tile0"] + par), 1), 0:T],
                                   ACT.Square).then_inc(hn_sq_ready, 1)

                def root(i, par):
                    act.wait_ge(hn_sum, i * 2 + (h0 + par + 1))
                    if isinstance(i, int):
                        act.wait_ge(hn_out, max(2 * i + h0 + par - 1, h0))
                    else:
                        act.wait_ge(hn_out, i * 2 + (h0 + par - 1))
                    act.activation(hn_r[par][:, 0:T], sums[par][:, 0:T], ACT.Sqrt, bias=eps1[:]).then_inc(hn_std, 1)

                def body(i, split):
                    for par in range(2):
                        act.wait_ge(mm_done, i * 2 + (ph["unit0"] + par + 1))
                        split(par)
                        square(i, par)
                        if par:
                            root(i, 0)
                        elif not (isinstance(i, int) and i == 0):
                            root(i - 1, 1)
                units_of(ph, body, peel=1 if h0 else 2)
                root(ph["units"] // 2 - 1, 1)

            def glu(ph):
                act.wait_ge(acc_free, ph["unit0"])

                def body(f, split):
                    act.wait_ge(mm_done, f * 2 + (ph["unit0"] + 1))
                    split(0)
                    act.activation(glu_g[:], acc[0][:, 0:S], ACT.Silu).then_inc(acc_free, 1)
                    act.wait_ge(mm_done, f * 2 + (ph["unit0"] + 2))
                    split(1)
                    act.wait_ge(acc_free, f * 2 + (ph["unit0"] + 2))
                    act.activation(b_hi[:, dyn(f), :], row(glu_a[:]), ACT.Copy).then_inc(glu_hi, 1)
                units_of(ph, body)

            def conv(ph):
                n0, T = ph["conv0"], ph["T"]
                W = ACTW if T == T2 else S
                act.wait_ge(acc_free, ph["unit0"])

                def body(f, split):
                    for par in range(2):
                        act.wait_ge(mm_done, f * 2 + (ph["unit0"] + par + 1))
                        split(par)
                        act.wait_ge(conv_step, BEGUN + f * 7 + 7 * n0)
                        for to, frm, n, _ in segments(T, CTX_AT):
                            last = act.activation(u_pad[par][:, 2 + frm:2 + frm + n], acc[par][:, to:to + n], ACT.Copy)
                        last.then_inc(acc_free, 1)
                    act.wait_ge(conv_step, BEGUN + f * 7 + (7 * n0 + 6))
                    act.activation(conv_y[1][:, 0:W], conv_y[1][:, 0:W], ACT.Silu).then_inc(conv_gate, 1)
                    act.wait_ge(conv_step, BEGUN + f * 7 + (7 * n0 + 7))
                    act.activation(a_hi[:, dyn(f), 0:W], row(conv_y[0][:, 0:W]), ACT.Copy).then_inc(conv_hi, 1)
                units_of(ph, body)

            def retention(ph):
                q, l = sems["r"], ph["layer"]
                with act.Fori(0, 4) as j:
                    act.wait_ge(q["scored"], BEGUN + j * 8 + 32 * l)
                    act.activation(row(r_q[:]), proj1[:, bass.ds(j + 8, 1), :], ACT.Copy).then_inc(q["staged_act"], 1)
                    act.wait_ge(q["v_turned"], BEGUN + j + (4 * l + 1))
                    act.wait_ge(q["summed"], BEGUN + j * 8 + 32 * l)
                    act.activation(r_vs[:].rearrange("p t n -> p (t n)"), bank(0), ACT.Copy).then_inc(q["v_kept"], 1)
                    for hd in range(2):
                        act.wait_ge(q["mask_arg"], BEGUN + j * 4 + (16 * l + 2 * hd + 2))
                        act.activation(r_mask[hd][:], r_mask[hd][:], ACT.Exp).then_inc(q["bias"], 1)

            def diff(ph):
                q, l = sems["d"], ph["layer"]
                act.wait_ge(sems["r"]["summed"], BEGUN + 32 * (l + 1))

                def exp(j, b):
                    for t in (2 * b, 2 * b + 1):
                        act.wait_ge(q["negmax"], j * 8 + (32 * l + t + 1))
                        act.activation(d_s[t][:], d_s[t][:], ACT.Exp, bias=stats[:, 8 + t % 4:9 + t % 4],
                                       accum_out=stats[:, 12 + t % 4:13 + t % 4]).then_inc(q["exped"], 1)

                def keep(j, b):
                    act.wait_ge(q["turned"], BEGUN + j * 4 + (16 * l + b + 1))
                    if b == 0:
                        act.wait_ge(q["summed"], BEGUN + j + 4 * l)
                    act.activation(d_aT[:, :, b * P:b * P + P], bank(b % 2).rearrange("p (t n) -> p t n", n=P),
                                   ACT.Copy).then_inc(q["kept"], 1)

                def head(j, first):
                    act.wait_ge(q["scored"], BEGUN + j * 8 + 32 * l)
                    act.activation(row(d_q[:]), proj1[:, dyn(j), :], ACT.Copy).then_inc(q["staged_act"], 1)
                    act.wait_ge(q["biased"], BEGUN + j * 8 + 32 * l)
                    act.activation(d_bias[:], d_dist[:], ACT.Copy, scale=dcol("slope", j)).then_inc(q["bias"], 1)
                    exp(j, 0)
                    if not first:
                        keep(j - 1, 2)
                    exp(j, 1)
                    if not first:
                        keep(j - 1, 3)
                    act.wait_ge(q["v_turned"], BEGUN + j + (4 * l + 1))
                    act.wait_ge(q["summed"], BEGUN + j + 4 * l)
                    act.activation(d_vs[:].rearrange("p t n -> p (t n)"), bank(0), ACT.Copy).then_inc(q["v_kept"], 1)
                    exp(j, 2)
                    keep(j, 0)
                    exp(j, 3)
                    keep(j, 1)

                head(0, True)
                with act.Fori(1, 4) as j:
                    head(j, False)
                keep(3, 2)
                keep(3, 3)

            def fin1(ph):
                l = ph["layer"]
                for n in range(8 + 4):
                    if n < 8:
                        tile = 8 + n if n < 4 else n - 4
                        if n == 0:
                            act.wait_ge(sems["r"]["evacuated"], BEGUN + 8 * (l + 1))
                            act.wait_ge(sems["d"]["evacuated"], BEGUN + 4 * (l + 1))
                        if n >= 2:
                            act.wait_ge(f_sum, 8 * l + n - 1)
                        act.activation(f_sq[n % 2][:], proj1[:, tile, :], ACT.Square).then_inc(f_sq_ready, 1)
                    if 1 <= n <= 8:
                        act.wait_ge(f_sum, 8 * l + n)
                        if n >= 3:
                            act.wait_ge(f_y_ready, 12 * l + _f_y(n - 3))
                        act.activation(f_r[(n - 1) % 2][:], bank(4 + (n - 1) % 2), ACT.Sqrt,
                                       bias=eps1[:]).then_inc(f_std, 1)
                    if n >= 4:
                        k = n - 4
                        act.wait_ge(f_y_ready, 12 * l + _f_y(k))
                        act.activation(h_hi[:, k, 0:S], proj1[:, 8 + k if k < 4 else k - 4, :], ACT.Copy
                                       ).then_inc(h_hi_ready, 1)

            def na(ph):
                q = sems["n"]
                with act.Fori(0, 8) as j:
                    act.wait_ge(q["scored"], BEGUN + j * 12)
                    act.activation(row(n_q[:]), proj[:, bass.ds(j, 1), :], ACT.Copy).then_inc(q["staged_act"], 1)

                    def keep_v():
                        act.wait_ge(q["v_turned"], BEGUN + j + 1)
                        act.wait_ge(q["summed"], BEGUN + j * 12)
                        for b in range(3):
                            n = (P if b == 2 else S)
                            last = act.activation(n_vs[:].rearrange("p t n -> p (t n)")[:, b * S:b * S + n],
                                                  bank(b, n), ACT.Copy)
                        last.then_inc(q["v_kept"], 1)

                    def exp(t):
                        w = S if t % 6 < 4 else C
                        act.wait_ge(q["negmax"], j * 12 + (t + 1))
                        act.activation(n_s[t % 3][:, 0:w], n_s[t % 3][:, 0:w], ACT.Exp,
                                       bias=stats[:, 3 + t % 3:4 + t % 3],
                                       accum_out=stats[:, 6 + t % 3:7 + t % 3]).then_inc(q["exped"], 1)

                    def keep(t):
                        w = S if t % 6 < 4 else C
                        act.wait_ge(q["turned"], BEGUN + j * 12 + (t + 1))
                        if t >= 2:
                            act.wait_ge(q["summed"], BEGUN + j * 12 + (t - 1))
                        act.activation(n_pT[t % 2][:, 0:w], bank(t % 2, w), ACT.Copy).then_inc(q["kept"], 1)

                    for t in range(12 + 2):
                        if t < 12:
                            exp(t)
                        if t == 1:
                            keep_v()
                        if t >= 2:
                            keep(t - 2)

            def swa(ph):
                q = sems["s"]
                act.wait_ge(hn_out, ph["hn0"])
                act.wait_ge(rope_out, len(ROPE_TILES))
                for kv in range(2):
                    act.wait_ge(q["v_turned"], BEGUN + kv + 1)
                    if kv:
                        act.wait_ge(q["summed"], BEGUN + 32)
                    act.activation(s_vs[:].rearrange("p t n -> p (t n)"), ps[:, 0:6 * P], ACT.Copy).then_inc(q["v_kept"], 1)
                    with act.Fori(0, 4) as g:
                        n = g * 8 + 32 * kv
                        act.wait_ge(q["scored"], BEGUN + n)
                        act.activation(row(s_q[:]), proj[:, bass.ds(g + 4 * kv, 1), 0:S], ACT.Copy
                                       ).then_inc(q["staged_act"], 1)

                        def width(t):
                            return (5 if 0 < t % 4 < 3 else 4) * P

                        def exp(t):
                            act.wait_ge(q["negmax"], n + (t + 1))
                            act.activation(s_s[t % 3][:, 0:width(t) + 1], s_s[t % 3][:, 0:width(t) + 1], ACT.Exp,
                                           bias=stats[:, 3 + t % 3:4 + t % 3],
                                           accum_out=stats[:, 6 + t % 3:7 + t % 3]).then_inc(q["exped"], 1)

                        def keep(t):
                            act.wait_ge(q["turned"], BEGUN + n + (t + 1))
                            act.wait_ge(q["summed"], BEGUN + n + max(t - 1, 0))
                            act.activation(s_pT[t % 2][:, 0:width(t)], ps[:, 0:width(t)], ACT.Copy).then_inc(q["kept"], 1)

                        for t in range(8 + 2):
                            if t < 8:
                                exp(t)
                            if t >= 2:
                                keep(t - 2)

            def fin2(ph):
                s_done = sems["n"]["evacuated"] if ph["T"] == T2 else sems["s"]["evacuated"]
                act.wait_ge(s_done, BEGUN + (32 if ph["T"] == T2 else 16))
                for n in range(8):
                    act.activation(h_hi[:, n, 0:ph["T"]], proj[:, n, 0:ph["T"]], ACT.Copy).then_inc(h_hi_ready, 1)

            for ph in phases:
                kind = ph["kind"]
                if kind == "norm":
                    norm(ph)
                    if ph["norm0"] == 0:
                        setup()
                elif kind == "normed":
                    head_norm(ph)
                elif kind == "proj":
                    take_out(ph)
                elif kind == "resid":
                    resid(ph)
                elif kind == "glu":
                    glu(ph)
                elif kind == "conv":
                    conv(ph)
                elif kind == "retention":
                    act.wait_ge(hn_out, ph["hn0"])
                    act.wait_ge(mm_done, ph["unit0"])
                    retention(ph)
                elif kind == "diff":
                    diff(ph)
                elif kind == "fin1":
                    fin1(ph)
                elif kind == "na":
                    act.wait_ge(hn_out, ph["hn0"])
                    act.wait_ge(mm_done, ph["unit0"])
                    na(ph)
                elif kind == "swa":
                    act.wait_ge(mm_done, ph["unit0"])
                    swa(ph)
                elif kind == "fin2":
                    fin2(ph)

        @block.vector
        def _(dve):
            def row(ap):
                return ap.rearrange("p (a n) -> p a n", a=1)

            begin(dve, ("biased", "evacuated", "mask_arg", "probs"), (conv_step, a_lo_ready))
            dve.memset(zero1[:], 0.0).then_inc(ready, 1)
            dve.memset(eps1[:], EPS).then_inc(ready, 1)
            def setup():
                dve.wait_ge(loaded, N_INPUTS)
                for l in range(DEPTH):
                    for m in range(2):
                        n = 2 * l + m
                        if n:
                            dve.wait_ge(lam_step, n)
                        dve.tensor_tensor_reduce(lam_prod[:], lam_vec[:, 4 * l + 2 * m, :], lam_vec[:, 4 * l + 2 * m + 1, :],
                                                 1.0, 0.0, ALU.mult, ALU.add, lam[:, n:n + 1]).then_inc(lam_step, 1)
                dve.wait_ge(lam_exp, 2)
                for l in range(DEPTH):
                    init = 0.8 - 0.6 * float(np.exp(-0.3 * l))
                    dve.scalar_tensor_tensor(out=lam[:, 8 + l:9 + l], in0=lam[:, 4 + 2 * l:5 + 2 * l], scalar=init,
                                             in1=lam[:, 5 + 2 * l:6 + 2 * l], op0=ALU.add, op1=ALU.subtract
                                             ).then_inc(lam_step, 1)
                    dve.tensor_scalar(lam[:, 10 + l:11 + l], col("g_diff", l), 1.0 - init, None, ALU.mult
                                      ).then_inc(lam_step, 1)
                    dve.tensor_scalar(col("g_dqk", 8 * l, 4), col("g_dqk", 8 * l, 4), HD ** -0.5, None, ALU.mult
                                      ).then_inc(lam_step, 1)
                dve.tensor_scalar(col("g_na", 0, 8), col("g_na", 0, 8), HD ** -0.5, None, ALU.mult).then_inc(lam_step, 1)
                dve.tensor_scalar(col("g_swa", 0, 8), col("g_swa", 0, 8), HD ** -0.5, None, ALU.mult).then_inc(lam_step, 1)
                dve.tensor_scalar(lgam[:], lgam[:], -1.0, None, ALU.mult).then_inc(lam_step, 1)
                dve.wait_ge(lam_step, 13)

            def modulation(i, u0):
                first = isinstance(i, int) and i == 0 and u0 == 0
                dve.wait_ge(silu_c_ready, 1)
                dve.wait_ge(mod_loaded, i * 16 + (8 * u0 + 16))
                if not first:
                    dve.wait_ge(mod_kept, i + u0 // 2)
                    dve.wait_ge(mod_step, i * 2 + u0)
                dve.tensor_tensor_reduce(mod_junk[:], mod_w[:], silu_c[:, 0, :], 1.0, 0.0, ALU.mult, ALU.add,
                                         mod_sum[:, 0:1]).then_inc(mod_step, 1)
                dve.wait_ge(mod_step, i * 2 + (u0 + 1))
                dve.tensor_tensor_reduce(mod_junk[:], mod_w[:], silu_c[:, 1, :], 1.0, 0.0, ALU.mult, ALU.add,
                                         mod_sum[:, 1:2]).then_inc(mod_step, 1)
                dve.wait_ge(mod_step, i * 2 + (u0 + 2))
                dve.tensor_copy(mod[:].rearrange("p l s k c -> p (l s k c)")[:, bass.ds(i * 2 + u0, 2)],
                                mod_sum[:]).then_inc(mod_kept, 1)

            def modulation_pairs(ph):
                if ph["unit0"] < MOD_UNITS:
                    with dve.Fori(0, ph["units"] // 2) as i:
                        modulation(i, ph["unit0"])

            def modulation_end():
                dve.wait_ge(mod_kept, DEPTH * 48)
                dve.tensor_tensor(mod[:].rearrange("p l s k c -> p (l s k c)"),
                                  mod[:].rearrange("p l s k c -> p (l s k c)"),
                                  col("b_mod", 0, DEPTH * 96), ALU.add).then_inc(mod_ready, 1)
                dve.wait_ge(mod_ready, 1)
                for l in range(DEPTH):
                    for w, name in enumerate(("g2_attn", "g2_ffn")):
                        dve.scalar_tensor_tensor(
                            out=gs[:, l, w].rearrange("p k c -> p (k c)"),
                            in0=mod[:, l, 1 + 3 * w].rearrange("p k c -> p (k c)"), scalar=1.0,
                            in1=col(name, 16 * l, 16), op0=ALU.add, op1=ALU.mult).then_inc(mod_ready, 1)
                dve.wait_ge(mod_ready, 5)

            def norm(ph):
                n0, T, g = ph["norm0"], ph["T"], ph["h0"]
                w_i = 0 if ph["which"] == "attn" else 1
                if n0 == 0:
                    dve.wait_ge(constants_in, 32)
                dve.wait_ge(n_std, n0 + 1)
                dve.reciprocal(n_rstd[:, 0:T], n_rstd[:, 0:T]).then_inc(n_recip, 1)
                dve.wait_ge(n_recip, n0 + 1)

                def shift(k, c):
                    return mod[:, ph["layer"], 3 * w_i, k, c:c + 1]

                def normed(k):
                    if k >= 4:
                        dve.wait_ge((h_even, h_odd)[k % 2], 4 * g + (k - 4) // 2 + 1)
                    for to, _, w, c in segments(T):
                        gain = col("g_" + ph["which"], KT * ph["layer"] + k) if ph["block"] == 1 else \
                            gs[:, ph["layer"], w_i, k, c:c + 1]
                        last = dve.scalar_tensor_tensor(
                            out=n_xn[k % 4][:, to:to + w], in0=xT[:, k, to:to + w], scalar=gain,
                            in1=n_rstd[:, to:to + w], op0=ALU.mult, op1=ALU.mult)
                    if ph["block"] == 2 and k % 2 == 0:
                        last.then_inc(n_scaled, 1)
                        dve.wait_ge(n_scaled, 4 * (n0 - 2 * DEPTH) + k // 2 + 1)
                        for to, _, w, c in segments(T):
                            last = dve.tensor_scalar(n_xn[k % 4][:, to:to + w], n_xn[k % 4][:, to:to + w],
                                                     shift(k, c), None, ALU.add)
                    last.then_inc(n_xn_ready, 1)

                def odd_lo(k):
                    dve.wait_ge(h_hi_ready, KT * g + k + 1)
                    for to, _, w, c in segments(T):
                        last = dve.scalar_tensor_tensor(
                            out=h_lo[:, k, to:to + w], in0=n_xn[k % 4][:, to:to + w],
                            scalar=zero1[:] if ph["block"] == 1 else shift(k, c),
                            in1=h_hi[:, k, to:to + w].bitcast(F32), op0=ALU.add, op1=ALU.subtract)
                    last.then_inc(h_odd, 1)

                normed(0)
                for k in range(1, KT, 2):
                    normed(k)
                    if k < KT - 1:
                        normed(k + 1)
                    odd_lo(k)

            def head_norm(ph):
                T, h0 = ph["T"], ph["hn0"]
                dst = proj1 if ph["weight"] == "w_in" else proj

                def tile(i, par):
                    return dst[:, bass.ds(i * 2 + (ph["tile0"] + par), 1), 0:T]

                def take(i, par):
                    dve.wait_ge(mm_done, i * 2 + (ph["unit0"] + par + 1))
                    if ph["weight"] == "na_qkv":
                        dve.tensor_copy(by_columns(dst[:, bass.ds(i * 2 + (ph["tile0"] + par), 1), 0:S]),
                                        from_rows(acc[par][:, 0:S]))
                        dve.tensor_copy(dst[:, bass.ds(i * 2 + (ph["tile0"] + par), 1), S:T2],
                                        row(acc[par][:, S:T2])).then_inc(acc_free, 1)
                    else:
                        dve.tensor_copy(tile(i, par), row(acc[par][:, 0:T])).then_inc(acc_free, 1)

                def scale(i, par):
                    dve.wait_ge(hn_std, i * 2 + (h0 + par + 1))
                    dve.reciprocal(hn_r[par][:, 0:T], hn_r[par][:, 0:T]).then_inc(hn_recip, 1)
                    dve.wait_ge(hn_recip, i * 2 + (h0 + par + 1))
                    dve.scalar_tensor_tensor(out=tile(i, par), in0=tile(i, par),
                                             scalar=dcol(ph["gains"][0], i * 2 + (ph["gains"][1] + par)),
                                             in1=row(hn_r[par][:, 0:T]), op0=ALU.mult, op1=ALU.mult
                                             ).then_inc(hn_out, 1)

                beside = ph["unit0"] < MOD_UNITS
                if beside:
                    modulation(0, ph["unit0"])
                take(0, 0)
                take(0, 1)
                scale(0, 0)
                if ph["units"] > 2:
                    with dve.Fori(1, ph["units"] // 2) as i:
                        if beside:
                            modulation(i, ph["unit0"])
                        take(i, 0)
                        scale(i - 1, 1)
                        take(i, 1)
                        scale(i, 0)
                scale(ph["units"] // 2 - 1, 1)

            def resid(ph):
                T, n0 = ph["norm_T"], ph["norm0"]
                if T is not None:
                    dve.wait_ge(a_lo_ready, BEGUN + ph["glu0"] + ph["conv0"])
                    dve.memset(n_sum_sq[:, 0:T], 0.0).then_inc(n_added, 1)

                def body(i, first):
                    if ph["unit0"] < MOD_UNITS:
                        modulation(i, ph["unit0"])
                    for par in range(2):
                        dve.wait_ge(mm_done, i * 2 + (ph["unit0"] + par + 1))
                        for to, _, n, c in segments(ph["T"]):
                            x_ = xT[:, bass.ds(i * 2 + par, 1), to:to + n]
                            if ph["gate"] is None:
                                gate = 1.0
                            else:
                                l, part = ph["gate"]
                                gate = mod[:].rearrange("p l s k c -> p (l s k c)")[
                                    :, bass.ds(i * 4 + (2 * KT * (6 * l + part) + 2 * par + c), 1)]
                            last = dve.scalar_tensor_tensor(out=x_, in0=row(acc[par][:, to:to + n]), scalar=gate,
                                                            in1=x_, op0=ALU.mult, op1=ALU.add)
                        last.then_inc(acc_free, 1)
                        if T is not None and not (isinstance(i, int) and i + par == 0):
                            before = KT * (n0 - 1) + par
                            dve.wait_ge(n_sq_ready, i * 2 + (KT * n0 + par))
                            dve.wait_ge(n_added, i * 2 + before)
                            dve.tensor_tensor(n_sum_sq[:, 0:T], n_sum_sq[:, 0:T], n_sq[1 - par][:, 0:T], ALU.add
                                              ).then_inc(n_added, 1)
                pairs(dve, ph, body, T is not None)

            def glu(ph):
                n0 = ph["glu0"]
                with dve.Fori(0, FH) as f:
                    modulation(f, ph["unit0"])
                    dve.wait_ge(acc_free, f * 2 + (ph["unit0"] + 1))
                    dve.wait_ge(mm_done, f * 2 + (ph["unit0"] + 2))
                    dve.wait_ge(a_lo_ready, BEGUN + f + n0)
                    dve.tensor_tensor(glu_a[:], acc[1][:, 0:S], glu_g[:], ALU.mult).then_inc(acc_free, 1)
                    dve.wait_ge(glu_hi, f + (n0 + 1))
                    dve.tensor_tensor(b_lo[:, bass.ds(f, 1), :], row(glu_a[:]),
                                      b_hi[:, bass.ds(f, 1), :].bitcast(F32), ALU.subtract).then_inc(a_lo_ready, 1)

            def conv(ph):
                n0, T, l = ph["conv0"], ph["T"], ph["layer"]
                W = ACTW if T == T2 else S
                for par in range(2):
                    for c in (0, 2 + S, 2 + ACTW):
                        dve.memset(u_pad[par][:, c:c + 2], 0.0).then_inc(conv_zero, 1)
                with dve.Fori(0, FH) as f:
                    m = 7 * n0

                    def tap(par, j):
                        return dcol("conv", f * 8 + (((l * FT + ph["half"] * FH) * 2 + par) * 4 + j))
                    for j in range(3):
                        for par in range(2):
                            y, u = conv_y[par][:, 0:W], u_pad[par][:, 1 + j:1 + j + W]
                            if j == 0:
                                dve.wait_ge(a_lo_ready, BEGUN + f + (ph["glu0"] + n0))
                                dve.wait_ge(acc_free, f * 2 + (ph["unit0"] + par + 1))
                                dve.wait_ge(conv_zero, 6 * (n0 // FH + 1))
                                dve.tensor_scalar(y, u, tap(par, 0), tap(par, 3), ALU.mult, ALU.add
                                                  ).then_inc(conv_step, 1)
                            else:
                                dve.wait_ge(conv_step, BEGUN + f * 7 + (m + 2 * j + par - 1))
                                dve.scalar_tensor_tensor(out=y, in0=u, scalar=tap(par, j), in1=y,
                                                         op0=ALU.mult, op1=ALU.add).then_inc(conv_step, 1)
                    dve.wait_ge(conv_gate, f + (n0 + 1))
                    dve.wait_ge(conv_step, BEGUN + f * 7 + (m + 6))
                    dve.tensor_tensor(conv_y[0][:, 0:W], conv_y[0][:, 0:W], conv_y[1][:, 0:W], ALU.mult
                                      ).then_inc(conv_step, 1)
                    dve.wait_ge(conv_hi, f + (n0 + 1))
                    dve.tensor_tensor(a_lo[:, bass.ds(f, 1), 0:W], row(conv_y[0][:, 0:W]),
                                      a_hi[:, bass.ds(f, 1), 0:W].bitcast(F32), ALU.subtract).then_inc(a_lo_ready, 1)

            def retention(ph):
                q, l = sems["r"], ph["layer"]
                dve.wait_ge(tab["retention"], 48 * (l + 1))
                with dve.Fori(0, 4) as j:
                    dve.wait_ge(q["scored"], BEGUN + j * 8 + 32 * l)
                    dve.wait_ge(q["v_turned"], BEGUN + j + 4 * l)
                    dve.tensor_scalar(row(r_k[:]), proj1[:, bass.ds(j + 12, 1), :], HD ** -0.5, None, ALU.mult
                                      ).then_inc(q["staged_dve"], 1)
                    dve.tensor_copy(row(r_v[:]), proj1[:, bass.ds(j + 16, 1), :]).then_inc(q["staged_dve"], 1)
                    for hd in range(2):
                        lg = [lgam[:, bass.ds(j * 2 + (16 * l + 8 * b + hd), 1)] for b in range(2)]
                        m = 16 * l + 2 * hd
                        dve.wait_ge(q["mask_arg"], BEGUN + j * 4 + m)
                        dve.tensor_scalar(r_tmp[:], r_dpos[:], lg[0], None, ALU.mult).then_inc(q["mask_arg"], 1)
                        dve.wait_ge(q["mask_arg"], BEGUN + j * 4 + (m + 1))
                        dve.wait_ge(q["biased"], BEGUN + j * 8 + 32 * l)
                        dve.scalar_tensor_tensor(out=r_mask[hd][:], in0=r_dneg[:], scalar=lg[1], in1=r_tmp[:],
                                                 op0=ALU.mult, op1=ALU.add).then_inc(q["mask_arg"], 1)
                    for t in range(8 + 1):
                        if t < 8:
                            hd, s = divmod(t, 4)
                            dve.wait_ge(q["bias"], j * 2 + (8 * l + hd + 1))
                            dve.wait_ge(q["scored"], BEGUN + j * 8 + (32 * l + t + 1))
                            if t >= 3:
                                dve.wait_ge(q["summed"], BEGUN + j * 8 + (32 * l + t - 2))
                            else:
                                dve.wait_ge(q["summed"], BEGUN + j * 8 + 32 * l)
                            dve.tensor_tensor(r_sc[t % 3][:], bank(4 + t % 2),
                                              r_mask[hd][:, (3 - s) * P:(3 - s) * P + S], ALU.mult
                                              ).then_inc(q["biased"], 1)
                        if t in (5, 8):
                            hd = 0 if t == 5 else 1
                            half = slice(HD * hd, HD * hd + HD)
                            dve.wait_ge(q["summed"], BEGUN + j * 8 + (32 * l + 4 * hd + 4))
                            dve.tensor_copy(proj1[half, bass.ds(j + 8, 1), :], row(bank(2 + hd)[half, :])
                                            ).then_inc(q["evacuated"], 1)

            def diff(ph):
                q, l = sems["d"], ph["layer"]
                dve.wait_ge(sems["r"]["evacuated"], BEGUN + 8 * (l + 1))

                def bias(j, b):
                    for t in (2 * b, 2 * b + 1):
                        dve.wait_ge(q["bias"], j + (4 * l + 1))
                        dve.wait_ge(q["scored"], BEGUN + j * 8 + (32 * l + t + 1))
                        if isinstance(j, int):
                            dve.wait_ge(q["turned"], BEGUN + 16 * l)
                        else:
                            dve.wait_ge(q["turned"], BEGUN + j * 4 + (16 * l + b - 3))
                        dve.memset(pace[:, 2:3], 0.0)
                        dve.tensor_tensor_reduce(d_s[t][:], bank(4 + t % 4), d_bias[:, (3 - b) * P:(3 - b) * P + S],
                                                 1.0, NEG, ALU.add, ALU.max,
                                                 stats[:, 4 + t % 4:5 + t % 4]).then_inc(q["biased"], 1)
                        dve.wait_ge(q["biased"], BEGUN + j * 8 + (32 * l + t + 1))
                        dve.tensor_scalar(stats[:, 8 + t % 4:9 + t % 4], stats[:, 4 + t % 4:5 + t % 4],
                                          -1.0, None, ALU.mult).then_inc(q["negmax"], 1)

                def probs(j, b):
                    t0, t1 = 2 * b, 2 * b + 1
                    n = 32 * l + 2 * b
                    dve.wait_ge(q["exped"], j * 8 + (32 * l + t1 + 1))
                    sm = stats[:, 12 + t0 % 4:14 + t0 % 4]
                    dve.wait_ge(q["probs"], BEGUN + j * 8 + n)
                    dve.reciprocal(stats[:, 16:18], sm).then_inc(q["recip"], 1)
                    dve.wait_ge(q["recip"], j * 8 + (n + 1))
                    dve.tensor_scalar(stats[:, 18:19], stats[:, 17:18], lam[:, 8 + l:9 + l], None, ALU.mult
                                      ).then_inc(q["recip"], 1)
                    dve.wait_ge(q["recip"], j * 8 + (n + 2))
                    dve.tensor_scalar(d_s[t1][:], d_s[t1][:], stats[:, 18:19], None, ALU.mult
                                      ).then_inc(q["probs"], 1)
                    dve.wait_ge(q["probs"], BEGUN + j * 8 + (n + 1))
                    dve.scalar_tensor_tensor(out=d_s[t0][:], in0=d_s[t0][:], scalar=stats[:, 16:17],
                                             in1=d_s[t1][:], op0=ALU.mult, op1=ALU.subtract
                                             ).then_inc(q["probs"], 1)

                def take_out(j):
                    dve.wait_ge(q["summed"], BEGUN + j + (4 * l + 1))
                    dve.tensor_copy(proj1[:, dyn(j), :], row(bank(2))).then_inc(q["evacuated"], 1)

                def head(j, first):
                    dve.wait_ge(q["scored"], BEGUN + j * 8 + 32 * l)
                    dve.tensor_copy(row(d_k[:]), proj1[:, bass.ds(j + 4, 1), :]).then_inc(q["staged_dve"], 1)
                    dve.wait_ge(q["v_turned"], BEGUN + j + 4 * l)
                    dve.tensor_copy(row(d_v[:]), proj1[:, bass.ds(j + 20, 1), :]).then_inc(q["staged_dve"], 1)
                    if not first:
                        probs(j - 1, 3)
                    bias(j, 0)
                    bias(j, 1)
                    probs(j, 0)
                    if not first:
                        take_out(j - 1)
                    bias(j, 2)
                    probs(j, 1)
                    bias(j, 3)
                    probs(j, 2)

                head(0, True)
                with dve.Fori(1, 4) as j:
                    head(j, False)
                probs(3, 3)
                take_out(3)

            def fin1(ph):
                l = ph["layer"]

                def odd_lo(k):
                    dve.wait_ge(h_hi_ready, KT * ph["h0"] + k + 1)
                    dve.tensor_tensor(h_lo[:, k, 0:S], proj1[:, 8 + k if k < 4 else k - 4, :],
                                      h_hi[:, k, 0:S].bitcast(F32), ALU.subtract).then_inc(h_odd, 1)

                for n in range(8):
                    tile = proj1[:, 8 + n if n < 4 else n - 4, :]
                    gain = col("g_ret", l) if n < 4 else lam[:, 10 + l:11 + l]
                    dve.wait_ge(f_std, 8 * l + n + 1)
                    dve.reciprocal(f_r[n % 2][:], f_r[n % 2][:]).then_inc(f_recip, 1)
                    dve.wait_ge(f_recip, 8 * l + n + 1)
                    dve.scalar_tensor_tensor(out=tile, in0=tile, scalar=gain, in1=f_r[n % 2][:],
                                             op0=ALU.mult, op1=ALU.mult).then_inc(f_y_ready, 1)
                    if n < 4:
                        dve.wait_ge(f_y_ready, 12 * l + _f_y(n) - 1)
                        dve.tensor_tensor(tile, tile, proj1[:, 24 + n, :], ALU.mult).then_inc(f_y_ready, 1)
                    if n in (5, 7):
                        odd_lo(n - 4)
                odd_lo(5)
                odd_lo(7)

            def fin2(ph):
                for n in range(1, 8, 2):
                    dve.wait_ge(h_hi_ready, KT * ph["h0"] + n + 1)
                    dve.tensor_tensor(h_lo[:, n, 0:ph["T"]], proj[:, n, 0:ph["T"]],
                                      h_hi[:, n, 0:ph["T"]].bitcast(F32), ALU.subtract).then_inc(h_odd, 1)

            def na(ph):
                q = sems["n"]
                for hd in range(2):
                    for kind in range(3):
                        last = dve.memset(n_bias[:, hd, kind, 2 * P:4 * P], 0.0)
                        last.then_inc(q["mask_arg"], 1)
                dve.wait_ge(q["mask_arg"], BEGUN + 6)

                def pair(j, first):
                    dve.wait_ge(q["scored"], BEGUN + j * 12)
                    dve.tensor_copy(row(n_k[:]), proj[:, bass.ds(j + 8, 1), :]).then_inc(q["staged_dve"], 1)
                    dve.wait_ge(q["v_turned"], BEGUN + j)
                    dve.tensor_copy(row(n_v[:]), proj[:, bass.ds(j + 16, 1), :]).then_inc(q["staged_dve"], 1)

                    def bias(t):
                        hd, b = divmod(t, 6)
                        w = S if b < 4 else C
                        table = n_bias[:, hd, MASK_KIND[b], :] if b < 4 else n_bias[:, 0, 0, 2 * P:4 * P]
                        dve.wait_ge(q["bias"], j * 6 + (3 * hd + 3))
                        dve.wait_ge(q["scored"], BEGUN + j * 12 + (t + 1))
                        if t >= 3:
                            dve.wait_ge(q["turned"], BEGUN + j * 12 + (t - 2))
                        else:
                            dve.wait_ge(q["turned"], BEGUN + j * 12)
                        dve.memset(pace[:, 2:3], 0.0)
                        dve.tensor_tensor_reduce(n_s[t % 3][:, 0:w], bank(4 + t % 2, w), table, 1.0, NEG,
                                                 ALU.add, ALU.max, stats[:, t % 3:t % 3 + 1]).then_inc(q["biased"], 1)
                        dve.wait_ge(q["biased"], BEGUN + j * 12 + (t + 1))
                        dve.tensor_scalar(stats[:, 3 + t % 3:4 + t % 3], stats[:, t % 3:t % 3 + 1], -1.0, None,
                                          ALU.mult).then_inc(q["negmax"], 1)

                    def probs(t):
                        w = S if t % 6 < 4 else C
                        dve.wait_ge(q["exped"], j * 12 + (t + 1))
                        dve.reciprocal(stats[:, 9 + t % 3:10 + t % 3], stats[:, 6 + t % 3:7 + t % 3]
                                       ).then_inc(q["recip"], 1)
                        dve.wait_ge(q["recip"], j * 12 + (t + 1))
                        dve.tensor_scalar(n_s[t % 3][:, 0:w], n_s[t % 3][:, 0:w], stats[:, 9 + t % 3:10 + t % 3],
                                          None, ALU.mult).then_inc(q["probs"], 1)

                    for t in range(13):
                        if t == 2 and not first:
                            evacuate(j - 1, 1)
                        if t == 9:
                            evacuate(j, 0)
                        if t < 12:
                            bias(t)
                        if t >= 1:
                            probs(t - 1)

                def evacuate(j, hd):
                    half = slice(HD * hd, HD * hd + HD)
                    dve.wait_ge(q["summed"], BEGUN + j * 12 + (6 * hd + 6))
                    dve.tensor_copy(
                        proj[half, dyn(j), 0:S].rearrange("p a (r b c) -> p (a b) r c", b=8, c=8),
                        bank(2 + 4 * hd)[half, :].rearrange("p (b r c) -> p b r c", b=8, c=8)
                        ).then_inc(q["evacuated"], 1)
                    dve.tensor_copy(proj[half, dyn(j), S:T2], row(bank(3 + 4 * hd)[half, 0:C])
                                    ).then_inc(q["evacuated"], 1)

                pair(0, True)
                with dve.Fori(1, 8) as j:
                    pair(j, False)
                evacuate(7, 1)

            def swa(ph):
                q = sems["s"]
                dve.wait_ge(tab["swa"], 48)
                for n, tile in enumerate(ROPE_TILES):
                    t1 = s_t1[n % 2]
                    dve.wait_ge(rope_mm, n + 1)
                    if n >= 2:
                        dve.wait_ge(rope_out, n - 1)
                    dve.tensor_tensor(t1[:], bank(6 + n % 2), s_sin[:], ALU.mult).then_inc(rope_a, 1)
                    dve.wait_ge(rope_a, n + 1)
                    dve.wait_ge(rope_b, n + 1)
                    dve.tensor_tensor(proj[:, tile, 0:S], t1[:], s_t2[n % 2][:], ALU.add).then_inc(rope_out, 1)
                for kv in range(2):
                    def heads(g, first):
                        n = g * 8 + 32 * kv

                        def width(t):
                            return (5 if 0 < t % 4 < 3 else 4) * P

                        def bias(t):
                            hd, b = divmod(t, 4)
                            w, s = width(t), s_s[t % 3]
                            frm = (P, 0, 0, 5 * P)[b]
                            sink = dcol("sink", g * 2 + (8 * kv + hd))
                            dve.wait_ge(q["scored"], BEGUN + n + (t + 1))
                            dve.wait_ge(q["turned"], BEGUN + n + max(t - 2, 0))
                            dve.memset(pace[:, 2:3], 0.0)
                            dve.tensor_tensor_reduce(s[:, 0:w], sums[t % 2][:, 0:w], s_band[:, frm:frm + w], 1.0, NEG,
                                                     ALU.add, ALU.max, stats[:, t % 3:t % 3 + 1]
                                                     ).then_inc(q["biased"], 1)
                            dve.tensor_copy(s[:, w:w + 1], sink).then_inc(q["mask_arg"], 1)
                            dve.wait_ge(q["biased"], BEGUN + n + (t + 1))
                            dve.wait_ge(q["mask_arg"], BEGUN + n + (t + 1))
                            dve.tensor_scalar(stats[:, 3 + t % 3:4 + t % 3], stats[:, t % 3:t % 3 + 1], sink, -1.0,
                                              ALU.max, ALU.mult).then_inc(q["negmax"], 1)

                        def probs(t):
                            w = width(t)
                            dve.wait_ge(q["exped"], n + (t + 1))
                            dve.reciprocal(stats[:, 9 + t % 3:10 + t % 3], stats[:, 6 + t % 3:7 + t % 3]
                                           ).then_inc(q["recip"], 1)
                            dve.wait_ge(q["recip"], n + (t + 1))
                            dve.tensor_scalar(s_s[t % 3][:, 0:w], s_s[t % 3][:, 0:w], stats[:, 9 + t % 3:10 + t % 3],
                                              None, ALU.mult).then_inc(q["probs"], 1)

                        for t in range(9):
                            if t == 2 and not first:
                                evacuate(g + (4 * kv - 1), 1)
                            if t == 7:
                                evacuate(g + 4 * kv, 0)
                            if t < 8:
                                bias(t)
                            if t >= 1:
                                probs(t - 1)

                    def evacuate(tile, hd):
                        half = slice(HD * hd, HD * hd + HD)
                        dve.wait_ge(q["summed"], BEGUN + tile * 8 + (4 * hd + 4))
                        dve.tensor_copy(proj[half, dyn(tile), 0:S], row(bank(2 + hd)[half, :])
                                        ).then_inc(q["evacuated"], 1)

                    if kv == 0:
                        heads(0, True)
                    with dve.Fori(1 - kv, 4) as g:
                        heads(g, False)
                evacuate(7, 1)

            for ph in phases:
                kind = ph["kind"]
                if kind == "norm":
                    if ph["unit0"] == MOD_UNITS:
                        modulation_end()
                    norm(ph)
                    if ph["norm0"] == 0:
                        setup()
                elif kind == "normed":
                    head_norm(ph)
                elif kind == "proj":
                    modulation_pairs(ph)
                elif kind == "resid":
                    resid(ph)
                elif kind == "glu":
                    glu(ph)
                elif kind == "conv":
                    conv(ph)
                elif kind == "retention":
                    dve.wait_ge(acc_free, ph["unit0"])
                    dve.wait_ge(mm_done, ph["unit0"])
                    retention(ph)
                elif kind == "diff":
                    diff(ph)
                elif kind == "fin1":
                    fin1(ph)
                elif kind == "na":
                    dve.wait_ge(acc_free, ph["unit0"])
                    dve.wait_ge(mm_done, ph["unit0"])
                    na(ph)
                elif kind == "swa":
                    dve.wait_ge(acc_free, ph["unit0"])
                    dve.wait_ge(mm_done, ph["unit0"])
                    swa(ph)
                elif kind == "fin2":
                    fin2(ph)


def constants():
    p = np.arange(P)[:, None]
    j = np.arange(STRIP)[None, :]
    dist = (j - (S - P) - p).astype(np.float32)
    strips = np.stack([np.maximum(dist, 0), np.maximum(-dist, 0), np.abs(dist)])
    mats = np.zeros((P, 5, P), np.float32)
    mats[:, IDENT] = np.eye(P)
    mats[:, MEAN64] = np.kron(np.eye(2), np.full((HD, HD), 1 / HD))
    mats[:, MEAN128] = 1 / P
    mats[:, MEAN1024] = 1 / D
    rot = np.zeros((P, P), np.float32)
    for h in range(2):
        for i in range(HD // 2):
            rot[h * HD + HD // 2 + i, h * HD + i] = -1.0
            rot[h * HD + i, h * HD + HD // 2 + i] = 1.0
    mats[:, ROT] = rot
    mask = np.zeros((P, 3, 4, ROWS, 8), np.float32)
    qc = np.arange(P) // HD * 8 + np.arange(P) % 8
    for kind, b in enumerate((0, 1, 3)):
        c = 16 * b + qc
        first = np.clip(c - 8, 0, GRID - 16)
        key = KEY_COL[b] + np.arange(32).reshape(4, 8)
        ok = (key[None] >= first[:, None, None]) & (key[None] < first[:, None, None] + 16)
        mask[:, kind] = np.where(ok, 0.0, NEG)[:, :, None, :]
    k = np.arange(P)[None, :]
    before = np.where(k >= p, 0.0, NEG)
    after = np.where(k <= p, 0.0, NEG)
    zero = np.zeros((P, P))
    band = np.concatenate([before, zero, after, zero, zero, before, zero, zero, zero], 1)
    t = np.arange(S)
    inv = (10000.0 ** (-np.arange(HD // 4, dtype=np.float32) / (HD // 4))).astype(np.float32)
    ang = np.concatenate([(t // GRID).astype(np.float32)[:, None] * inv,
                          (t % GRID).astype(np.float32)[:, None] * inv], -1).astype(np.float32)
    rope = np.stack([np.tile(f(ang).T, (4, 1)) for f in (np.cos, np.sin)])
    f32 = lambda a: np.ascontiguousarray(a, dtype=np.float32)
    return dict(dist=f32(strips), mats=f32(mats), na_mask=f32(mask.reshape(P, 3, 2 * P)),
                band=f32(band), rope=f32(rope))


def lay_out(i):
    def units(w):
        L, K, N = w.shape
        return w.reshape(L, K // P, P, N // P, P).transpose(0, 3, 2, 1, 4).reshape(L * N // P, P, K)

    def cols(v):
        return v.reshape(-1, P).T

    def rep(v):
        return np.broadcast_to(v.reshape(1, -1), (P, v.size))

    def head(v):
        return np.concatenate([v, v])[:, None]

    x, ctx = i["x"][0], i["ctx_2"][0]
    o = {}
    o["x"] = x.T.reshape(KT, P, S).transpose(1, 0, 2)
    o["ctx"] = ctx.T.reshape(KT, P, C).transpose(1, 0, 2)
    w = i["w_in"].reshape(DEPTH, D, 7, 512)
    o["w_in"] = units(np.concatenate([w[:, :, n] for n in (4, 5, 0, 1, 2, 6, 3)], 2))
    o["w_out"] = units(i["w_out"])
    gu = np.stack([i["w_gate"].reshape(DEPTH, D, FT, P), i["w_up"].reshape(DEPTH, D, FT, P)], 3)
    o["w_gu"] = units(gu.reshape(DEPTH, D, 2 * D_FF))
    o["w_down"] = units(i["w_down"].reshape(DEPTH * 2, D_FF // 2, D))
    o["w_mod"] = i["w_mod_2"].transpose(0, 2, 1).reshape(-1, P, D)
    o["c"] = rep(np.stack([i["c_2"][0], i["c_ctx_2"]])).reshape(P, 2, D)
    o["na_qkv"] = units(i["na_w_qkv_2"])
    o["na_o"] = units(i["na_w_o_2"])
    def pair_heads(a, axis):
        shape = a.shape
        a = np.moveaxis(a, axis, 0).reshape(2, 2, 4, HD, -1).transpose(0, 2, 1, 3, 4)
        return np.moveaxis(a.reshape((D,) + tuple(np.delete(shape, axis))), 0, axis)
    sw = i["swa_w_qkv_2"]
    o["swa_qkv"] = units(np.concatenate([pair_heads(sw[:, :, :D], 2), sw[:, :, D:]], 2))
    o["swa_o"] = units(pair_heads(i["swa_w_o_2"], 1))
    up = i["ffn_w_up_2"].reshape(DEPTH, D, 2, FT, P).transpose(0, 1, 3, 2, 4)
    o["w_up2"] = units(up.reshape(DEPTH, D, 2 * D_FF))
    o["w_down2"] = units(i["ffn_w_down_2"].reshape(DEPTH * 2, D_FF // 2, D))
    o["lam"] = rep(np.stack([i[n] for n in ("lambda_q1", "lambda_k1", "lambda_q2", "lambda_k2")], 1)
                   ).reshape(P, DEPTH * 4, HD)
    pad = np.pad(i["na_rpb_2"][0], ((0, 0), (0, 0), (16, 16)))
    r, c, kr, u = np.ogrid[0:ROWS, 0:16, 0:ROWS, 0:48]
    e = pad[:, kr - r + ROWS - 1, u - c + 15]
    e = e.reshape(16, ROWS, 2, 8, ROWS, 48).transpose(0, 2, 1, 3, 4, 5)
    o["rpb"] = e.reshape(8, 2, P, ROWS * 48).transpose(0, 2, 1, 3)
    conv = np.concatenate([i["ffn_conv_w_2"], i["ffn_conv_b_2"][:, None]], 1)
    conv = conv.reshape(DEPTH, 4, 2, FT, P).transpose(4, 0, 3, 2, 1)
    two = lambda v: np.repeat(cols(v), 2, 1)
    heads = lambda v: v.reshape(2, 2, 4).transpose(0, 2, 1)
    s = {
        "g_attn": cols(i["attn_norm_g"]), "g_ffn": cols(i["ffn_norm_g"]),
        "g_ret": np.concatenate([head(v) for v in i["ret_norm_g"]], 1), "g_diff": i["diff_norm_g"].T,
        "g_dqk": np.concatenate([np.repeat(head(i[n][l]), 4, 1) for l in range(DEPTH)
                                 for n in ("dq_norm_g", "dk_norm_g")], 1),
        "g_na": np.concatenate([np.repeat(head(i[n][0]), 8, 1) for n in ("na_g_q_2", "na_g_k_2")], 1),
        "g_swa": np.concatenate([np.repeat(head(i["swa_g_q_2"][0]), 8, 1),
                                 np.repeat(head(i["swa_g_k_2"][0]), 2, 1)], 1),
        "decay": rep(np.stack([i["ret_decay_fwd"], i["ret_decay_bwd"]], 1)),
        "slope": rep(-(2.0 ** (-8.0 * np.arange(1, 5) / 4)).astype(np.float32)),
        "sink": rep(heads(i["swa_sink_2"][0])), "conv": conv.reshape(P, -1),
        "g2_attn": two(i["g_attn_2"]), "g2_ffn": two(i["g_ffn_2"]), "b_mod": two(i["b_mod_2"]),
    }
    for n, (_, width) in SMALL.items():
        assert s[n].shape == (P, width), (n, s[n].shape, width)
    o["small"] = np.concatenate([s[n] for n in SMALL], 1)
    return o


def kernel(**inputs):
    import concourse.bacc as bacc
    from concourse.bass_utils import run_bass_kernel_spmd

    arrays = lay_out({n: np.asarray(a) for n, a in inputs.items()})
    arrays.update(constants())
    arrays = {n + "_dram": np.ascontiguousarray(a) for n, a in arrays.items()}
    nc = bacc.Bacc("TRN2", target_bir_lowering=False, num_devices=1)
    d = {n[:-5]: nc.dram_tensor(n, a.shape, mybir.dt.from_np(a.dtype), kind="ExternalInput").ap()
         for n, a in arrays.items()}
    out = nc.dram_tensor("out_dram", (P, KT, S), F32, kind="ExternalOutput").ap()
    build(nc, d, out)
    r = run_bass_kernel_spmd(nc, [arrays], core_ids=[0])
    got = r.results[0]["out_dram"]
    return np.ascontiguousarray(got.transpose(2, 1, 0)).reshape(1, S, D)
```

```python
from contextlib import ExitStack

import concourse.bass as bass
from concourse import mybir
import numpy as np

P = 128
D = 1024
KT = D // P
S = 512
C = 256
T2 = S + C
DEPTH = 2
HD = 64
D_FF = 2816
FT = D_FF // P
FH = FT // 2
GRID = 64
ROWS = S // GRID
EPS = 1e-6
NEG = -1e30
UNIT = FH * P
STRIP = S + S - P
CTX_AT = S + 2
ACTW = CTX_AT + C

ALU = mybir.AluOpType
ACT = mybir.ActivationFunctionType
F32 = mybir.dt.float32
F32R = mybir.dt.float32r
AX_X = mybir.AxisListType.X

SMALL = {}


def _small(name, width):
    SMALL[name] = (sum(w for _, w in SMALL.values()), width)


for _name, _width in (
    ("g_attn", DEPTH * KT), ("g_ffn", DEPTH * KT), ("g_ret", DEPTH), ("g_diff", DEPTH),
    ("g_dqk", DEPTH * 8), ("g_na", 16), ("g_swa", 10), ("decay", DEPTH * 16), ("slope", 4),
    ("sink", 16), ("conv", DEPTH * 2 * FT * 4), ("g2_attn", DEPTH * KT * 2), ("g2_ffn", DEPTH * KT * 2),
    ("b_mod", DEPTH * 48 * 2),
):
    _small(_name, _width)
NSMALL = sum(w for _, w in SMALL.values())

IDENT, MEAN64, MEAN128, MEAN1024, ROT = range(5)

MOD_UNITS = 2 * DEPTH * 48

BEGUN = 1

ROPE_TILES = 10
ROPE_AT = {3: 0, 4: 1, 9: 2, 10: 3, 12: 4, 13: 5, 15: 6}

KEY_COL = [0, 8, 24, 32]
MASK_KIND = [0, 1, 1, 2]


POOL_TILES = {"norm": (2, 4, 6), "fin1": (0, 1, 2, 4, 6), "fin2": (0, 2, 4, 6)}


def lo_part(ph, k):
    tiles = POOL_TILES[ph["kind"]]
    if k in tiles:
        return True, ph["h_pool0"] + tiles.index(k) + 1
    return False, ph["h_dve0"] + [t for t in range(KT) if t not in tiles].index(k) + 1


def schedule():
    phases, count = [], {"unit": 0, "norm": 0, "hn": 0, "glu": 0, "conv": 0, "h": 0, "h_pool": 0, "h_dve": 0}

    def add(kind, **kw):
        kw.update(kind=kind, **{k + "0": v for k, v in count.items()})
        phases.append(kw)

    def split_h():
        count["h"] += 1
        count["h_pool"] += len(POOL_TILES[phases[-1]["kind"]])
        count["h_dve"] += KT - len(POOL_TILES[phases[-1]["kind"]])

    def norm(block, layer, which, T):
        add("norm", block=block, layer=layer, which=which, T=T)
        count["norm"] += 1
        split_h()

    def proj(weight, first, units, T, tile0, func="copy"):
        add("proj", weight=weight, first=first, units=units, T=T, tile0=tile0, func=func, K=KT)
        count["unit"] += units

    def normed(weight, first, units, T, tile0, gains):
        add("normed", weight=weight, first=first, units=units, T=T, tile0=tile0, gains=gains, K=KT)
        count["unit"] += units
        count["hn"] += units

    def resid(weight, first, T, gate, K):
        add("resid", weight=weight, first=first, units=KT, T=T, gate=gate, K=K)
        count["unit"] += KT

    def hidden(kind, weight, first, T, layer, half):
        add(kind, weight=weight, first=first, units=2 * FH, T=T, layer=layer, half=half, K=KT)
        count["unit"] += 2 * FH
        count[kind] += FH

    for l in range(DEPTH):
        norm(1, l, "attn", S)
        normed("w_in", 28 * l, 8, S, 0, ("g_dqk", 8 * l))
        proj("w_in", 28 * l + 8, 16, S, 8)
        proj("w_in", 28 * l + 24, 4, S, 24, "silu")
        add("retention", layer=l)
        add("diff", layer=l)
        add("fin1", layer=l)
        split_h()
        resid("w_out", 8 * l, S, None, KT)
        norm(1, l, "ffn", S)
        for half in range(2):
            hidden("glu", "w_gu", 44 * l + 22 * half, S, l, half)
            resid("w_down", 16 * l + 8 * half, S, None, FH)
    norm(2, 0, "attn", T2)
    normed("na_qkv", 0, 16, T2, 0, ("g_na", 0))
    proj("na_qkv", 16, 8, T2, 16)
    add("na")
    add("fin2", T=T2)
    split_h()
    resid("na_o", 0, T2, (0, 2), KT)
    norm(2, 0, "ffn", T2)
    for half in range(2):
        hidden("conv", "w_up2", 22 * half, T2, 0, half)
        resid("w_down2", 8 * half, T2, (0, 5), FH)
    norm(2, 1, "attn", T2)
    normed("swa_qkv", 0, 8, S, 0, ("g_swa", 0))
    normed("swa_qkv", 8, 2, T2, 8, ("g_swa", 8))
    proj("swa_qkv", 10, 2, T2, 10)
    add("swa")
    add("fin2", T=S)
    split_h()
    resid("swa_o", 0, S, (1, 2), KT)
    norm(2, 1, "ffn", S)
    for half in range(2):
        hidden("conv", "w_up2", 44 + 22 * half, S, 1, half)
        resid("w_down2", 16 + 8 * half, S, (1, 5), FH)
    add("end")
    for ph, after in zip(phases, phases[1:]):
        after["fresh"] = ph if "weight" in after and ph["kind"] in POOL_TILES else None
        ph["norm_T"] = after["T"] if after["kind"] == "norm" else None
    return phases


def ahead(phases):
    out, moved = [], None
    for n, ph in enumerate(phases):
        if "weight" in ph:
            out.append(dict(ph, pairs=(1, ph["units"] // 2)) if ph is moved else ph)
            moved = None
        else:
            if moved is None and ph["kind"] != "end":
                moved = next(p for p in phases[n:] if "weight" in p)
                out.append(dict(moved, pairs=(0, 1)))
            out.append(ph)
    return out


def segments(T, at=S):
    segs = [(0, 0, S, 0)]
    if T == T2:
        segs.append((S, at, C, 1))
    return segs


def _f_y(n):
    return 2 * (n + 1) if n < 4 else 8 + (n - 3)


def build(nc, d, out):
    phases = schedule()
    total_units = phases[-1]["unit0"]

    with ExitStack() as stack:
        def sem(name):
            return stack.enter_context(nc.semaphore(name))

        top = [nc.sbuf_base]
        names = [0]

        def at(offset, shape, dt=F32, name="t"):
            names[0] += 1
            return nc.alloc_sbuf_tensor_at(f"{name}{names[0]}", shape, dt, offset=offset)

        def nbytes(shape):
            n = 4
            for s in shape[1:]:
                n *= s
            return (n + 31) // 32 * 32

        def sb(name, shape, dt=F32):
            t = at(top[0], shape, dt, name)
            top[0] += nbytes(shape)
            return t

        class Area:

            def __init__(self, offset, size):
                self.offset, self.end = offset, offset + size

            def __call__(self, name, shape, dt=F32):
                t = at(self.offset, shape, dt, name)
                self.offset += nbytes(shape)
                assert self.offset <= self.end, (name, self.offset - self.end)
                return t

        top[0] = (top[0] + 31) // 32 * 32
        base = top[0]
        xT = sb("xT", [P, KT, T2])
        h_at = top[0]
        h_hi = sb("h_hi", [P, KT, T2], F32R)
        h_lo = sb("h_lo", [P, KT, T2], F32R)
        h_size = top[0] - h_at
        w_raw = [sb(f"w_raw{i}", [P, UNIT]) for i in range(2)]
        w_hi = [sb(f"w_hi{i}", [P, UNIT], F32R) for i in range(2)]
        w_lo = [sb(f"w_lo{i}", [P, UNIT], F32R) for i in range(2)]
        small = sb("small", [P, NSMALL])
        mats = sb("mats", [P, 5, P])
        mod = sb("mod", [P, DEPTH, 6, KT, 2])
        gs = sb("gs", [P, DEPTH, 2, KT, 2])
        mod_sum = sb("mod_sum", [P, 2])
        zero1 = sb("zero1", [P, 1])
        eps1 = sb("eps1", [P, 1])
        lgam = sb("lgam", [P, DEPTH * 16 + 2])
        lam = sb("lam", [P, 16])
        stats = sb("stats", [P, 24])
        pace = sb("pace", [P, 4])
        wide_at = top[0]
        wide_size = nbytes([P, 24, T2])
        top[0] += wide_size
        temp_at = top[0]
        temp_size = 4 * nbytes([P, 4 + ACTW])
        top[0] += temp_size
        assert top[0] <= nc.sbuf_usable_end, (top[0], nc.sbuf_usable_end)

        wide = Area(wide_at, wide_size)
        proj = wide("proj", [P, 24, T2])
        proj1 = at(wide_at, [P, 28, S], F32, "proj1")
        wide = Area(wide_at, wide_size)
        a_hi = wide("a_hi", [P, FH, ACTW], F32R)
        a_lo = wide("a_lo", [P, FH, ACTW], F32R)
        wide = Area(wide_at, wide_size)
        b_hi = wide("b_hi", [P, FH, S], F32R)
        b_lo = wide("b_lo", [P, FH, S], F32R)
        wide = Area(wide_at, wide_size)
        n_rstd = wide("n_rstd", [P, T2])
        n_xn = [wide(f"n_xn{i}", [P, T2]) for i in range(4)]
        lam_vec = wide("lam_vec", [P, DEPTH * 4, HD])
        lam_prod = wide("lam_prod", [P, HD])

        wide = Area(wide_at + nbytes([P, 28, S]), wide_size - nbytes([P, 28, S]))
        mod_w = wide("mod_w", [P, D])
        mod_junk = wide("mod_junk", [P, D])
        silu_c = wide("silu_c", [P, 2, D])

        temp = Area(temp_at, temp_size)
        u_pad = [temp(f"u_pad{i}", [P, 4 + ACTW]) for i in range(2)]
        conv_y = [temp(f"conv_y{i}", [P, ACTW]) for i in range(2)]
        temp = Area(temp_at, temp_size)
        n_sq = [temp(f"n_sq{i}", [P, T2]) for i in range(2)]
        n_sum_sq = temp("n_sum_sq", [P, T2])
        temp = Area(temp_at, temp_size)
        hn_sq = [temp(f"hn_sq{i}", [P, T2]) for i in range(2)]
        hn_r = [temp(f"hn_r{i}", [P, T2]) for i in range(2)]
        temp = Area(temp_at, temp_size)
        d_s_more = [temp(f"d_s{i}", [P, S]) for i in (6, 7)]
        f_sq = [temp(f"f_sq{i}", [P, S]) for i in range(2)]
        f_r = [temp(f"f_r{i}", [P, S]) for i in range(2)]
        temp = Area(temp_at, temp_size)
        r_dpos, r_dneg = temp("r_dpos", [P, STRIP]), temp("r_dneg", [P, STRIP])
        temp = Area(temp_at, temp_size)
        glu_g = temp("glu_g", [P, S])
        glu_a = temp("glu_a", [P, S])

        area = Area(h_at, h_size)
        r_q, r_k, r_v = (area(f"r_{n}", [P, S]) for n in "qkv")
        r_vs = area("r_vs", [P, 4, P])
        r_tmp = area("r_tmp", [P, STRIP])
        r_mask = [area(f"r_mask{i}", [P, STRIP]) for i in range(2)]
        r_sc = [area(f"r_sc{i}", [P, S]) for i in range(3)]
        d_dist = at(h_at + h_size - nbytes([P, STRIP]), [P, STRIP], name="d_dist")
        area = Area(h_at, h_size)
        d_q, d_k, d_v = (area(f"d_{n}", [P, S]) for n in "qkv")
        d_vs = area("d_vs", [P, 4, P])
        d_bias = area("d_bias", [P, STRIP])
        d_s = [area(f"d_s{i}", [P, S]) for i in range(6)] + d_s_more
        d_aT = area("d_aT", [P, 4, S])
        area = Area(h_at, h_size)
        n_q, n_k, n_v = (area(f"n_{n}", [P, T2]) for n in "qkv")
        n_vs = area("n_vs", [P, 9, P])
        n_s = [area(f"n_s{i}", [P, S]) for i in range(3)]
        n_pT = [area(f"n_pT{i}", [P, S]) for i in range(2)]
        n_bias = area("n_bias", [P, 2, 3, S])
        n_rpb = area("n_rpb", [P, 2, ROWS * 48])
        n_mask = area("n_mask", [P, 3, 2 * P])
        area = Area(h_at, h_size)
        s_q = area("s_q", [P, S])
        s_vs = area("s_vs", [P, 6, P])
        s_s = [area(f"s_s{i}", [P, 5 * P + 8]) for i in range(3)]
        s_pT = [area(f"s_pT{i}", [P, 5 * P]) for i in range(2)]
        s_band = area("s_band", [P, 9 * P])
        wide = Area(wide_at + nbytes([P, 12, T2]), wide_size - nbytes([P, 12, T2]))
        s_cos, s_sin = wide("s_cos", [P, S]), wide("s_sin", [P, S])
        s_t1, s_t2 = ([wide(f"s_t{n}{i}", [P, S]) for i in range(2)] for n in (1, 2))

        ps = stack.enter_context(nc.psum_tensor("ps", [P, 8 * 512], F32))
        acc = [ps[:, 1024 * i:1024 * i + 1024] for i in range(2)]
        sums = [ps[:, 2048 + 1024 * i:3072 + 1024 * i] for i in range(2)]

        def bank(i, n=512):
            return ps[:, 512 * i:512 * i + n]

        loaded = sem("loaded")
        ready = sem("ready")
        w_loaded = [sem(f"w_loaded{i}") for i in range(2)]
        w_hi_ready = sem("w_hi_ready")
        w_lo_ready = sem("w_lo_ready")
        mm_done = sem("mm_done")
        acc_free = sem("acc_free")
        mod_loaded, mod_step, mod_kept = sem("mod_loaded"), sem("mod_step"), sem("mod_kept")
        silu_c_ready, mod_ready = sem("silu_c_ready"), sem("mod_ready")
        lam_step, lam_exp = sem("lam_step"), sem("lam_exp")
        n_sq_ready, n_sum, n_std = sem("n_sq_ready"), sem("n_sum"), sem("n_std")
        n_recip, n_xn_ready, n_scaled, n_added = sem("n_recip"), sem("n_xn_ready"), sem("n_scaled"), sem("n_added")
        h_hi_ready = sem("h_hi_ready")
        h_pool, h_dve = sem("h_pool"), sem("h_dve")
        x_in = [sem(f"x_in{i}") for i in range(4)]
        constants_in, table_in = sem("constants_in"), sem("table_in")
        hn_sq_ready, hn_sum, hn_std = sem("hn_sq_ready"), sem("hn_sum"), sem("hn_std")
        hn_recip, hn_out = sem("hn_recip"), sem("hn_out")
        a_lo_ready = sem("a_lo_ready")
        conv_step, conv_gate, conv_hi = sem("conv_step"), sem("conv_gate"), sem("conv_hi")
        conv_zero, glu_hi = sem("conv_zero"), sem("glu_hi")
        f_sq_ready, f_sum, f_std, f_recip = sem("f_sq_ready"), sem("f_sum"), sem("f_std"), sem("f_recip")
        f_y_ready = sem("f_y_ready")
        tab = {k: sem("tab_" + k) for k in ("retention", "diff", "na", "swa", "rope")}
        sems = {}
        for k, stage in (("r", "retention"), ("d", "diff"), ("n", "neighbour"), ("s", "sliding")):
            sems[k] = {n: sem(f"{stage}_{n}") for n in (
                "staged_act", "staged_dve", "v_turned", "v_kept", "scored", "biased", "negmax",
                "exped", "recip", "probs", "turned", "kept", "summed", "evacuated", "bias", "mask_arg")}
        rope_mm, rope_a, rope_b, rope_out = sem("rope_mm"), sem("rope_a"), sem("rope_b"), sem("rope_out")
        rpb_loaded, ctx_in = sem("rpb_loaded"), sem("ctx_in")
        stored = sem("stored")

        block = stack.enter_context(nc.Block())

        def begin(eng, names, others=()):
            for k in sems:
                for n in names:
                    eng.sem_inc(sems[k][n], BEGUN)
            for s_ in others:
                eng.sem_inc(s_, BEGUN)

        def col(name, i=0, n=1):
            return small[:, SMALL[name][0] + i:SMALL[name][0] + i + n]

        def dcol(name, i):
            return small[:, bass.ds(SMALL[name][0] + i, 1)]

        def wait_lo(eng, ph, k):
            by_pool, count = lo_part(ph, k)
            eng.wait_ge(h_pool if by_pool else h_dve, count)

        def pairs(eng, ph, body, peel=False):
            begin_, end = ph.get("pairs", (0, ph["units"] // 2))
            if begin_ == 0 and (ph["unit0"] == 0 or peel):
                body(0, ph["unit0"] == 0)
                begin_ = 1
            if end - begin_ == 1:
                body(begin_, False)
            elif end > begin_:
                with eng.Fori(begin_, end) as i:
                    body(i, False)

        def dyn(i):
            return bass.ds(i, 1)

        def by_columns(ap):
            return ap.rearrange("p a (b r c) -> p (a b) r c", b=8, c=8)

        def from_rows(ap):
            return ap.rearrange("p (r b c) -> p b r c", b=8, c=8)

        def mat(i):
            return mats[:, i, :]

        N_INPUTS = 16 * 2

        @block.sync
        def _(sp):
            sp.wait_ge(x_in[2], 16)

            def weights(ph):
                u0 = ph["unit0"]

                def body(i, first):
                    for par in range(2):
                        if not first:
                            sp.wait_ge(w_lo_ready, i * 2 + (u0 + par - 1))
                        sp.dma_start(w_raw[par][:, 0:ph["K"] * P].rearrange("p (a n) -> p a n", a=1),
                                     d[ph["weight"]][bass.ds(i * 2 + (ph["first"] + par), 1)].rearrange(
                                         "a p n -> p a n")).then_inc(w_loaded[par], 16)
                    if u0 < MOD_UNITS:
                        if not first:
                            sp.wait_ge(mod_step, i * 2 + u0)
                        sp.dma_start(mod_w[:].rearrange("p (a n) -> p a n", a=1),
                                     d["w_mod"][bass.ds(i + u0 // 2, 1)].rearrange("a p n -> p a n")
                                     ).then_inc(mod_loaded, 16)
                pairs(sp, ph, body)

            for ph in ahead(phases):
                if ph["kind"] == "proj" and ph["func"] == "silu":
                    sp.wait_ge(hn_out, ph["hn0"])
                    sp.dma_start(r_dpos[:], d["dist"][0]).then_inc(tab["retention"], 16)
                    sp.dma_start(r_dneg[:], d["dist"][1]).then_inc(tab["retention"], 16)
                if ph.get("weight") == "swa_qkv" and ph["first"] == 8:
                    sp.wait_ge(n_xn_ready, KT * ph["norm0"])
                    sp.dma_start(s_cos[:], d["rope"][0]).then_inc(tab["rope"], 16)
                    sp.dma_start(s_sin[:], d["rope"][1]).then_inc(tab["rope"], 16)
                if "weight" in ph:
                    weights(ph)
                elif ph["kind"] == "retention":
                    sp.wait_ge(mm_done, ph["unit0"])
                    sp.dma_start(d_dist[:], d["dist"][2]).then_inc(tab["diff"], 16)
                    if ph["layer"] == 0:
                        sp.dma_start(xT[:, :, S:T2], d["ctx"]).then_inc(ctx_in, 16)
                elif ph["kind"] == "na":
                    sp.wait_ge(mm_done, ph["unit0"])
                    sp.dma_start(n_mask[:], d["na_mask"]).then_inc(tab["na"], 16)
                    sp.dma_start(n_rpb[:], d["rpb"][0]).then_inc(rpb_loaded, 16)
                    with sp.Fori(1, 8) as j:
                        sp.wait_ge(sems["n"]["bias"], j * 6)
                        sp.dma_start(n_rpb[:].rearrange("p (a h) n -> p a h n", a=1),
                                     d["rpb"][bass.ds(j, 1)].rearrange("a p h n -> p a h n")
                                     ).then_inc(rpb_loaded, 16)
                elif ph["kind"] == "swa":
                    sp.wait_ge(mm_done, ph["unit0"])
                    sp.dma_start(s_band[:], d["band"]).then_inc(tab["swa"], 16)
            for k in range(KT):
                sp.wait_ge(acc_free, total_units - KT + k + 1)
                sp.dma_start(out[:, k, :], xT[:, k, 0:S]).then_inc(stored, 16)
            sp.wait_ge(stored, 16 * KT)

        @block.gpsimd
        def _(pool):
            def split(ph):
                u0, cols = ph["unit0"], ph["K"] * P

                def body(i, first):
                    for par in range(2):
                        pool.wait_ge(w_hi_ready, i * 2 + (u0 + par + 1))
                        pool.tensor_tensor(w_lo[par][:, 0:cols], w_raw[par][:, 0:cols],
                                           w_hi[par][:, 0:cols].bitcast(F32), ALU.subtract).then_inc(w_lo_ready, 1)
                pairs(pool, ph, body)

            def na_bias(ph):
                q = sems["n"]
                pool.wait_ge(tab["na"], 16)

                def tables(j, first):
                    pool.wait_ge(rpb_loaded, j * 16 + 16)
                    for hd in range(2):
                        if not first:
                            pool.wait_ge(q["biased"], BEGUN + j * 12 + (6 * hd + 4 - 12))
                        for kind, off in enumerate((16, 8, 0)):
                            strip = n_rpb[:, hd, :].rearrange("p (r u) -> p r u", u=48)
                            pool.tensor_tensor(
                                n_bias[:, hd, kind, 0:2 * P].rearrange("p (i r c) -> p i r c", i=4, c=8),
                                strip[:, :, off:off + 32].rearrange("p r (i c) -> p i r c", c=8),
                                n_mask[:, kind, :].rearrange("p (i r c) -> p i r c", i=4, c=8),
                                ALU.add).then_inc(q["bias"], 1)

                tables(0, True)
                with pool.Fori(1, 8) as j:
                    tables(j, False)

            def rope(ph):
                pool.wait_ge(tab["rope"], 32)
                for n in range(ROPE_TILES):
                    pool.wait_ge(hn_out, ph["hn0"] - ROPE_TILES + n + 1)
                    if n >= 2:
                        pool.wait_ge(rope_out, n - 1)
                    pool.tensor_tensor(s_t2[n % 2][:], proj[:, n, 0:S], s_cos[:], ALU.mult).then_inc(rope_b, 1)

            def lo_tiles(ph, source, T):
                for k in POOL_TILES[ph["kind"]]:
                    pool.wait_ge(h_hi_ready, 8 * ph["h0"] + k + 1)
                    pool.tensor_tensor(h_lo[:, k, 0:T], source(k), h_hi[:, k, 0:T].bitcast(F32), ALU.subtract
                                       ).then_inc(h_pool, 1)

            for ph in ahead(phases):
                if "weight" in ph:
                    split(ph)
                    if ph["kind"] == "proj" and ph["weight"] == "swa_qkv":
                        rope(ph)
                elif ph["kind"] == "norm":
                    lo_tiles(ph, lambda k: n_xn[k % 4][:, 0:ph["T"]], ph["T"])
                elif ph["kind"] == "fin1":
                    lo_tiles(ph, lambda k: proj1[:, 8 + k if k < 4 else k - 4, :], S)
                elif ph["kind"] == "fin2":
                    lo_tiles(ph, lambda k: proj[:, k, 0:ph["T"]], ph["T"])
                elif ph["kind"] == "na":
                    na_bias(ph)

        @block.tensor
        def _(pe):
            def tile_ready(ph, k):
                if ph["K"] == FH:
                    pe.wait_ge(a_lo_ready, BEGUN + ph["glu0"] + ph["conv0"] - FH + k + 1)
                elif ph["fresh"]:
                    wait_lo(pe, ph["fresh"], k)

            def unit(ph, i, par, first, beside=None):
                u0, K = ph["unit0"], ph["K"]
                hidden = ph["K"] == FH
                hi, lo = (h_hi, h_lo) if not hidden else (b_hi, b_lo) if u0 < MOD_UNITS else (a_hi, a_lo)
                segs = segments(ph["T"], CTX_AT if hidden else S)
                pe.wait_ge(w_lo_ready, i * 2 + (u0 + par + 1))
                if not first:
                    pe.wait_ge(acc_free, i * 2 + (u0 + par - 1))
                for k in range(K):
                    if isinstance(i, int) and i + par == 0:
                        tile_ready(ph, k)
                    for w, r, begin, end in ((w_hi, hi, k == 0, False), (w_hi, lo, False, False),
                                             (w_lo, hi, False, k == K - 1)):
                        for to, frm, n, _ in segs:
                            last = pe.matmul(acc[par][:, to:to + n], w[par][:, k * P:k * P + P],
                                             r[:, k, frm:frm + n], start=begin, stop=end)
                    if k == K - 1:
                        last.then_inc(mm_done, 1)
                    if beside is not None:
                        beside(K * par + k)

            def rotate(ph, n):
                pe.wait_ge(hn_out, ph["hn0"] - ROPE_TILES + n + 1)
                if n >= 2:
                    pe.wait_ge(rope_a, n - 1)
                else:
                    pe.wait_ge(hn_std, ph["hn0"])
                pe.matmul(bank(6 + n % 2), mat(ROT), proj[:, n, 0:S], start=True, stop=True).then_inc(rope_mm, 1)

            def units_beside_rotations(ph):
                def beside(at_):
                    if at_ in ROPE_AT:
                        rotate(ph, ROPE_AT[at_])
                for par in range(2):
                    unit(ph, 0, par, False, beside)

            def plain_units(ph):
                def body(i, first):
                    for par in range(2):
                        unit(ph, i, par, first)
                pairs(pe, ph, body, ph["fresh"] is not None or ph["K"] == FH)

            def head_sum(ph, n, par):
                pe.wait_ge(hn_sq_ready, n + (ph["hn0"] + 1))
                for to, _, w, _ in segments(ph["T"]):
                    last = pe.matmul(sums[par][:, to:to + w], mat(MEAN64), hn_sq[par][:, to:to + w],
                                     start=True, stop=True)
                last.then_inc(hn_sum, 1)

            def normed_units(ph):
                first = ph["unit0"] == 0
                unit(ph, 0, 0, first)
                unit(ph, 0, 1, first)
                head_sum(ph, 0, 0)
                if ph["units"] > 2:
                    with pe.Fori(1, ph["units"] // 2) as i:
                        unit(ph, i, 0, False)
                        head_sum(ph, i * 2 - 1, 1)
                        unit(ph, i, 1, False)
                        head_sum(ph, i * 2, 0)
                head_sum(ph, ph["units"] - 1, 1)

            def norm(ph):
                n0, segs = ph["norm0"], segments(ph["T"])

                def add_up(square, begin, end):
                    for to, _, w, _ in segs:
                        last = pe.matmul(sums[0][:, to:to + w], mat(MEAN1024), square[:, to:to + w],
                                         start=begin, stop=end)
                    return last

                if n0 == 0:
                    for k in range(KT):
                        pe.wait_ge(n_sq_ready, k + 1)
                        add_up(n_sq[k % 2], k == 0, k == KT - 1).then_inc(n_sum, 1)
                else:
                    pe.wait_ge(n_added, KT * n0)
                    add_up(n_sum_sq, True, False)
                    pe.wait_ge(n_sq_ready, KT * n0 + KT)
                    add_up(n_sq[1], False, True).then_inc(n_sum, 1)

            def retention(ph):
                q = sems["r"]
                l = ph["layer"]
                pe.wait_ge(acc_free, ph["unit0"])
                with pe.Fori(0, 4) as j:
                    pe.wait_ge(q["staged_act"], j * 1 + (5 * l + 1))
                    pe.wait_ge(q["staged_dve"], j * 2 + (10 * l + 2))

                    def turn_v():
                        for t in range(4):
                            last = pe.transpose(bank(0)[:, t * P:t * P + P], r_v[:, t * P:t * P + P], mat(IDENT))
                        last.then_inc(q["v_turned"], 1)

                    def score(t):
                        hd, s = divmod(t, 4)
                        half = slice(HD * hd, HD * hd + HD)
                        if t >= 2:
                            pe.wait_ge(q["biased"], BEGUN + j * 8 + (32 * l + t - 1))
                        else:
                            pe.wait_ge(q["biased"], BEGUN + j * 8 + 32 * l)
                        pe.matmul(bank(4 + t % 2), r_k[half, s * P:s * P + P], r_q[half, :],
                                  start=True, stop=True).then_inc(q["scored"], 1)

                    def values(t):
                        hd, s = divmod(t, 4)
                        if t == 0:
                            pe.wait_ge(q["v_kept"], j * 1 + (4 * l + 1))
                        if t == 4:
                            pe.wait_ge(q["evacuated"], BEGUN + j * 2 + 8 * l)
                        pe.wait_ge(q["biased"], BEGUN + j * 8 + (32 * l + t + 1))
                        pe.matmul(bank(2 + hd), r_vs[:, s, :], r_sc[t % 3][:],
                                  start=(s == 0), stop=(s == 3)).then_inc(q["summed"], 1)

                    for t in range(8 + 2):
                        if t < 8:
                            score(t)
                        if t == 1:
                            turn_v()
                        if t >= 2:
                            values(t - 2)
                    pe.wait_ge(q["evacuated"], BEGUN + j * 2 + (8 * l + 1))

            def diff(ph):
                q = sems["d"]
                l = ph["layer"]
                pe.wait_ge(sems["r"]["evacuated"], BEGUN + 8 * (l + 1))

                def score(j, b):
                    for m in range(2):
                        half = slice(HD * m, HD * m + HD)
                        t = 2 * b + m
                        if b >= 2:
                            pe.wait_ge(q["biased"], BEGUN + j * 8 + (32 * l + t - 3))
                        elif isinstance(j, int):
                            pe.wait_ge(q["biased"], BEGUN + j * 8 + 32 * l)
                        else:
                            pe.wait_ge(q["biased"], BEGUN + j * 8 + (32 * l + t - 3))
                        pe.matmul(bank(4 + t % 4), d_q[half, b * P:b * P + P], d_k[half, :],
                                  start=True, stop=True).then_inc(q["scored"], 1)

                def turn(j, b):
                    pe.wait_ge(q["probs"], BEGUN + j * 8 + (32 * l + 2 * b + 2))
                    if b >= 2:
                        pe.wait_ge(q["kept"], BEGUN + j * 4 + (16 * l + b - 1))
                    else:
                        pe.wait_ge(q["v_kept"], j * 1 + (4 * l + 1))
                    for t in range(4):
                        last = pe.transpose(bank(b % 2)[:, t * P:t * P + P],
                                            d_s[2 * b][:, t * P:t * P + P], mat(IDENT))
                    last.then_inc(q["turned"], 1)

                def values(j):
                    pe.wait_ge(q["kept"], BEGUN + j * 4 + (16 * l + 4))
                    pe.wait_ge(q["evacuated"], BEGUN + j * 1 + 4 * l)
                    for t in range(4):
                        last = pe.matmul(bank(2), d_vs[:, t, :], d_aT[:, t, :], start=(t == 0), stop=(t == 3))
                    last.then_inc(q["summed"], 1)

                def head(j, first):
                    pe.wait_ge(q["staged_act"], j * 1 + (5 * l + 1))
                    pe.wait_ge(q["staged_dve"], j * 2 + (10 * l + 2))
                    score(j, 0)
                    if not first:
                        turn(j - 1, 2)
                    score(j, 1)
                    if not first:
                        turn(j - 1, 3)
                        pe.wait_ge(q["kept"], BEGUN + j * 4 + (16 * l - 1))
                    else:
                        pe.wait_ge(q["kept"], BEGUN + 16 * l)
                    for t in range(4):
                        last = pe.transpose(bank(0)[:, t * P:t * P + P], d_v[:, t * P:t * P + P], mat(IDENT))
                    last.then_inc(q["v_turned"], 1)
                    if not first:
                        values(j - 1)
                    score(j, 2)
                    turn(j, 0)
                    pe.wait_ge(f_sq_ready, j + (8 * l + 1))
                    pe.wait_ge(f_std, j + 8 * l)
                    pe.matmul(bank(3), mat(MEAN64), f_sq[0][:], start=True, stop=True).then_inc(f_sum, 1)
                    score(j, 3)
                    turn(j, 1)

                head(0, True)
                with pe.Fori(1, 4) as j:
                    head(j, False)
                turn(3, 2)
                turn(3, 3)
                values(3)

            def fin1(ph):
                l8 = 8 * ph["layer"]
                for n in range(4, 8):
                    pe.wait_ge(f_sq_ready, l8 + n + 1)
                    if n == 4:
                        pe.wait_ge(sems["d"]["biased"], BEGUN + 32 * (ph["layer"] + 1))
                    if n >= 6:
                        pe.wait_ge(f_std, l8 + n - 1)
                    pe.matmul(bank(4 + n % 2), mat(MEAN128), f_sq[n % 2][:],
                              start=True, stop=True).then_inc(f_sum, 1)

            def na(ph):
                q = sems["n"]

                with pe.Fori(0, 8) as j:
                    pe.wait_ge(q["staged_act"], j * 1 + 1)
                    pe.wait_ge(q["staged_dve"], j * 2 + 1)

                    def turn_v():
                        pe.wait_ge(q["staged_dve"], j * 2 + 2)
                        pe.wait_ge(q["kept"], BEGUN + j * 12)
                        pe.wait_ge(acc_free, ph["unit0"])
                        for t in range(9):
                            frm = 8 * ROWS * t if t < 7 else S + (t - 7) * P
                            last = pe.transpose(bank(t // 4)[:, t % 4 * P:t % 4 * P + P],
                                                n_v[:, frm:frm + P], mat(IDENT))
                        last.then_inc(q["v_turned"], 1)

                    def score(t):
                        hd, b = divmod(t, 6)
                        half = slice(HD * hd, HD * hd + HD)
                        if t >= 2:
                            pe.wait_ge(q["biased"], BEGUN + j * 12 + (t - 1))
                        S_ = bank(4 + t % 2)
                        if b < 4:
                            queries = n_q[half, b * P:b * P + P]
                            frm = KEY_COL[b] * ROWS
                            pe.matmul(S_[:, 0:2 * P], queries, n_k[half, frm:frm + 2 * P], start=True, stop=True)
                            pe.matmul(S_[:, 2 * P:4 * P], queries, n_k[half, S:T2],
                                      start=True, stop=True).then_inc(q["scored"], 1)
                        else:
                            pe.matmul(S_[:, 0:C], n_q[half, S + (b - 4) * P:S + (b - 3) * P],
                                      n_k[half, S:T2], start=True, stop=True).then_inc(q["scored"], 1)

                    def turn(t):
                        b = t % 6
                        pe.wait_ge(q["probs"], BEGUN + j * 12 + (t + 1))
                        if t >= 2:
                            pe.wait_ge(q["kept"], BEGUN + j * 12 + (t - 1))
                        else:
                            pe.wait_ge(q["v_kept"], j * 1 + 1)
                        for c in range(4 if b < 4 else 2):
                            last = pe.transpose(bank(t % 2)[:, c * P:c * P + P],
                                                n_s[t % 3][:, c * P:c * P + P], mat(IDENT))
                        last.then_inc(q["turned"], 1)

                    def values(t):
                        hd, b = divmod(t, 6)
                        pe.wait_ge(q["kept"], BEGUN + j * 12 + (t + 1))
                        if hd and b == 0:
                            pe.wait_ge(q["evacuated"], BEGUN + j * 4)
                        if b < 4:
                            o = bank(2 + 4 * hd)[:, b * P:b * P + P]
                            tiles = [KEY_COL[b] // 8, KEY_COL[b] // 8 + 2, 7, 8]
                        else:
                            o = bank(3 + 4 * hd)[:, (b - 4) * P:(b - 3) * P]
                            tiles = [7, 8]
                        for c, v in enumerate(tiles):
                            last = pe.matmul(o, n_vs[:, v, :], n_pT[t % 2][:, c * P:c * P + P],
                                             start=(c == 0), stop=(c == len(tiles) - 1))
                        last.then_inc(q["summed"], 1)

                    for t in range(12 + 3):
                        if t < 12:
                            score(t)
                        if t == 1:
                            turn_v()
                        if 2 <= t < 14:
                            turn(t - 2)
                        if t >= 3:
                            values(t - 3)
                    pe.wait_ge(q["evacuated"], BEGUN + j * 4 + 2)

            def swa(ph):
                q = sems["s"]
                pe.wait_ge(acc_free, ph["unit0"])
                pe.wait_ge(hn_out, ph["hn0"])
                for n in range(len(ROPE_AT), ROPE_TILES):
                    rotate(ph, n)
                pe.wait_ge(rope_a, ROPE_TILES)
                pe.wait_ge(rope_out, ROPE_TILES)
                for kv in range(2):
                    if kv:
                        pe.wait_ge(q["kept"], BEGUN + 32)
                    for t in range(6):
                        last = pe.transpose(bank(t // 4)[:, t % 4 * P:t % 4 * P + P],
                                            proj[:, 10 + kv, t * P:t * P + P], mat(IDENT))
                    last.then_inc(q["v_turned"], 1)
                    with pe.Fori(0, 4) as g:
                        n = g * 8 + 32 * kv
                        pe.wait_ge(q["staged_act"], g * 1 + (4 * kv + 1))

                        def score(t):
                            hd, b = divmod(t, 4)
                            half = slice(HD * hd, HD * hd + HD)
                            if t >= 2:
                                pe.wait_ge(q["biased"], BEGUN + n + (t - 1))
                            else:
                                pe.wait_ge(q["biased"], BEGUN + n)
                            S_ = sums[t % 2]
                            lo, hi = max(b - 1, 0) * P, min(b + 2, 4) * P
                            queries = s_q[half, b * P:b * P + P]
                            pe.matmul(S_[:, 0:hi - lo], queries, proj[half, 8 + kv, lo:hi], start=True, stop=True)
                            for c in range(2):
                                at_ = hi - lo + c * P
                                last = pe.matmul(S_[:, at_:at_ + P], queries,
                                                 proj[half, 8 + kv, S + c * P:S + c * P + P], start=True, stop=True)
                            last.then_inc(q["scored"], 1)

                        def turn(t):
                            b = t % 4
                            pe.wait_ge(q["probs"], BEGUN + n + (t + 1))
                            pe.wait_ge(q["kept"], BEGUN + n + t)
                            if t == 0:
                                pe.wait_ge(q["v_kept"], kv + 1)
                            for c in range(5 if 0 < b < 3 else 4):
                                last = pe.transpose(ps[:, c * P:c * P + P],
                                                    s_s[t % 3][:, c * P:c * P + P], mat(IDENT))
                            last.then_inc(q["turned"], 1)

                        def values(t):
                            hd, b = divmod(t, 4)
                            pe.wait_ge(q["kept"], BEGUN + n + (t + 1))
                            if hd and b == 0:
                                pe.wait_ge(q["evacuated"], BEGUN + g * 2 + 8 * kv)
                            lo, hi = max(b - 1, 0), min(b + 2, 4)
                            tiles = list(range(lo, hi)) + [4, 5]
                            for c, v in enumerate(tiles):
                                last = pe.matmul(bank(2 + hd)[:, b * P:b * P + P], s_vs[:, v, :],
                                                 s_pT[t % 2][:, c * P:c * P + P],
                                                 start=(c == 0), stop=(c == len(tiles) - 1))
                            last.then_inc(q["summed"], 1)

                        for t in range(8 + 3):
                            if t < 8:
                                score(t)
                            if 2 <= t < 10:
                                turn(t - 2)
                            if t >= 3:
                                values(t - 3)
                        pe.wait_ge(q["evacuated"], BEGUN + g * 2 + (8 * kv + 1))

            begin(pe, ("v_turned", "scored", "turned", "summed"))
            pe.wait_ge(constants_in, 32)
            for ph in phases:
                kind = ph["kind"]
                if kind == "norm":
                    norm(ph)
                elif kind == "normed":
                    normed_units(ph)
                elif kind == "proj" and ph["weight"] == "swa_qkv":
                    units_beside_rotations(ph)
                elif kind in ("proj", "glu", "conv", "resid"):
                    plain_units(ph)
                elif kind == "retention":
                    pe.wait_ge(hn_out, ph["hn0"])
                    retention(ph)
                elif kind == "diff":
                    diff(ph)
                elif kind == "fin1":
                    fin1(ph)
                elif kind == "na":
                    pe.wait_ge(hn_out, ph["hn0"])
                    na(ph)
                elif kind == "swa":
                    swa(ph)

        @block.scalar
        def _(act):
            begin(act, ("kept",))
            for q in range(4):
                act.dma_start(xT[:, 2 * q:2 * q + 2, 0:S], d["x"][:, 2 * q:2 * q + 2, :]).then_inc(x_in[q], 16)
                if q == 0:
                    act.dma_start(mats[:], d["mats"]).then_inc(constants_in, 16)
            act.dma_start(small[:], d["small"]).then_inc(constants_in, 16)
            act.dma_start(lam_vec[:], d["lam"]).then_inc(loaded, 16)
            act.dma_start(silu_c[:], d["c"]).then_inc(loaded, 16)

            def row(ap):
                return ap.rearrange("p (a n) -> p a n", a=1)

            def hi_part(par, loads, K):
                act.wait_ge(w_loaded[par], loads)
                act.activation(w_hi[par][:, 0:K * P], w_raw[par][:, 0:K * P], ACT.Copy).then_inc(w_hi_ready, 1)

            def setup():
                act.wait_ge(loaded, N_INPUTS)
                act.activation(silu_c[:], silu_c[:], ACT.Silu).then_inc(silu_c_ready, 1)
                act.activation(lgam[:, 0:DEPTH * 16], col("decay", 0, DEPTH * 16), ACT.Exp).then_inc(lam_exp, 1)
                act.wait_ge(lam_step, 4)
                act.activation(lam[:, 4:8], lam[:, 0:4], ACT.Exp).then_inc(lam_exp, 1)

            act.wait_ge(ready, 2)

            def units_of(ph, body, peel=0):
                n, u0 = ph["units"] // 2, ph["unit0"]
                k_next = next((p["K"] for p in phases if p.get("weight") and p["unit0"] == u0 + 2 * n), None)
                same = n if k_next == ph["K"] else n - 1

                def pair(i, K):
                    def split(par):
                        if K is not None:
                            hi_part(par, i * 16 + (8 * u0 + 32), K)
                    body(i, split)

                peel = max(peel, same if same == 1 else 0)
                for i in range(min(peel, n)):
                    pair(i, ph["K"] if i < same else k_next)
                if same > peel:
                    with act.Fori(peel, same) as i:
                        pair(i, ph["K"])
                if same < n and n > peel:
                    pair(n - 1, k_next)

            def resid(ph):
                T, n0 = ph["norm_T"], ph["norm0"]
                if T == T2:
                    act.wait_ge(ctx_in, 16)

                def body(i, split):
                    for par in range(2):
                        act.wait_ge(mm_done, i * 2 + (ph["unit0"] + par + 1))
                        split(par)
                        if T is not None:
                            act.wait_ge(acc_free, i * 2 + (ph["unit0"] + par + 1))
                            if not (isinstance(i, int) and i == 0):
                                act.wait_ge(n_added, i * 2 + (KT * (n0 - 1) + par))
                            act.activation(row(n_sq[par][:, 0:T]), xT[:, bass.ds(i * 2 + par, 1), 0:T],
                                           ACT.Square).then_inc(n_sq_ready, 1)
                units_of(ph, body, peel=0 if T is None else 1)

            def norm(ph):
                n0, T = ph["norm0"], ph["T"]
                if n0 == 0:
                    for k in range(KT):
                        act.wait_ge(x_in[k // 2], 16)
                        if k >= 2:
                            act.wait_ge(n_sum, k - 1)
                        act.activation(n_sq[k % 2][:, 0:T], xT[:, k, 0:T], ACT.Square).then_inc(n_sq_ready, 1)
                    for par in range(2):
                        hi_part(par, 16, KT)
                else:
                    act.activation(stats[:, 20:21], eps1[:], ACT.Sqrt).then_inc(table_in, 1)
                    act.wait_ge(table_in, n0)
                    act.wait_ge(mm_done, ph["unit0"])
                act.wait_ge(n_sum, 8 + n0)
                act.activation(n_rstd[:, 0:T], sums[0][:, 0:T], ACT.Sqrt, bias=eps1[:]).then_inc(n_std, 1)
                for k in range(KT):
                    act.wait_ge(n_xn_ready, KT * n0 + k + 1)
                    if ph["block"] == 1 or k in POOL_TILES["norm"]:
                        act.activation(h_hi[:, k, 0:T], n_xn[k % 4][:, 0:T], ACT.Copy).then_inc(h_hi_ready, 1)
                        continue
                    for to, _, w, c in segments(T):
                        shift = mod[:, ph["layer"], 0 if ph["which"] == "attn" else 3, k, c:c + 1]
                        last = act.activation(h_hi[:, k, to:to + w], n_xn[k % 4][:, to:to + w], ACT.Identity,
                                              bias=shift)
                    last.then_inc(h_hi_ready, 1)

            def take_out(ph):
                def body(i, split):
                    for par in range(2):
                        act.wait_ge(mm_done, i * 2 + (ph["unit0"] + par + 1))
                        dst = proj1 if ph["T"] == S and ph["weight"] == "w_in" else proj
                        if ph["weight"] == "na_qkv":
                            act.activation(by_columns(proj[:, bass.ds(i * 2 + (ph["tile0"] + par), 1), 0:S]),
                                           from_rows(acc[par][:, 0:S]), ACT.Copy)
                            act.activation(proj[:, bass.ds(i * 2 + (ph["tile0"] + par), 1), S:T2],
                                           row(acc[par][:, S:T2]), ACT.Copy).then_inc(acc_free, 1)
                            split(par)
                            continue
                        act.activation(dst[:, bass.ds(i * 2 + (ph["tile0"] + par), 1), 0:ph["T"]],
                                       row(acc[par][:, 0:ph["T"]]),
                                       ACT.Silu if ph["func"] == "silu" else ACT.Copy).then_inc(acc_free, 1)
                        split(par)
                units_of(ph, body)

            def head_norm(ph):
                T, h0 = ph["T"], ph["hn0"]
                dst = proj1 if ph["weight"] == "w_in" else proj

                def square(i, par):
                    act.wait_ge(acc_free, i * 2 + (ph["unit0"] + par + 1))
                    act.activation(row(hn_sq[par][:, 0:T]), dst[:, bass.ds(i * 2 + (ph["tile0"] + par), 1), 0:T],
                                   ACT.Square).then_inc(hn_sq_ready, 1)

                def root(i, par):
                    act.wait_ge(hn_sum, i * 2 + (h0 + par + 1))
                    if isinstance(i, int):
                        act.wait_ge(hn_out, max(2 * i + h0 + par - 1, h0))
                    else:
                        act.wait_ge(hn_out, i * 2 + (h0 + par - 1))
                    act.activation(hn_r[par][:, 0:T], sums[par][:, 0:T], ACT.Sqrt, bias=eps1[:]).then_inc(hn_std, 1)

                def body(i, split):
                    for par in range(2):
                        act.wait_ge(mm_done, i * 2 + (ph["unit0"] + par + 1))
                        split(par)
                        square(i, par)
                        if par:
                            root(i, 0)
                        elif not (isinstance(i, int) and i == 0):
                            root(i - 1, 1)
                units_of(ph, body, peel=1 if h0 else 2)
                root(ph["units"] // 2 - 1, 1)

            def glu(ph):
                act.wait_ge(acc_free, ph["unit0"])

                def body(f, split):
                    act.wait_ge(mm_done, f * 2 + (ph["unit0"] + 1))
                    split(0)
                    act.activation(glu_g[:], acc[0][:, 0:S], ACT.Silu).then_inc(acc_free, 1)
                    act.wait_ge(mm_done, f * 2 + (ph["unit0"] + 2))
                    split(1)
                    act.wait_ge(acc_free, f * 2 + (ph["unit0"] + 2))
                    act.activation(b_hi[:, dyn(f), :], row(glu_a[:]), ACT.Copy).then_inc(glu_hi, 1)
                units_of(ph, body)

            def conv(ph):
                n0, T = ph["conv0"], ph["T"]
                W = ACTW if T == T2 else S
                act.wait_ge(acc_free, ph["unit0"])

                def body(f, split):
                    for par in range(2):
                        act.wait_ge(mm_done, f * 2 + (ph["unit0"] + par + 1))
                        split(par)
                        act.wait_ge(conv_step, BEGUN + f * 7 + 7 * n0)
                        for to, frm, n, _ in segments(T, CTX_AT):
                            last = act.activation(u_pad[par][:, 2 + frm:2 + frm + n], acc[par][:, to:to + n], ACT.Copy)
                        last.then_inc(acc_free, 1)
                    act.wait_ge(conv_step, BEGUN + f * 7 + (7 * n0 + 6))
                    act.activation(conv_y[1][:, 0:W], conv_y[1][:, 0:W], ACT.Silu).then_inc(conv_gate, 1)
                    act.wait_ge(conv_step, BEGUN + f * 7 + (7 * n0 + 7))
                    act.activation(a_hi[:, dyn(f), 0:W], row(conv_y[0][:, 0:W]), ACT.Copy).then_inc(conv_hi, 1)
                units_of(ph, body)

            def retention(ph):
                q, l = sems["r"], ph["layer"]

                def stage(j, scored):
                    act.wait_ge(q["scored"], scored)
                    act.activation(row(r_q[:]), proj1[:, bass.ds(j + 8, 1), :], ACT.Copy).then_inc(q["staged_act"], 1)

                def mask(j, hd):
                    act.wait_ge(q["mask_arg"], BEGUN + j * 4 + (20 * l + 2 * hd + 2))
                    act.activation(r_mask[hd][:], r_mask[hd][:], ACT.Exp).then_inc(q["bias"], 1)

                stage(0, BEGUN + 32 * l)
                mask(0, 0)
                mask(0, 1)
                with act.Fori(0, 4) as j:
                    act.wait_ge(q["v_turned"], BEGUN + j + (4 * l + 1))
                    act.wait_ge(q["summed"], BEGUN + j * 8 + 32 * l)
                    act.activation(r_vs[:].rearrange("p t n -> p (t n)"), bank(0), ACT.Copy).then_inc(q["v_kept"], 1)
                    mask(j + 1, 0)
                    stage(j + 1, BEGUN + j * 8 + (32 * l + 8))
                    mask(j + 1, 1)

            def diff(ph):
                q, l = sems["d"], ph["layer"]
                act.wait_ge(tab["diff"], 16 * (l + 1))
                for name, n in (("staged_act", 5), ("staged_dve", 10), ("bias", 10), ("mask_arg", 20)):
                    act.wait_ge(sems["r"][name], (BEGUN if name == "mask_arg" else 0) + n * (l + 1))
                act.wait_ge(sems["r"]["summed"], BEGUN + 32 * (l + 1))

                def exp(j, b):
                    for t in (2 * b, 2 * b + 1):
                        act.wait_ge(q["negmax"], j * 8 + (32 * l + t + 1))
                        act.activation(d_s[t][:], d_s[t][:], ACT.Exp, bias=stats[:, 8 + t % 4:9 + t % 4],
                                       accum_out=stats[:, 12 + t % 4:13 + t % 4]).then_inc(q["exped"], 1)

                def keep(j, b):
                    act.wait_ge(q["turned"], BEGUN + j * 4 + (16 * l + b + 1))
                    if b == 0:
                        act.wait_ge(q["summed"], BEGUN + j + 4 * l)
                    act.activation(d_aT[:, :, b * P:b * P + P], bank(b % 2).rearrange("p (t n) -> p t n", n=P),
                                   ACT.Copy).then_inc(q["kept"], 1)

                def stage(j, scored):
                    act.wait_ge(q["scored"], scored)
                    act.activation(row(d_q[:]), proj1[:, dyn(j), :], ACT.Copy).then_inc(q["staged_act"], 1)

                def head(j, first):
                    act.wait_ge(q["biased"], BEGUN + j * 8 + 32 * l)
                    act.activation(d_bias[:], d_dist[:], ACT.Copy, scale=dcol("slope", j)).then_inc(q["bias"], 1)
                    if not first:
                        keep(j - 1, 1)
                        root(j - 1)
                    act.wait_ge(f_sum, j + 8 * l)
                    act.activation(row(f_sq[0][:]), proj1[:, bass.ds(j + 8, 1), :], ACT.Square
                                   ).then_inc(f_sq_ready, 1)
                    exp(j, 0)
                    if not first:
                        keep(j - 1, 2)
                    exp(j, 1)
                    if not first:
                        keep(j - 1, 3)
                    act.wait_ge(q["v_turned"], BEGUN + j + (4 * l + 1))
                    act.wait_ge(q["summed"], BEGUN + j + 4 * l)
                    act.activation(d_vs[:].rearrange("p t n -> p (t n)"), bank(0), ACT.Copy).then_inc(q["v_kept"], 1)
                    exp(j, 2)
                    keep(j, 0)
                    stage(j + 1, BEGUN + j * 8 + (32 * l + 8))
                    exp(j, 3)

                def root(j):
                    act.wait_ge(f_sum, j + (8 * l + 1))
                    act.wait_ge(f_y_ready, j * 2 + 12 * l)
                    act.activation(f_r[0][:], bank(3), ACT.Sqrt, bias=eps1[:]).then_inc(f_std, 1)

                stage(0, BEGUN + 32 * l)
                head(0, True)
                with act.Fori(1, 4) as j:
                    head(j, False)
                keep(3, 1)
                root(3)
                keep(3, 2)
                keep(3, 3)

            def fin1(ph):
                l = ph["layer"]
                act.wait_ge(sems["d"]["staged_act"], 5 * (l + 1))
                act.wait_ge(sems["d"]["staged_dve"], 10 * (l + 1))

                def square(n):
                    act.wait_ge(f_sum, 8 * l + max(n - 1, 4))
                    act.activation(f_sq[n % 2][:], proj1[:, n - 4, :], ACT.Square).then_inc(f_sq_ready, 1)

                def root(n):
                    act.wait_ge(f_sum, 8 * l + n + 1)
                    act.wait_ge(f_y_ready, 12 * l + _f_y(max(n - 2, 3)))
                    act.activation(f_r[n % 2][:], bank(4 + n % 2), ACT.Sqrt, bias=eps1[:]).then_inc(f_std, 1)

                def hi(k):
                    act.wait_ge(f_y_ready, 12 * l + _f_y(k))
                    act.activation(h_hi[:, k, 0:S], proj1[:, 8 + k if k < 4 else k - 4, :], ACT.Copy
                                   ).then_inc(h_hi_ready, 1)

                act.wait_ge(sems["d"]["evacuated"], BEGUN + 4 * (l + 1))
                square(4)
                hi(0)
                square(5)
                root(4)
                hi(1)
                square(6)
                root(5)
                hi(2)
                square(7)
                root(6)
                hi(3)
                root(7)
                for k in range(4, 8):
                    hi(k)

            def na(ph):
                q = sems["n"]

                def stage(j, scored):
                    act.wait_ge(q["scored"], scored)
                    act.activation(row(n_q[:]), proj[:, dyn(j), :], ACT.Copy).then_inc(q["staged_act"], 1)

                stage(0, BEGUN)
                with act.Fori(0, 8) as j:
                    def keep_v():
                        act.wait_ge(q["v_turned"], BEGUN + j + 1)
                        act.wait_ge(q["summed"], BEGUN + j * 12)
                        for b in range(3):
                            n = (P if b == 2 else S)
                            last = act.activation(n_vs[:].rearrange("p t n -> p (t n)")[:, b * S:b * S + n],
                                                  bank(b, n), ACT.Copy)
                        last.then_inc(q["v_kept"], 1)

                    def exp(t):
                        w = S if t % 6 < 4 else C
                        act.wait_ge(q["negmax"], j * 12 + (t + 1))
                        act.activation(n_s[t % 3][:, 0:w], n_s[t % 3][:, 0:w], ACT.Exp,
                                       bias=stats[:, 3 + t % 3:4 + t % 3],
                                       accum_out=stats[:, 6 + t % 3:7 + t % 3]).then_inc(q["exped"], 1)

                    def keep(t):
                        w = S if t % 6 < 4 else C
                        act.wait_ge(q["turned"], BEGUN + j * 12 + (t + 1))
                        if t >= 2:
                            act.wait_ge(q["summed"], BEGUN + j * 12 + (t - 1))
                        act.activation(n_pT[t % 2][:, 0:w], bank(t % 2, w), ACT.Copy).then_inc(q["kept"], 1)

                    for t in range(12 + 2):
                        if t < 12:
                            exp(t)
                        if t == 1:
                            keep_v()
                        if t == 12:
                            stage(j + 1, BEGUN + j * 12 + 12)
                        if t >= 2:
                            keep(t - 2)

            def swa(ph):
                q = sems["s"]
                act.wait_ge(hn_out, ph["hn0"])
                act.wait_ge(rope_out, ROPE_TILES)

                def stage(tile, scored):
                    act.wait_ge(q["scored"], scored)
                    act.activation(row(s_q[:]), proj[:, dyn(tile), 0:S], ACT.Copy).then_inc(q["staged_act"], 1)

                stage(0, BEGUN)
                for kv in range(2):
                    act.wait_ge(q["v_turned"], BEGUN + kv + 1)
                    if kv:
                        act.wait_ge(q["summed"], BEGUN + 32)
                    act.activation(s_vs[:].rearrange("p t n -> p (t n)"), ps[:, 0:6 * P], ACT.Copy).then_inc(q["v_kept"], 1)
                    with act.Fori(0, 4) as g:
                        n = g * 8 + 32 * kv

                        def width(t):
                            return (5 if 0 < t % 4 < 3 else 4) * P

                        def exp(t):
                            act.wait_ge(q["negmax"], n + (t + 1))
                            act.activation(s_s[t % 3][:, 0:width(t) + 1], s_s[t % 3][:, 0:width(t) + 1], ACT.Exp,
                                           bias=stats[:, 3 + t % 3:4 + t % 3],
                                           accum_out=stats[:, 6 + t % 3:7 + t % 3]).then_inc(q["exped"], 1)

                        def keep(t):
                            act.wait_ge(q["turned"], BEGUN + n + (t + 1))
                            act.wait_ge(q["summed"], BEGUN + n + max(t - 1, 0))
                            act.activation(s_pT[t % 2][:, 0:width(t)], ps[:, 0:width(t)], ACT.Copy).then_inc(q["kept"], 1)

                        for t in range(8 + 2):
                            if t < 8:
                                exp(t)
                            if t == 8:
                                stage(g + (4 * kv + 1), BEGUN + n + 8)
                            if t >= 2:
                                keep(t - 2)

            def fin2(ph):
                s_done = sems["n"]["evacuated"] if ph["T"] == T2 else sems["s"]["evacuated"]
                act.wait_ge(s_done, BEGUN + (32 if ph["T"] == T2 else 16))
                act.wait_ge((sems["n"] if ph["T"] == T2 else sems["s"])["staged_act"], 9)
                for n in range(8):
                    act.activation(h_hi[:, n, 0:ph["T"]], proj[:, n, 0:ph["T"]], ACT.Copy).then_inc(h_hi_ready, 1)

            for ph in phases:
                kind = ph["kind"]
                if kind == "norm":
                    norm(ph)
                    if ph["norm0"] == 0:
                        setup()
                elif kind == "normed":
                    head_norm(ph)
                elif kind == "proj":
                    take_out(ph)
                elif kind == "resid":
                    resid(ph)
                elif kind == "glu":
                    glu(ph)
                elif kind == "conv":
                    conv(ph)
                elif kind == "retention":
                    act.wait_ge(hn_out, ph["hn0"])
                    act.wait_ge(mm_done, ph["unit0"])
                    retention(ph)
                elif kind == "diff":
                    diff(ph)
                elif kind == "fin1":
                    fin1(ph)
                elif kind == "na":
                    act.wait_ge(hn_out, ph["hn0"])
                    act.wait_ge(mm_done, ph["unit0"])
                    na(ph)
                elif kind == "swa":
                    act.wait_ge(mm_done, ph["unit0"])
                    swa(ph)
                elif kind == "fin2":
                    fin2(ph)

        @block.vector
        def _(dve):
            def row(ap):
                return ap.rearrange("p (a n) -> p a n", a=1)

            begin(dve, ("biased", "evacuated", "mask_arg", "probs"), (conv_step, a_lo_ready))
            dve.memset(zero1[:], 0.0).then_inc(ready, 1)
            dve.memset(eps1[:], EPS).then_inc(ready, 1)
            dve.memset(lgam[:, DEPTH * 16:], 0.0).then_inc(ready, 1)
            dve.wait_ge(ready, 3)
            def setup():
                dve.wait_ge(loaded, N_INPUTS)
                for l in range(DEPTH):
                    for m in range(2):
                        n = 2 * l + m
                        if n:
                            dve.wait_ge(lam_step, n)
                        dve.tensor_tensor_reduce(lam_prod[:], lam_vec[:, 4 * l + 2 * m, :], lam_vec[:, 4 * l + 2 * m + 1, :],
                                                 1.0, 0.0, ALU.mult, ALU.add, lam[:, n:n + 1]).then_inc(lam_step, 1)
                dve.wait_ge(lam_exp, 2)
                for l in range(DEPTH):
                    init = 0.8 - 0.6 * float(np.exp(-0.3 * l))
                    dve.scalar_tensor_tensor(out=lam[:, 8 + l:9 + l], in0=lam[:, 4 + 2 * l:5 + 2 * l], scalar=init,
                                             in1=lam[:, 5 + 2 * l:6 + 2 * l], op0=ALU.add, op1=ALU.subtract
                                             ).then_inc(lam_step, 1)
                    dve.tensor_scalar(lam[:, 10 + l:11 + l], col("g_diff", l), 1.0 - init, None, ALU.mult
                                      ).then_inc(lam_step, 1)
                    dve.tensor_scalar(col("g_dqk", 8 * l, 4), col("g_dqk", 8 * l, 4), HD ** -0.5, None, ALU.mult
                                      ).then_inc(lam_step, 1)
                dve.tensor_scalar(col("g_na", 0, 8), col("g_na", 0, 8), HD ** -0.5, None, ALU.mult).then_inc(lam_step, 1)
                dve.tensor_scalar(col("g_swa", 0, 8), col("g_swa", 0, 8), HD ** -0.5, None, ALU.mult).then_inc(lam_step, 1)
                dve.tensor_scalar(lgam[:], lgam[:], -1.0, None, ALU.mult).then_inc(lam_step, 1)
                dve.wait_ge(lam_step, 13)

            def modulation(i, u0):
                first = isinstance(i, int) and i == 0 and u0 == 0
                dve.wait_ge(silu_c_ready, 1)
                dve.wait_ge(mod_loaded, i * 16 + (8 * u0 + 16))
                if not first:
                    dve.wait_ge(mod_kept, i + u0 // 2)
                    dve.wait_ge(mod_step, i * 2 + u0)
                dve.tensor_tensor_reduce(mod_junk[:], mod_w[:], silu_c[:, 0, :], 1.0, 0.0, ALU.mult, ALU.add,
                                         mod_sum[:, 0:1]).then_inc(mod_step, 1)
                dve.wait_ge(mod_step, i * 2 + (u0 + 1))
                dve.tensor_tensor_reduce(mod_junk[:], mod_w[:], silu_c[:, 1, :], 1.0, 0.0, ALU.mult, ALU.add,
                                         mod_sum[:, 1:2]).then_inc(mod_step, 1)
                dve.wait_ge(mod_step, i * 2 + (u0 + 2))
                dve.tensor_copy(mod[:].rearrange("p l s k c -> p (l s k c)")[:, bass.ds(i * 2 + u0, 2)],
                                mod_sum[:]).then_inc(mod_kept, 1)

            def modulation_pairs(ph):
                if ph["unit0"] < MOD_UNITS:
                    with dve.Fori(0, ph["units"] // 2) as i:
                        modulation(i, ph["unit0"])

            def modulation_end():
                dve.wait_ge(mod_kept, DEPTH * 48)
                dve.tensor_tensor(mod[:].rearrange("p l s k c -> p (l s k c)"),
                                  mod[:].rearrange("p l s k c -> p (l s k c)"),
                                  col("b_mod", 0, DEPTH * 96), ALU.add).then_inc(mod_ready, 1)
                dve.wait_ge(mod_ready, 1)
                for l in range(DEPTH):
                    for w, name in enumerate(("g2_attn", "g2_ffn")):
                        dve.scalar_tensor_tensor(
                            out=gs[:, l, w].rearrange("p k c -> p (k c)"),
                            in0=mod[:, l, 1 + 3 * w].rearrange("p k c -> p (k c)"), scalar=1.0,
                            in1=col(name, 16 * l, 16), op0=ALU.add, op1=ALU.mult).then_inc(mod_ready, 1)
                dve.wait_ge(mod_ready, 5)

            def norm(ph):
                n0, T, g = ph["norm0"], ph["T"], ph["h0"]
                w_i = 0 if ph["which"] == "attn" else 1
                if n0 == 0:
                    dve.wait_ge(constants_in, 32)
                dve.wait_ge(n_std, n0 + 1)
                dve.reciprocal(n_rstd[:, 0:T], n_rstd[:, 0:T]).then_inc(n_recip, 1)
                dve.wait_ge(n_recip, n0 + 1)

                def shift(k, c):
                    return mod[:, ph["layer"], 3 * w_i, k, c:c + 1]

                def normed(k):
                    if k >= 4:
                        wait_lo(dve, ph, k - 4)
                    for to, _, w, c in segments(T):
                        gain = col("g_" + ph["which"], KT * ph["layer"] + k) if ph["block"] == 1 else \
                            gs[:, ph["layer"], w_i, k, c:c + 1]
                        last = dve.scalar_tensor_tensor(
                            out=n_xn[k % 4][:, to:to + w], in0=xT[:, k, to:to + w], scalar=gain,
                            in1=n_rstd[:, to:to + w], op0=ALU.mult, op1=ALU.mult)
                    if ph["block"] == 2 and k in POOL_TILES["norm"]:
                        last.then_inc(n_scaled, 1)
                        dve.wait_ge(n_scaled, 3 * (n0 - 2 * DEPTH) + k // 2)
                        for to, _, w, c in segments(T):
                            last = dve.tensor_scalar(n_xn[k % 4][:, to:to + w], n_xn[k % 4][:, to:to + w],
                                                     shift(k, c), None, ALU.add)
                    last.then_inc(n_xn_ready, 1)

                def lo(k):
                    dve.wait_ge(h_hi_ready, KT * g + k + 1)
                    for to, _, w, c in segments(T):
                        last = dve.scalar_tensor_tensor(
                            out=h_lo[:, k, to:to + w], in0=n_xn[k % 4][:, to:to + w],
                            scalar=zero1[:] if ph["block"] == 1 else shift(k, c),
                            in1=h_hi[:, k, to:to + w].bitcast(F32), op0=ALU.add, op1=ALU.subtract)
                    last.then_inc(h_dve, 1)

                normed(0)
                normed(1)
                lo(0)
                for k in range(1, KT, 2):
                    if k > 1:
                        normed(k)
                    if k < KT - 1:
                        normed(k + 1)
                    lo(k)

            def head_norm(ph):
                T, h0 = ph["T"], ph["hn0"]
                dst = proj1 if ph["weight"] == "w_in" else proj

                def tile(i, par):
                    return dst[:, bass.ds(i * 2 + (ph["tile0"] + par), 1), 0:T]

                def take(i, par):
                    dve.wait_ge(mm_done, i * 2 + (ph["unit0"] + par + 1))
                    if ph["weight"] == "na_qkv":
                        dve.tensor_copy(by_columns(dst[:, bass.ds(i * 2 + (ph["tile0"] + par), 1), 0:S]),
                                        from_rows(acc[par][:, 0:S]))
                        dve.tensor_copy(dst[:, bass.ds(i * 2 + (ph["tile0"] + par), 1), S:T2],
                                        row(acc[par][:, S:T2])).then_inc(acc_free, 1)
                    else:
                        dve.tensor_copy(tile(i, par), row(acc[par][:, 0:T])).then_inc(acc_free, 1)

                def scale(i, par):
                    dve.wait_ge(hn_std, i * 2 + (h0 + par + 1))
                    dve.reciprocal(hn_r[par][:, 0:T], hn_r[par][:, 0:T]).then_inc(hn_recip, 1)
                    dve.wait_ge(hn_recip, i * 2 + (h0 + par + 1))
                    dve.scalar_tensor_tensor(out=tile(i, par), in0=tile(i, par),
                                             scalar=dcol(ph["gains"][0], i * 2 + (ph["gains"][1] + par)),
                                             in1=row(hn_r[par][:, 0:T]), op0=ALU.mult, op1=ALU.mult
                                             ).then_inc(hn_out, 1)

                beside = ph["unit0"] < MOD_UNITS
                if beside:
                    modulation(0, ph["unit0"])
                take(0, 0)
                take(0, 1)
                scale(0, 0)
                if ph["units"] > 2:
                    with dve.Fori(1, ph["units"] // 2) as i:
                        if beside:
                            modulation(i, ph["unit0"])
                        take(i, 0)
                        scale(i - 1, 1)
                        take(i, 1)
                        scale(i, 0)
                scale(ph["units"] // 2 - 1, 1)

            def resid(ph):
                T, n0 = ph["norm_T"], ph["norm0"]
                if T == T2:
                    dve.wait_ge(ctx_in, 16)
                if T is not None:
                    dve.wait_ge(a_lo_ready, BEGUN + ph["glu0"] + ph["conv0"])
                    dve.memset(n_sum_sq[:, 0:T], 0.0).then_inc(n_added, 1)

                def body(i, first):
                    if ph["unit0"] < MOD_UNITS:
                        modulation(i, ph["unit0"])
                    for par in range(2):
                        dve.wait_ge(mm_done, i * 2 + (ph["unit0"] + par + 1))
                        for to, _, n, c in segments(ph["T"]):
                            x_ = xT[:, bass.ds(i * 2 + par, 1), to:to + n]
                            if ph["gate"] is None:
                                gate = 1.0
                            else:
                                l, part = ph["gate"]
                                gate = mod[:].rearrange("p l s k c -> p (l s k c)")[
                                    :, bass.ds(i * 4 + (2 * KT * (6 * l + part) + 2 * par + c), 1)]
                            last = dve.scalar_tensor_tensor(out=x_, in0=row(acc[par][:, to:to + n]), scalar=gate,
                                                            in1=x_, op0=ALU.mult, op1=ALU.add)
                        last.then_inc(acc_free, 1)
                        if T is not None and not (isinstance(i, int) and i + par == 0):
                            before = KT * (n0 - 1) + par
                            dve.wait_ge(n_sq_ready, i * 2 + (KT * n0 + par))
                            dve.wait_ge(n_added, i * 2 + before)
                            dve.tensor_tensor(n_sum_sq[:, 0:T], n_sum_sq[:, 0:T], n_sq[1 - par][:, 0:T], ALU.add
                                              ).then_inc(n_added, 1)
                pairs(dve, ph, body, T is not None)

            def glu(ph):
                n0 = ph["glu0"]
                with dve.Fori(0, FH) as f:
                    modulation(f, ph["unit0"])
                    dve.wait_ge(acc_free, f * 2 + (ph["unit0"] + 1))
                    dve.wait_ge(mm_done, f * 2 + (ph["unit0"] + 2))
                    dve.wait_ge(a_lo_ready, BEGUN + f + n0)
                    dve.tensor_tensor(glu_a[:], acc[1][:, 0:S], glu_g[:], ALU.mult).then_inc(acc_free, 1)
                    dve.wait_ge(glu_hi, f + (n0 + 1))
                    dve.tensor_tensor(b_lo[:, bass.ds(f, 1), :], row(glu_a[:]),
                                      b_hi[:, bass.ds(f, 1), :].bitcast(F32), ALU.subtract).then_inc(a_lo_ready, 1)

            def conv(ph):
                n0, T, l = ph["conv0"], ph["T"], ph["layer"]
                W = ACTW if T == T2 else S
                for par in range(2):
                    for c in (0, 2 + S, 2 + ACTW):
                        dve.memset(u_pad[par][:, c:c + 2], 0.0).then_inc(conv_zero, 1)
                with dve.Fori(0, FH) as f:
                    m = 7 * n0

                    def tap(par, j):
                        return dcol("conv", f * 8 + (((l * FT + ph["half"] * FH) * 2 + par) * 4 + j))
                    for par in range(2):
                        for j in range(3):
                            y, u = conv_y[par][:, 0:W], u_pad[par][:, 1 + j:1 + j + W]
                            if j == 0:
                                dve.wait_ge(a_lo_ready, BEGUN + f + (ph["glu0"] + n0))
                                dve.wait_ge(acc_free, f * 2 + (ph["unit0"] + par + 1))
                                dve.wait_ge(conv_zero, 6 * (n0 // FH + 1))
                                dve.tensor_scalar(y, u, tap(par, 0), tap(par, 3), ALU.mult, ALU.add
                                                  ).then_inc(conv_step, 1)
                            else:
                                dve.wait_ge(conv_step, BEGUN + f * 7 + (m + 3 * par + j))
                                dve.scalar_tensor_tensor(out=y, in0=u, scalar=tap(par, j), in1=y,
                                                         op0=ALU.mult, op1=ALU.add).then_inc(conv_step, 1)
                    dve.wait_ge(conv_gate, f + (n0 + 1))
                    dve.wait_ge(conv_step, BEGUN + f * 7 + (m + 6))
                    dve.tensor_tensor(conv_y[0][:, 0:W], conv_y[0][:, 0:W], conv_y[1][:, 0:W], ALU.mult
                                      ).then_inc(conv_step, 1)
                    dve.wait_ge(conv_hi, f + (n0 + 1))
                    dve.tensor_tensor(a_lo[:, bass.ds(f, 1), 0:W], row(conv_y[0][:, 0:W]),
                                      a_hi[:, bass.ds(f, 1), 0:W].bitcast(F32), ALU.subtract).then_inc(a_lo_ready, 1)

            def retention(ph):
                q, l = sems["r"], ph["layer"]
                dve.wait_ge(tab["retention"], 32 * (l + 1))

                def evacuate(j, hd):
                    half = slice(HD * hd, HD * hd + HD)
                    dve.wait_ge(q["summed"], BEGUN + j * 8 + (32 * l + 4 * hd + 4))
                    dve.tensor_copy(proj1[half, bass.ds(j + 8, 1), :], row(bank(2 + hd)[half, :])
                                    ).then_inc(q["evacuated"], 1)

                def stage_k(j, scored):
                    dve.wait_ge(q["scored"], scored)
                    dve.tensor_scalar(row(r_k[:]), proj1[:, bass.ds(j + 12, 1), :], HD ** -0.5, None, ALU.mult
                                      ).then_inc(q["staged_dve"], 1)

                def stage_v(j, turned):
                    dve.wait_ge(q["v_turned"], turned)
                    dve.tensor_copy(row(r_v[:]), proj1[:, bass.ds(j + 16, 1), :]).then_inc(q["staged_dve"], 1)

                def mask(j, hd, used):
                    lg = [lgam[:, bass.ds(j * 2 + (16 * l + 8 * b + hd), 1)] for b in range(2)]
                    m = 20 * l + 2 * hd
                    dve.wait_ge(q["mask_arg"], BEGUN + j * 4 + m)
                    dve.tensor_scalar(r_tmp[:], r_dpos[:], lg[0], None, ALU.mult).then_inc(q["mask_arg"], 1)
                    dve.wait_ge(q["mask_arg"], BEGUN + j * 4 + (m + 1))
                    dve.wait_ge(q["biased"], used)
                    dve.scalar_tensor_tensor(out=r_mask[hd][:], in0=r_dneg[:], scalar=lg[1], in1=r_tmp[:],
                                             op0=ALU.mult, op1=ALU.add).then_inc(q["mask_arg"], 1)

                stage_k(0, BEGUN + 32 * l)
                stage_v(0, BEGUN + 4 * l)
                mask(0, 0, BEGUN + 32 * l)
                mask(0, 1, BEGUN + 32 * l)
                with dve.Fori(0, 4) as j:
                    for t in range(8):
                        hd, s = divmod(t, 4)
                        dve.wait_ge(q["bias"], j * 2 + (10 * l + hd + 1))
                        dve.wait_ge(q["scored"], BEGUN + j * 8 + (32 * l + t + 1))
                        if t >= 3:
                            dve.wait_ge(q["summed"], BEGUN + j * 8 + (32 * l + t - 2))
                        else:
                            dve.wait_ge(q["summed"], BEGUN + j * 8 + 32 * l)
                        dve.tensor_tensor(r_sc[t % 3][:], bank(4 + t % 2),
                                          r_mask[hd][:, (3 - s) * P:(3 - s) * P + S], ALU.mult
                                          ).then_inc(q["biased"], 1)
                        if t == 4:
                            mask(j + 1, 0, BEGUN + j * 8 + (32 * l + 4))
                        if t == 6:
                            evacuate(j, 0)
                    stage_k(j + 1, BEGUN + j * 8 + (32 * l + 8))
                    stage_v(j + 1, BEGUN + j + (4 * l + 1))
                    mask(j + 1, 1, BEGUN + j * 8 + (32 * l + 8))
                    evacuate(j, 1)

            def diff(ph):
                q, l = sems["d"], ph["layer"]
                for name, n in (("staged_act", 5), ("staged_dve", 10), ("bias", 10), ("mask_arg", 20)):
                    dve.wait_ge(sems["r"][name], (BEGUN if name == "mask_arg" else 0) + n * (l + 1))
                dve.wait_ge(sems["r"]["evacuated"], BEGUN + 8 * (l + 1))

                def bias(j, b):
                    for t in (2 * b, 2 * b + 1):
                        dve.wait_ge(q["bias"], j + (4 * l + 1))
                        dve.wait_ge(q["scored"], BEGUN + j * 8 + (32 * l + t + 1))
                        if isinstance(j, int):
                            dve.wait_ge(q["turned"], BEGUN + 16 * l)
                        else:
                            dve.wait_ge(q["turned"], BEGUN + j * 4 + (16 * l + b - 3))
                        dve.memset(pace[:, 2:3], 0.0)
                        dve.tensor_tensor_reduce(d_s[t][:], bank(4 + t % 4), d_bias[:, (3 - b) * P:(3 - b) * P + S],
                                                 1.0, NEG, ALU.add, ALU.max,
                                                 stats[:, 4 + t % 4:5 + t % 4]).then_inc(q["biased"], 1)
                        dve.wait_ge(q["biased"], BEGUN + j * 8 + (32 * l + t + 1))
                        dve.tensor_scalar(stats[:, 8 + t % 4:9 + t % 4], stats[:, 4 + t % 4:5 + t % 4],
                                          -1.0, None, ALU.mult).then_inc(q["negmax"], 1)

                def probs(j, b):
                    t0, t1 = 2 * b, 2 * b + 1
                    n = 32 * l + 2 * b
                    dve.wait_ge(q["exped"], j * 8 + (32 * l + t1 + 1))
                    sm = stats[:, 12 + t0 % 4:14 + t0 % 4]
                    dve.wait_ge(q["probs"], BEGUN + j * 8 + n)
                    dve.reciprocal(stats[:, 16:18], sm).then_inc(q["recip"], 1)
                    dve.wait_ge(q["recip"], j * 8 + (n + 1))
                    dve.tensor_scalar(stats[:, 18:19], stats[:, 17:18], lam[:, 8 + l:9 + l], None, ALU.mult
                                      ).then_inc(q["recip"], 1)
                    dve.wait_ge(q["recip"], j * 8 + (n + 2))
                    dve.tensor_scalar(d_s[t1][:], d_s[t1][:], stats[:, 18:19], None, ALU.mult
                                      ).then_inc(q["probs"], 1)
                    dve.wait_ge(q["probs"], BEGUN + j * 8 + (n + 1))
                    dve.scalar_tensor_tensor(out=d_s[t0][:], in0=d_s[t0][:], scalar=stats[:, 16:17],
                                             in1=d_s[t1][:], op0=ALU.mult, op1=ALU.subtract
                                             ).then_inc(q["probs"], 1)

                def finish(j):
                    tile = proj1[:, bass.ds(j + 8, 1), :]
                    dve.wait_ge(f_std, j + (8 * l + 1))
                    dve.reciprocal(f_r[0][:], f_r[0][:]).then_inc(f_recip, 1)
                    dve.wait_ge(f_recip, j + (8 * l + 1))
                    dve.scalar_tensor_tensor(out=tile, in0=tile, scalar=col("g_ret", l), in1=row(f_r[0][:]),
                                             op0=ALU.mult, op1=ALU.mult).then_inc(f_y_ready, 1)
                    dve.wait_ge(f_y_ready, j * 2 + (12 * l + 1))
                    dve.tensor_tensor(tile, tile, proj1[:, bass.ds(j + 24, 1), :], ALU.mult).then_inc(f_y_ready, 1)

                def take_out(j):
                    dve.wait_ge(q["summed"], BEGUN + j + (4 * l + 1))
                    dve.tensor_copy(proj1[:, dyn(j), :], row(bank(2))).then_inc(q["evacuated"], 1)

                def stage_k(j, scored):
                    dve.wait_ge(q["scored"], scored)
                    dve.tensor_copy(row(d_k[:]), proj1[:, bass.ds(j + 4, 1), :]).then_inc(q["staged_dve"], 1)

                def stage_v(j, turned):
                    dve.wait_ge(q["v_turned"], turned)
                    dve.tensor_copy(row(d_v[:]), proj1[:, bass.ds(j + 20, 1), :]).then_inc(q["staged_dve"], 1)

                def head(j, first):
                    if not first:
                        probs(j - 1, 2)
                    bias(j, 0)
                    if not first:
                        probs(j - 1, 3)
                    bias(j, 1)
                    probs(j, 0)
                    if not first:
                        finish(j - 1)
                        take_out(j - 1)
                    bias(j, 2)
                    stage_v(j + 1, BEGUN + j + (4 * l + 1))
                    probs(j, 1)
                    stage_k(j + 1, BEGUN + j * 8 + (32 * l + 8))
                    bias(j, 3)

                stage_k(0, BEGUN + 32 * l)
                stage_v(0, BEGUN + 4 * l)
                head(0, True)
                with dve.Fori(1, 4) as j:
                    head(j, False)
                probs(3, 2)
                probs(3, 3)
                finish(3)
                take_out(3)

            def fin1(ph):
                l = ph["layer"]
                dve.wait_ge(sems["d"]["staged_act"], 5 * (l + 1))
                dve.wait_ge(sems["d"]["staged_dve"], 10 * (l + 1))

                def lo(k):
                    dve.wait_ge(h_hi_ready, KT * ph["h0"] + k + 1)
                    dve.tensor_tensor(h_lo[:, k, 0:S], proj1[:, 8 + k if k < 4 else k - 4, :],
                                      h_hi[:, k, 0:S].bitcast(F32), ALU.subtract).then_inc(h_dve, 1)

                for n in range(4, 8):
                    tile = proj1[:, n - 4, :]
                    dve.wait_ge(f_std, 8 * l + n + 1)
                    dve.reciprocal(f_r[n % 2][:], f_r[n % 2][:]).then_inc(f_recip, 1)
                    dve.wait_ge(f_recip, 8 * l + n + 1)
                    dve.scalar_tensor_tensor(out=tile, in0=tile, scalar=lam[:, 10 + l:11 + l], in1=f_r[n % 2][:],
                                             op0=ALU.mult, op1=ALU.mult).then_inc(f_y_ready, 1)
                    if n == 6:
                        lo(3)
                lo(5)
                lo(7)

            def fin2(ph):
                for n in range(1, 8, 2):
                    dve.wait_ge(h_hi_ready, KT * ph["h0"] + n + 1)
                    dve.tensor_tensor(h_lo[:, n, 0:ph["T"]], proj[:, n, 0:ph["T"]],
                                      h_hi[:, n, 0:ph["T"]].bitcast(F32), ALU.subtract).then_inc(h_dve, 1)

            def na(ph):
                q = sems["n"]
                for hd in range(2):
                    for kind in range(3):
                        last = dve.memset(n_bias[:, hd, kind, 2 * P:4 * P], 0.0)
                        last.then_inc(q["mask_arg"], 1)
                dve.wait_ge(q["mask_arg"], BEGUN + 6)

                def pair(j, first):
                    dve.wait_ge(q["scored"], BEGUN + j * 12)
                    dve.tensor_copy(row(n_k[:]), proj[:, bass.ds(j + 8, 1), :]).then_inc(q["staged_dve"], 1)
                    dve.wait_ge(q["v_turned"], BEGUN + j)
                    dve.tensor_copy(row(n_v[:]), proj[:, bass.ds(j + 16, 1), :]).then_inc(q["staged_dve"], 1)

                    def bias(t):
                        hd, b = divmod(t, 6)
                        w = S if b < 4 else C
                        table = n_bias[:, hd, MASK_KIND[b], :] if b < 4 else n_bias[:, 0, 0, 2 * P:4 * P]
                        dve.wait_ge(q["bias"], j * 6 + (3 * hd + 3))
                        dve.wait_ge(q["scored"], BEGUN + j * 12 + (t + 1))
                        if t >= 3:
                            dve.wait_ge(q["turned"], BEGUN + j * 12 + (t - 2))
                        else:
                            dve.wait_ge(q["turned"], BEGUN + j * 12)
                        dve.memset(pace[:, 2:3], 0.0)
                        dve.tensor_tensor_reduce(n_s[t % 3][:, 0:w], bank(4 + t % 2, w), table, 1.0, NEG,
                                                 ALU.add, ALU.max, stats[:, t % 3:t % 3 + 1]).then_inc(q["biased"], 1)
                        dve.wait_ge(q["biased"], BEGUN + j * 12 + (t + 1))
                        dve.tensor_scalar(stats[:, 3 + t % 3:4 + t % 3], stats[:, t % 3:t % 3 + 1], -1.0, None,
                                          ALU.mult).then_inc(q["negmax"], 1)

                    def probs(t):
                        w = S if t % 6 < 4 else C
                        dve.wait_ge(q["exped"], j * 12 + (t + 1))
                        dve.reciprocal(stats[:, 9 + t % 3:10 + t % 3], stats[:, 6 + t % 3:7 + t % 3]
                                       ).then_inc(q["recip"], 1)
                        dve.wait_ge(q["recip"], j * 12 + (t + 1))
                        dve.tensor_scalar(n_s[t % 3][:, 0:w], n_s[t % 3][:, 0:w], stats[:, 9 + t % 3:10 + t % 3],
                                          None, ALU.mult).then_inc(q["probs"], 1)

                    for t in range(13):
                        if t == 2 and not first:
                            evacuate(j - 1, 1)
                        if t == 9:
                            evacuate(j, 0)
                        if t < 12:
                            bias(t)
                        if t >= 1:
                            probs(t - 1)

                def evacuate(j, hd):
                    half = slice(HD * hd, HD * hd + HD)
                    dve.wait_ge(q["summed"], BEGUN + j * 12 + (6 * hd + 6))
                    dve.tensor_copy(
                        proj[half, dyn(j), 0:S].rearrange("p a (r b c) -> p (a b) r c", b=8, c=8),
                        bank(2 + 4 * hd)[half, :].rearrange("p (b r c) -> p b r c", b=8, c=8)
                        ).then_inc(q["evacuated"], 1)
                    dve.tensor_copy(proj[half, dyn(j), S:T2], row(bank(3 + 4 * hd)[half, 0:C])
                                    ).then_inc(q["evacuated"], 1)

                pair(0, True)
                with dve.Fori(1, 8) as j:
                    pair(j, False)
                evacuate(7, 1)

            def rope(ph):
                dve.wait_ge(tab["rope"], 32)
                for n in range(ROPE_TILES):
                    t1 = s_t1[n % 2]
                    dve.wait_ge(rope_mm, n + 1)
                    if n >= 2:
                        dve.wait_ge(rope_out, n - 1)
                    dve.tensor_tensor(t1[:], bank(6 + n % 2), s_sin[:], ALU.mult).then_inc(rope_a, 1)
                    dve.wait_ge(rope_a, n + 1)
                    dve.wait_ge(rope_b, n + 1)
                    dve.tensor_tensor(proj[:, n, 0:S], t1[:], s_t2[n % 2][:], ALU.add).then_inc(rope_out, 1)

            def swa(ph):
                q = sems["s"]
                dve.wait_ge(tab["swa"], 16)
                for kv in range(2):
                    def heads(g, first):
                        n = g * 8 + 32 * kv

                        def width(t):
                            return (5 if 0 < t % 4 < 3 else 4) * P

                        def bias(t):
                            hd, b = divmod(t, 4)
                            w, s = width(t), s_s[t % 3]
                            frm = (P, 0, 0, 5 * P)[b]
                            sink = dcol("sink", g * 2 + (8 * kv + hd))
                            dve.wait_ge(q["scored"], BEGUN + n + (t + 1))
                            dve.wait_ge(q["turned"], BEGUN + n + max(t - 2, 0))
                            dve.memset(pace[:, 2:3], 0.0)
                            dve.tensor_tensor_reduce(s[:, 0:w], sums[t % 2][:, 0:w], s_band[:, frm:frm + w], 1.0, NEG,
                                                     ALU.add, ALU.max, stats[:, t % 3:t % 3 + 1]
                                                     ).then_inc(q["biased"], 1)
                            dve.tensor_copy(s[:, w:w + 1], sink).then_inc(q["mask_arg"], 1)
                            dve.wait_ge(q["biased"], BEGUN + n + (t + 1))
                            dve.wait_ge(q["mask_arg"], BEGUN + n + (t + 1))
                            dve.tensor_scalar(stats[:, 3 + t % 3:4 + t % 3], stats[:, t % 3:t % 3 + 1], sink, -1.0,
                                              ALU.max, ALU.mult).then_inc(q["negmax"], 1)

                        def probs(t):
                            w = width(t)
                            dve.wait_ge(q["exped"], n + (t + 1))
                            dve.reciprocal(stats[:, 9 + t % 3:10 + t % 3], stats[:, 6 + t % 3:7 + t % 3]
                                           ).then_inc(q["recip"], 1)
                            dve.wait_ge(q["recip"], n + (t + 1))
                            dve.tensor_scalar(s_s[t % 3][:, 0:w], s_s[t % 3][:, 0:w], stats[:, 9 + t % 3:10 + t % 3],
                                              None, ALU.mult).then_inc(q["probs"], 1)

                        for t in range(9):
                            if t == 2 and not first:
                                evacuate(g + (4 * kv - 1), 1)
                            if t == 7:
                                evacuate(g + 4 * kv, 0)
                            if t < 8:
                                bias(t)
                            if t >= 1:
                                probs(t - 1)

                    def evacuate(tile, hd):
                        half = slice(HD * hd, HD * hd + HD)
                        dve.wait_ge(q["summed"], BEGUN + tile * 8 + (4 * hd + 4))
                        dve.tensor_copy(proj[half, dyn(tile), 0:S], row(bank(2 + hd)[half, :])
                                        ).then_inc(q["evacuated"], 1)

                    if kv == 0:
                        heads(0, True)
                    with dve.Fori(1 - kv, 4) as g:
                        heads(g, False)
                evacuate(7, 1)

            for ph in phases:
                kind = ph["kind"]
                if kind == "norm":
                    if ph["unit0"] == MOD_UNITS:
                        modulation_end()
                    norm(ph)
                    if ph["norm0"] == 0:
                        setup()
                elif kind == "normed":
                    head_norm(ph)
                elif kind == "proj":
                    modulation_pairs(ph)
                    if ph["weight"] == "swa_qkv":
                        rope(ph)
                elif kind == "resid":
                    resid(ph)
                elif kind == "glu":
                    glu(ph)
                elif kind == "conv":
                    conv(ph)
                elif kind == "retention":
                    dve.wait_ge(acc_free, ph["unit0"])
                    dve.wait_ge(mm_done, ph["unit0"])
                    retention(ph)
                elif kind == "diff":
                    diff(ph)
                elif kind == "fin1":
                    fin1(ph)
                elif kind == "na":
                    dve.wait_ge(acc_free, ph["unit0"])
                    dve.wait_ge(mm_done, ph["unit0"])
                    na(ph)
                elif kind == "swa":
                    dve.wait_ge(acc_free, ph["unit0"])
                    dve.wait_ge(mm_done, ph["unit0"])
                    swa(ph)
                elif kind == "fin2":
                    fin2(ph)


def constants():
    p = np.arange(P)[:, None]
    j = np.arange(STRIP)[None, :]
    dist = (j - (S - P) - p).astype(np.float32)
    strips = np.stack([np.maximum(dist, 0), np.maximum(-dist, 0), np.abs(dist)])
    mats = np.zeros((P, 5, P), np.float32)
    mats[:, IDENT] = np.eye(P)
    mats[:, MEAN64] = np.kron(np.eye(2), np.full((HD, HD), 1 / HD))
    mats[:, MEAN128] = 1 / P
    mats[:, MEAN1024] = 1 / D
    rot = np.zeros((P, P), np.float32)
    for h in range(2):
        for i in range(HD // 2):
            rot[h * HD + HD // 2 + i, h * HD + i] = -1.0
            rot[h * HD + i, h * HD + HD // 2 + i] = 1.0
    mats[:, ROT] = rot
    mask = np.zeros((P, 3, 4, ROWS, 8), np.float32)
    qc = np.arange(P) // HD * 8 + np.arange(P) % 8
    for kind, b in enumerate((0, 1, 3)):
        c = 16 * b + qc
        first = np.clip(c - 8, 0, GRID - 16)
        key = KEY_COL[b] + np.arange(32).reshape(4, 8)
        ok = (key[None] >= first[:, None, None]) & (key[None] < first[:, None, None] + 16)
        mask[:, kind] = np.where(ok, 0.0, NEG)[:, :, None, :]
    k = np.arange(P)[None, :]
    before = np.where(k >= p, 0.0, NEG)
    after = np.where(k <= p, 0.0, NEG)
    zero = np.zeros((P, P))
    band = np.concatenate([before, zero, after, zero, zero, before, zero, zero, zero], 1)
    t = np.arange(S)
    inv = (10000.0 ** (-np.arange(HD // 4, dtype=np.float32) / (HD // 4))).astype(np.float32)
    ang = np.concatenate([(t // GRID).astype(np.float32)[:, None] * inv,
                          (t % GRID).astype(np.float32)[:, None] * inv], -1).astype(np.float32)
    rope = np.stack([np.tile(f(ang).T, (4, 1)) for f in (np.cos, np.sin)])
    f32 = lambda a: np.ascontiguousarray(a, dtype=np.float32)
    return dict(dist=f32(strips), mats=f32(mats), na_mask=f32(mask.reshape(P, 3, 2 * P)),
                band=f32(band), rope=f32(rope))


def lay_out(i):
    def units(w):
        L, K, N = w.shape
        return w.reshape(L, K // P, P, N // P, P).transpose(0, 3, 2, 1, 4).reshape(L * N // P, P, K)

    def cols(v):
        return v.reshape(-1, P).T

    def rep(v):
        return np.broadcast_to(v.reshape(1, -1), (P, v.size))

    def head(v):
        return np.concatenate([v, v])[:, None]

    x, ctx = i["x"][0], i["ctx_2"][0]
    o = {}
    o["x"] = x.T.reshape(KT, P, S).transpose(1, 0, 2)
    o["ctx"] = ctx.T.reshape(KT, P, C).transpose(1, 0, 2)
    w = i["w_in"].reshape(DEPTH, D, 7, 512)
    o["w_in"] = units(np.concatenate([w[:, :, n] for n in (4, 5, 0, 1, 2, 6, 3)], 2))
    o["w_out"] = units(i["w_out"])
    gu = np.stack([i["w_gate"].reshape(DEPTH, D, FT, P), i["w_up"].reshape(DEPTH, D, FT, P)], 3)
    o["w_gu"] = units(gu.reshape(DEPTH, D, 2 * D_FF))
    o["w_down"] = units(i["w_down"].reshape(DEPTH * 2, D_FF // 2, D))
    o["w_mod"] = i["w_mod_2"].transpose(0, 2, 1).reshape(-1, P, D)
    o["c"] = rep(np.stack([i["c_2"][0], i["c_ctx_2"]])).reshape(P, 2, D)
    o["na_qkv"] = units(i["na_w_qkv_2"])
    o["na_o"] = units(i["na_w_o_2"])
    def pair_heads(a, axis):
        shape = a.shape
        a = np.moveaxis(a, axis, 0).reshape(2, 2, 4, HD, -1).transpose(0, 2, 1, 3, 4)
        return np.moveaxis(a.reshape((D,) + tuple(np.delete(shape, axis))), 0, axis)
    sw = i["swa_w_qkv_2"]
    o["swa_qkv"] = units(np.concatenate([pair_heads(sw[:, :, :D], 2), sw[:, :, D:]], 2))
    o["swa_o"] = units(pair_heads(i["swa_w_o_2"], 1))
    up = i["ffn_w_up_2"].reshape(DEPTH, D, 2, FT, P).transpose(0, 1, 3, 2, 4)
    o["w_up2"] = units(up.reshape(DEPTH, D, 2 * D_FF))
    o["w_down2"] = units(i["ffn_w_down_2"].reshape(DEPTH * 2, D_FF // 2, D))
    o["lam"] = rep(np.stack([i[n] for n in ("lambda_q1", "lambda_k1", "lambda_q2", "lambda_k2")], 1)
                   ).reshape(P, DEPTH * 4, HD)
    pad = np.pad(i["na_rpb_2"][0], ((0, 0), (0, 0), (16, 16)))
    r, c, kr, u = np.ogrid[0:ROWS, 0:16, 0:ROWS, 0:48]
    e = pad[:, kr - r + ROWS - 1, u - c + 15]
    e = e.reshape(16, ROWS, 2, 8, ROWS, 48).transpose(0, 2, 1, 3, 4, 5)
    o["rpb"] = e.reshape(8, 2, P, ROWS * 48).transpose(0, 2, 1, 3)
    conv = np.concatenate([i["ffn_conv_w_2"], i["ffn_conv_b_2"][:, None]], 1)
    conv = conv.reshape(DEPTH, 4, 2, FT, P).transpose(4, 0, 3, 2, 1)
    two = lambda v: np.repeat(cols(v), 2, 1)
    heads = lambda v: v.reshape(2, 2, 4).transpose(0, 2, 1)
    s = {
        "g_attn": cols(i["attn_norm_g"]), "g_ffn": cols(i["ffn_norm_g"]),
        "g_ret": np.concatenate([head(v) for v in i["ret_norm_g"]], 1), "g_diff": i["diff_norm_g"].T,
        "g_dqk": np.concatenate([np.repeat(head(i[n][l]), 4, 1) for l in range(DEPTH)
                                 for n in ("dq_norm_g", "dk_norm_g")], 1),
        "g_na": np.concatenate([np.repeat(head(i[n][0]), 8, 1) for n in ("na_g_q_2", "na_g_k_2")], 1),
        "g_swa": np.concatenate([np.repeat(head(i["swa_g_q_2"][0]), 8, 1),
                                 np.repeat(head(i["swa_g_k_2"][0]), 2, 1)], 1),
        "decay": rep(np.stack([i["ret_decay_fwd"], i["ret_decay_bwd"]], 1)),
        "slope": rep(-(2.0 ** (-8.0 * np.arange(1, 5) / 4)).astype(np.float32)),
        "sink": rep(heads(i["swa_sink_2"][0])), "conv": conv.reshape(P, -1),
        "g2_attn": two(i["g_attn_2"]), "g2_ffn": two(i["g_ffn_2"]), "b_mod": two(i["b_mod_2"]),
    }
    for n, (_, width) in SMALL.items():
        assert s[n].shape == (P, width), (n, s[n].shape, width)
    o["small"] = np.concatenate([s[n] for n in SMALL], 1)
    return o


def kernel(**inputs):
    import concourse.bacc as bacc
    from concourse.bass_utils import run_bass_kernel_spmd

    arrays = lay_out({n: np.asarray(a) for n, a in inputs.items()})
    arrays.update(constants())
    arrays = {n + "_dram": np.ascontiguousarray(a) for n, a in arrays.items()}
    nc = bacc.Bacc("TRN2", target_bir_lowering=False, num_devices=1)
    d = {n[:-5]: nc.dram_tensor(n, a.shape, mybir.dt.from_np(a.dtype), kind="ExternalInput").ap()
         for n, a in arrays.items()}
    out = nc.dram_tensor("out_dram", (P, KT, S), F32, kind="ExternalOutput").ap()
    build(nc, d, out)
    r = run_bass_kernel_spmd(nc, [arrays], core_ids=[0])
    got = r.results[0]["out_dram"]
    return np.ascontiguousarray(got.transpose(2, 1, 0)).reshape(1, S, D)
```
